# Optimizing a Trainium2 kernel written in Bass

```python
import math
import jax, jax.numpy as jnp
from jax import lax
import numpy as np

D_MODEL = 1024
BATCH = 1
SEQ = 512
DEPTH = 2

HEAD_DIM = 64
MIX_WIDTH = D_MODEL
HG_WIDTH = MIX_WIDTH // 4
S5_WIDTH = MIX_WIDTH // 4
ATTN_WIDTH = MIX_WIDTH - HG_WIDTH - S5_WIDTH
HG_HEADS = HG_WIDTH // HEAD_DIM
HG_CHUNK = 16
ATTN_HEADS = ATTN_WIDTH // HEAD_DIM
KV_HEADS = 2
KV_WIDTH = KV_HEADS * HEAD_DIM
Q_BLOCK = 128
ROPE_THETA = 10000.0
GRID_W = 64
S5_CH_PER_GROUP = 16
S5_GROUPS = S5_WIDTH // S5_CH_PER_GROUP
S5_STATE = 64
N_EXPERT_GROUPS = 4
EXPERTS_PER_GROUP = 8
N_EXPERTS = N_EXPERT_GROUPS * EXPERTS_PER_GROUP
TOP_K_IN_GROUP = 2
EXPERT_FF = D_MODEL // 2
MOE_BLOCK = 128
NORM_EPS = 1e-6

IN_SPLITS = (HG_WIDTH, HG_WIDTH, HG_WIDTH, HG_WIDTH, HG_WIDTH, ATTN_WIDTH, KV_WIDTH, KV_WIDTH, S5_WIDTH)
IN_WIDTH = sum(IN_SPLITS)
IN_OFFSETS = tuple(sum(IN_SPLITS[:i + 1]) for i in range(len(IN_SPLITS) - 1))

kernel_name = "hybrid_hgrn2_gqa_s5_hmoe_encoder"

def rms_norm(x, g):
    xf = x.astype(jnp.float32)
    y = xf * lax.rsqrt(jnp.mean(xf * xf, axis=-1, keepdims=True) + NORM_EPS)
    return (y * g.astype(jnp.float32)).astype(x.dtype)

def split_heads(t, n_heads):
    B, S, _ = t.shape
    return t.reshape(B, S, n_heads, -1).transpose(0, 2, 1, 3)

def gla_chunkwise(q, k, v, log_f):
    B, H, S, dk = q.shape
    dv = v.shape[-1]
    n_chunks = S // HG_CHUNK
    rs = lambda t: t.reshape(B, H, n_chunks, HG_CHUNK, t.shape[-1])
    q, k, v, log_f = rs(q), rs(k), rs(v), rs(log_f)
    b = jnp.cumsum(log_f, axis=3)
    b_last = b[:, :, :, -1:, :]
    q_dec = q * jnp.exp(b)
    k_dec = k * jnp.exp(-b)
    scores = jnp.einsum('bhntd,bhnsd->bhnts', q_dec, k_dec)
    mask = jnp.tril(jnp.ones((HG_CHUNK, HG_CHUNK), dtype=bool))
    scores = jnp.where(mask, scores, 0.0)
    o_intra = jnp.einsum('bhnts,bhnsv->bhntv', scores, v)
    k_end = k * jnp.exp(b_last - b)
    chunk_kv = jnp.einsum('bhntd,bhntv->bhndv', k_end, v)
    chunk_decay = jnp.exp(b_last[:, :, :, 0, :])

    def step(state, inp):
        dec, kv = inp
        return dec[..., None] * state + kv, state

    _, s_start = lax.scan(step, jnp.zeros((B, H, dk, dv), jnp.float32),
                          (jnp.moveaxis(chunk_decay, 2, 0), jnp.moveaxis(chunk_kv, 2, 0)))
    s_start = jnp.moveaxis(s_start, 0, 2)
    o_inter = jnp.einsum('bhntd,bhndv->bhntv', q_dec, s_start)
    return (o_intra + o_inter).reshape(B, H, S, dv)

def hgrn2_mixer(q, i, g, zf, zb, lb, norm_g):
    B, S, _ = q.shape
    qh = split_heads(jax.nn.silu(q.astype(jnp.float32)), HG_HEADS)
    vh = split_heads(i.astype(jnp.float32), HG_HEADS)

    def log_forget(z, lbd):
        return jnp.logaddexp(jnp.log1p(-lbd) + jax.nn.log_sigmoid(z.astype(jnp.float32)), jnp.log(lbd))

    lf_f = split_heads(log_forget(zf, lb[0]), HG_HEADS)
    lf_b = split_heads(log_forget(zb, lb[1]), HG_HEADS)
    flip = lambda t: jnp.flip(t, axis=2)
    o_f = gla_chunkwise(qh, -jnp.expm1(lf_f), vh, lf_f)
    o_b = flip(gla_chunkwise(flip(qh), flip(-jnp.expm1(lf_b)), flip(vh), flip(lf_b)))
    o = (o_f + o_b).transpose(0, 2, 1, 3)
    gate = jax.nn.silu(g.astype(jnp.float32)).reshape(B, S, HG_HEADS, HEAD_DIM)
    o = rms_norm(o, norm_g) * gate
    return o.reshape(B, S, HG_WIDTH).astype(q.dtype)

def axial_rope_tables(S):
    rows_count = S // GRID_W
    rows = jnp.repeat(jnp.arange(rows_count, dtype=jnp.float32), GRID_W)
    cols = jnp.tile(jnp.arange(GRID_W, dtype=jnp.float32), rows_count)
    pairs = HEAD_DIM // 4
    freqs = jnp.power(jnp.float32(ROPE_THETA), -jnp.arange(pairs, dtype=jnp.float32) / pairs)
    ang = jnp.concatenate([rows[:, None] * freqs, cols[:, None] * freqs], axis=-1)
    return jnp.cos(ang), jnp.sin(ang)

def apply_rope(x, cos, sin):
    xf = x.astype(jnp.float32).reshape(*x.shape[:-1], HEAD_DIM // 2, 2)
    x0, x1 = xf[..., 0], xf[..., 1]
    c, s = cos[None, :, None, :], sin[None, :, None, :]
    return jnp.stack([x0 * c - x1 * s, x0 * s + x1 * c], axis=-1).reshape(x.shape)

def gqa_attention(q, k, v, q_gain, k_gain, cos, sin):
    B, S, _ = q.shape
    G = ATTN_HEADS // KV_HEADS
    qh = apply_rope(rms_norm(q.reshape(B, S, ATTN_HEADS, HEAD_DIM), q_gain), cos, sin)
    kh = apply_rope(rms_norm(k.reshape(B, S, KV_HEADS, HEAD_DIM), k_gain), cos, sin).transpose(0, 2, 1, 3)
    vh = v.reshape(B, S, KV_HEADS, HEAD_DIM).astype(jnp.float32).transpose(0, 2, 1, 3)
    n_blocks = S // Q_BLOCK
    qb = qh.reshape(B, n_blocks, Q_BLOCK, KV_HEADS, G, HEAD_DIM).transpose(1, 0, 3, 4, 2, 5)
    scale = HEAD_DIM ** -0.5

    def attend(q_blk):
        s = jnp.einsum('bkgqd,bksd->bkgqs', q_blk, kh) * scale
        p = jax.nn.softmax(s, axis=-1)
        return jnp.einsum('bkgqs,bksd->bkgqd', p, vh)

    o = lax.map(attend, qb)
    return o.transpose(1, 0, 4, 2, 3, 5).reshape(B, S, ATTN_WIDTH).astype(q.dtype)

def _linear_combine(left, right):
    a_l, b_l = left
    a_r, b_r = right
    return a_r * a_l, a_r * b_l + b_r

def s5_mixer(u, a_re, a_im, log_dt, b_re, b_im, c_re, c_im, d_skip, w_glu, b_glu):
    B, S, _ = u.shape
    uf = u.astype(jnp.float32)
    ug = uf.reshape(B, S, S5_GROUPS, S5_CH_PER_GROUP).astype(jnp.complex64)
    y = d_skip.astype(jnp.float32) * uf
    for d in range(2):
        lam = lax.complex(a_re[d].astype(jnp.float32), a_im[d].astype(jnp.float32))
        dt = jnp.exp(log_dt[d].astype(jnp.float32))[:, None]
        lam_bar = jnp.exp(lam * dt)
        b_mat = lax.complex(b_re[d].astype(jnp.float32), b_im[d].astype(jnp.float32))
        b_bar = ((lam_bar - 1.0) / lam)[..., None] * b_mat
        bu = jnp.einsum('bsgc,gpc->sbgp', ug, b_bar)
        a = jnp.broadcast_to(lam_bar[None, None], (S, 1, S5_GROUPS, S5_STATE))
        _, states = lax.associative_scan(_linear_combine, (a, bu), axis=0, reverse=(d == 1))
        c_mat = lax.complex(c_re[d].astype(jnp.float32), c_im[d].astype(jnp.float32))
        y = y + jnp.real(jnp.einsum('sbgp,gcp->bsgc', states, c_mat)).reshape(B, S, S5_WIDTH)
    z = jax.nn.gelu(y)
    out = z * jax.nn.sigmoid(z @ w_glu.astype(jnp.float32) + b_glu.astype(jnp.float32))
    return out.astype(u.dtype)

def hier_moe(h, w_rg, b_rg, w_re, b_re, w_gate, w_up, w_down):
    B, S, D = h.shape
    T = B * S
    hf = h.reshape(T, D)
    tok = jnp.arange(T, dtype=jnp.int32)
    g_logits = (hf @ w_rg + b_rg).astype(jnp.float32)
    g_prob = jax.nn.softmax(g_logits, axis=-1)
    g_sel = jnp.argmax(g_logits, axis=-1).astype(jnp.int32)
    p_group = g_prob[tok, g_sel]
    e_logits = (hf @ w_re + b_re).astype(jnp.float32).reshape(T, N_EXPERT_GROUPS, EXPERTS_PER_GROUP)
    top_val, top_idx = lax.top_k(e_logits[tok, g_sel], TOP_K_IN_GROUP)
    gate = p_group[:, None] * jax.nn.softmax(top_val, axis=-1)
    expert_id = g_sel[:, None] * EXPERTS_PER_GROUP + top_idx.astype(jnp.int32)

    n_assign = T * TOP_K_IN_GROUP
    flat_e = expert_id.reshape(n_assign)
    flat_w = gate.reshape(n_assign)
    flat_tok = jnp.repeat(tok, TOP_K_IN_GROUP)
    order = jnp.argsort(flat_e)
    sorted_e, sorted_tok, sorted_w = flat_e[order], flat_tok[order], flat_w[order]
    counts = jnp.bincount(flat_e, length=N_EXPERTS)
    padded = ((counts + MOE_BLOCK - 1) // MOE_BLOCK) * MOE_BLOCK
    starts = jnp.cumsum(counts) - counts
    pends = jnp.cumsum(padded)
    pstarts = pends - padded
    dest = pstarts[sorted_e] + (jnp.arange(n_assign, dtype=jnp.int32) - starts[sorted_e])
    n_blocks = -(-n_assign // MOE_BLOCK) + N_EXPERTS
    n_rows = n_blocks * MOE_BLOCK
    buf_tok = jnp.full((n_rows,), T, jnp.int32).at[dest].set(sorted_tok)
    buf_w = jnp.zeros((n_rows,), jnp.float32).at[dest].set(sorted_w)
    blk_e = jnp.minimum(jnp.searchsorted(pends, jnp.arange(n_blocks, dtype=jnp.int32) * MOE_BLOCK, side='right'),
                        N_EXPERTS - 1)
    x_pad = jnp.concatenate([hf, jnp.zeros((1, D), hf.dtype)], axis=0)

    def expert_block(args):
        rows, e = args
        xb = x_pad[rows]
        return (jax.nn.silu(xb @ w_gate[e]) * (xb @ w_up[e])) @ w_down[e]

    ys = lax.map(expert_block, (buf_tok.reshape(n_blocks, MOE_BLOCK), blk_e))
    ys = ys.reshape(n_rows, D) * buf_w[:, None].astype(ys.dtype)
    out = jax.ops.segment_sum(ys, buf_tok, num_segments=T + 1)[:T]
    return out.reshape(B, S, D)

def setup_inputs(seed: int = 0) -> dict:
    key = jax.random.key(seed)
    ks = jax.random.split(key, 32)
    f32 = jnp.float32
    nrm = lambda k, shape, scale: scale * jax.random.normal(k, shape, f32)
    L = DEPTH
    return {
        "x": nrm(ks[0], (BATCH, SEQ, D_MODEL), 1.0),
        "norm1_g": 1.0 + nrm(ks[1], (L, D_MODEL), 0.02),
        "w_in": nrm(ks[2], (L, D_MODEL, IN_WIDTH), D_MODEL ** -0.5),
        "hgrn_lower_bounds": nrm(ks[3], (L, 2, HG_WIDTH), 0.5),
        "hgrn_norm_g": 1.0 + nrm(ks[4], (L, HEAD_DIM), 0.02),
        "attn_q_norm_g": 1.0 + nrm(ks[5], (L, HEAD_DIM), 0.02),
        "attn_k_norm_g": 1.0 + nrm(ks[6], (L, HEAD_DIM), 0.02),
        "s5_a_re": -0.5 + nrm(ks[7], (L, 2, S5_GROUPS, S5_STATE), 0.01),
        "s5_a_im": jnp.pi * jnp.arange(S5_STATE, dtype=f32) + nrm(ks[8], (L, 2, S5_GROUPS, S5_STATE), 0.01),
        "s5_log_dt": jax.random.uniform(ks[9], (L, 2, S5_GROUPS), f32, math.log(1e-3), math.log(1e-1)),
        "s5_b_re": nrm(ks[10], (L, 2, S5_GROUPS, S5_STATE, S5_CH_PER_GROUP), (2 * S5_CH_PER_GROUP) ** -0.5),
        "s5_b_im": nrm(ks[11], (L, 2, S5_GROUPS, S5_STATE, S5_CH_PER_GROUP), (2 * S5_CH_PER_GROUP) ** -0.5),
        "s5_c_re": nrm(ks[12], (L, 2, S5_GROUPS, S5_CH_PER_GROUP, S5_STATE), 0.5),
        "s5_c_im": nrm(ks[13], (L, 2, S5_GROUPS, S5_CH_PER_GROUP, S5_STATE), 0.5),
        "s5_d": nrm(ks[14], (L, S5_WIDTH), 1.0),
        "s5_w_glu": nrm(ks[15], (L, S5_WIDTH, S5_WIDTH), S5_WIDTH ** -0.5),
        "s5_b_glu": nrm(ks[16], (L, S5_WIDTH), 0.01),
        "w_out": nrm(ks[17], (L, MIX_WIDTH, D_MODEL), MIX_WIDTH ** -0.5),
        "norm2_g": 1.0 + nrm(ks[18], (L, D_MODEL), 0.02),
        "router_group_w": nrm(ks[19], (L, D_MODEL, N_EXPERT_GROUPS), D_MODEL ** -0.5),
        "router_group_b": nrm(ks[20], (L, N_EXPERT_GROUPS), 0.01),
        "router_expert_w": nrm(ks[21], (L, D_MODEL, N_EXPERTS), D_MODEL ** -0.5),
        "router_expert_b": nrm(ks[22], (L, N_EXPERTS), 0.01),
        "expert_w_gate": nrm(ks[23], (L, N_EXPERTS, D_MODEL, EXPERT_FF), D_MODEL ** -0.5),
        "expert_w_up": nrm(ks[24], (L, N_EXPERTS, D_MODEL, EXPERT_FF), D_MODEL ** -0.5),
        "expert_w_down": nrm(ks[25], (L, N_EXPERTS, EXPERT_FF, D_MODEL), EXPERT_FF ** -0.5),
        "final_norm_g": 1.0 + nrm(ks[26], (D_MODEL,), 0.02),
    }

def reference(x, norm1_g, w_in, hgrn_lower_bounds, hgrn_norm_g, attn_q_norm_g, attn_k_norm_g,
              s5_a_re, s5_a_im, s5_log_dt, s5_b_re, s5_b_im, s5_c_re, s5_c_im, s5_d, s5_w_glu, s5_b_glu,
              w_out, norm2_g, router_group_w, router_group_b, router_expert_w, router_expert_b,
              expert_w_gate, expert_w_up, expert_w_down, final_norm_g):
    S = x.shape[1]
    cos, sin = axial_rope_tables(S)
    lb_all = jnp.cumsum(jax.nn.softmax(hgrn_lower_bounds.astype(jnp.float32), axis=0), axis=0)
    lb_all = lb_all - lb_all[0:1]
    for l in range(DEPTH):
        h = rms_norm(x, norm1_g[l])
        proj = h @ w_in[l]
        hg_q, hg_i, hg_g, hg_ff, hg_fb, a_q, a_k, a_v, s5_u = jnp.split(proj, IN_OFFSETS, axis=-1)
        o_a = hgrn2_mixer(hg_q, hg_i, hg_g, hg_ff, hg_fb, lb_all[l], hgrn_norm_g[l])
        o_b = gqa_attention(a_q, a_k, a_v, attn_q_norm_g[l], attn_k_norm_g[l], cos, sin)
        o_c = s5_mixer(s5_u, s5_a_re[l], s5_a_im[l], s5_log_dt[l], s5_b_re[l], s5_b_im[l],
                       s5_c_re[l], s5_c_im[l], s5_d[l], s5_w_glu[l], s5_b_glu[l])
        mixed = jnp.concatenate([o_a, o_b, o_c], axis=-1)
        x = x + (mixed @ w_out[l]).astype(x.dtype)
        h = rms_norm(x, norm2_g[l])
        x = x + hier_moe(h, router_group_w[l], router_group_b[l], router_expert_w[l], router_expert_b[l],
                         expert_w_gate[l], expert_w_up[l], expert_w_down[l]).astype(x.dtype)
    return rms_norm(x, final_norm_g)


_drawn_inputs = setup_inputs


def setup_inputs(seed=0):
    import zlib

    import numpy as np

    out = dict(_drawn_inputs(seed))
    spreads = {}
    factors = {'attn_q_norm_g': 4.516,
     'attn_k_norm_g': 8.0,
     's5_a_re': 8.0,
     's5_b_glu': 8.0,
     'router_group_b': 2.792,
     'final_norm_g': 2.8}
    for name, (base, spread) in spreads.items():
        noise = np.random.default_rng([zlib.crc32(name.encode()), seed]).standard_normal(out[name].shape)
        drawn = base * np.exp(spread * noise) if base else spread * noise
        out[name] = __import__('jax').numpy.asarray(drawn.astype(out[name].dtype))
    for name, factor in factors.items():
        out[name] = (out[name] * factor).astype(out[name].dtype)
    return out
```

```python
from contextlib import ExitStack

import numpy as np

import concourse.bass as bass
from concourse import mybir

F32 = mybir.dt.float32
I32 = mybir.dt.int32
ALU = mybir.AluOpType
ACT = mybir.ActivationFunctionType
AX = mybir.AxisListType

P = 128
D = 1024
T = 512
L = 2
NB = T // P
KT = D // P
HD = 64
HG = 4
CH = 16
NCH = T // CH
CB = P // CH
QH = 8
G5 = 16
C5 = 16
DG = 2 * G5
SC = 8
NK = T // SC
NPOW = SC + 1
NE = 32
EG = 4
EPG = NE // EG
FF = 512
FT = FF // P
CAP = 64
NOVER = (2 * T) // CAP - 1
NROWS = (NE + NOVER) * CAP
RW = EG + NE
EPS = 1e-6
SCALE = HD ** -0.5
BIG = 1000.0
NEG = 1.0e30
TWO_PI = 2.0 * np.pi
ROUND = 12582912.0

def _cols(spec):
    at, out = 0, {}
    for name, n in spec:
        out[name] = (at, n)
        at += n
    return out, at


CONST, CONST_W = _cols([
    ("ident", P), ("mask_f", P), ("mask_b", P), ("head_ones", P), ("rope_swap", P), ("half_swap", P),
    ("before", P), ("ones", P), ("cos", T), ("sin", T), ("chunk_start", T), ("chunk_of", CB),
    ("group_id", EG), ("expert_id", NE), ("expert_row", NE), ("chunk_end", 7), ("over_id", NOVER),
    ("is_re", 1), ("is_im", 1), ("sign", 1), ("eps", 1)])
PACK, PACK_W = _cols([
    ("lb", L * HG), ("lb_sum", L), ("hgrn_g", 1), ("q_g", 1), ("k_g", 1), ("s5_d", 2), ("b_glu", 2),
    ("router_b", RW), ("router_w", KT * RW), ("w_glu", 2 * 256)])
S5P, S5P_W = _cols([
    ("a_re", DG), ("a_im", DG), ("log_dt", DG), ("b_re", DG * C5), ("b_im", DG * C5),
    ("c_re", DG * C5), ("c_im", DG * C5)])


def trunk(nc, x_in, w_in, w_out, pack, s5p, gains, final_g, wg, wu, wd, consts, out):
    ctx = ExitStack()
    with ctx:
        def sb(name, shape, dt=F32):
            return ctx.enter_context(nc.sbuf_tensor(name, shape, dt))

        def sem(name):
            return ctx.enter_context(nc.semaphore(name))

        u_dram = nc.dram_tensor("u_scratch", (G5, C5, SC, NK), F32).ap()
        y_dram = nc.dram_tensor("y_scratch", (G5, C5, SC, NK), F32).ap()
        xbuf = nc.dram_tensor("dispatched_tokens", (NROWS, D), F32).ap()
        ybuf = nc.dram_tensor("expert_rows", (NROWS, D), F32).ap()

        ring = sb("ring", [P, 6, 4096])
        hbuf = sb("hbuf", [P, 8192])
        x = sb("x", [P, NB, D])
        raw = sb("raw", [P, 9216])
        qd = sb("qd", [P, 2048])
        C = sb("consts_sb", [P, CONST_W])
        gB = sb("gain_rows", [P, D])
        pk = sb("pack_sb", [P, PACK_W])
        small = sb("small", [P, 64])
        dec4 = sb("dec4", [P, HG * NCH])
        lbs = sb("lower_bounds", [P, 24])
        over_i = sb("over_i", [P, 16], I32)
        dest_i = sb("dest_i", [P, 2 * NB], I32)
        gate_w = sb("gate_w", [P, 2 * NB])

        def cst(name):
            a, n = CONST[name]
            return C[:, a:a + n]

        def pcol(name):
            a, n = PACK[name]
            return pk[:, a:a + n]

        ident = cst("ident")
        h = hbuf[:, 0:4096].rearrange("p (b d) -> p b d", b=NB)
        hT = hbuf[:, 4096:8192].rearrange("p (k t) -> p k t", k=KT)

        def tile(buf, at, n=T):
            return buf[:, at:at + n]

        Z = [tile(raw, 512 * i) for i in range(HG)]
        hq = [tile(raw, 2048 + 512 * i) for i in range(2)]
        ak = tile(raw, 3072)
        av = raw[:, 3584:4096].rearrange("p (b c) -> p b c", b=NB)
        aq = [tile(raw, 4096 + 512 * i) for i in range(4)]
        hg = [tile(raw, 6144 + 512 * i) for i in range(2)]
        hv = raw[:, 7168:8192].rearrange("p (b c) -> p b c", b=NB)
        uT = [tile(raw, 8192 + 512 * i) for i in range(2)]
        q_dec = [tile(qd, 512 * i) for i in range(HG)]
        k_dec = [ring[:, 4, 2048 + 512 * i:2560 + 512 * i] for i in range(HG)]
        k_end = Z
        ht_e, ht_s, ht_k, ht_f, ht_d0, ht_d1, ht_F, ht_R = (ring[:, 5, 512 * i:512 * i + 512] for i in range(8))
        dec_n = small[:, 0:NCH]
        dec_s = [dec4[:, NCH * i:NCH * i + NCH] for i in range(HG)]
        kv_sb = hbuf[:, 0:2048].rearrange("p (v c) -> p v c", c=NCH)
        dec_sb = hbuf[:, 2048:4096].rearrange("p (v c) -> p v c", c=NCH)
        st_sb = hbuf[:, 4096:6144].rearrange("p (v c) -> p v c", c=NCH)
        v_blk = [hbuf[:, 6144 + 512 * i:6656 + 512 * i] for i in range(2)]
        k_endT = [hbuf[:, 7168 + 512 * i:7680 + 512 * i] for i in range(2)]
        sc_a = [ring[:, 2, 512 * i:512 * i + 512] for i in range(2)]
        sc_t = ring[:, 2, 1024:1536]
        o_sb = [ring[:, 2, 1536 + 512 * i:2048 + 512 * i] for i in range(2)]
        o_rs = [ring[:, 2, 2560 + 512 * i:3072 + 512 * i] for i in range(2)]
        rope_sq = [ring[:, 1, 512 * i:512 * i + 512] for i in range(5)]
        rope_t = ring[:, 1, 2560:3072]
        k_dup = [tile(qd, 1024 + 512 * i) for i in range(2)]
        p_sb = [tile(qd, 512 * i) for i in range(2)]
        pT_sb = [hbuf[:, 7168 + 512 * i:7680 + 512 * i] for i in range(2)]
        s5 = hbuf[:, 4608:4608 + S5P_W]
        Bt = ring[:, 0, :].rearrange("p (d m) -> p d m", d=DG)
        cosT = ring[:, 1, 0:2048].rearrange("p (d k) -> p d k", d=DG)
        sinT = ring[:, 1, 2048:4096].rearrange("p (d k) -> p d k", d=DG)
        BtT = ring[:, 2, :].rearrange("p (d s c) -> p d s c", d=DG, s=SC)
        T1 = ring[:, 2, 0:2048].rearrange("p (d k) -> p d k", d=DG)
        T2 = ring[:, 2, 2048:4096].rearrange("p (d k) -> p d k", d=DG)
        rho = ring[:, 3, 0:2048].rearrange("p (d k) -> p d k", d=DG)
        M5 = ring[:, 3, 2048:4096].rearrange("p (g m) -> p g m", g=G5)
        Kf = ring[0:C5, 3, 0:2048].rearrange("p (g i c) -> p g i c", g=G5, i=SC)
        Kb = ring[0:C5, 0, 0:2048].rearrange("p (g i c) -> p g i c", g=G5, i=SC)
        Ct = hbuf[:, 0:4608].rearrange("p (d i c) -> p d i c", d=DG, i=NPOW)
        U5 = raw[:, 0:1024].rearrange("p (g k) -> p g k", g=G5)
        Y5 = raw[:, 1024:2048].rearrange("p (g k) -> p g k", g=G5)
        s_tmp = ring[:, 0, :]
        gt = [hbuf[:, 512 * i:512 * i + 512] for i in range(4)]
        yT = [tile(raw, 512 * i) for i in range(2)]
        pw = raw[:, 6144:6144 + 2048]
        Wr = pw[:, 0:NPOW * DG].rearrange("p (i d) -> p i d", i=NPOW)
        Wi = pw[:, 288:288 + NPOW * DG].rearrange("p (i d) -> p i d", i=NPOW)
        A1 = pw[:, 576:864].rearrange("p (i d) -> p i d", i=NPOW)
        A2 = pw[:, 864:1152].rearrange("p (i d) -> p i d", i=NPOW)
        A3 = pw[:, 1152:1440].rearrange("p (i d) -> p i d", i=NPOW)
        A4 = pw[:, 1440:1728].rearrange("p (i d) -> p i d", i=NPOW)
        ss = [pw[:, 1728 + 32 * i:1760 + 32 * i] for i in range(10)]
        rt = [qd[:, 160 * i:160 * i + 160] for i in range(12)]
        xg = [tile(raw, 1024 * i, 1024) for i in range(2)]
        xT = [raw[:, 2048 + 512 * i:2560 + 512 * i].rearrange("p (k c) -> p k c", k=KT) for i in range(2)]
        e_e = tile(raw, 3072)
        e_s = tile(raw, 3584)
        hid = [tile(raw, 4096 + 512 * i) for i in range(2)]
        hidT = [raw[:, 5120 + 256 * i:5376 + 256 * i].rearrange("p (k c) -> p k c", k=FT) for i in range(2)]
        y_sb = [tile(raw, 5632 + 512 * i) for i in range(2)]

        pb = [ctx.enter_context(nc.psum_tensor(f"bank{i}", [P, 512], F32)) for i in range(8)]

        s_boot = sem("boot_loads")
        s_zero = sem("zero_tile")
        s_xz = sem("xbuf_zeroed")
        s_fin_g = sem("final_gain_loaded")
        s_fa = sem("final_act")
        s_fd = sem("final_dve")
        s_out = sem("out_stored")

        with nc.Block() as block:
            @block.sync
            def _(sp):
                sp.dma_start(C[:, :], consts).then_inc(s_boot, 16)
                sp.dma_start(x[:, :, :], x_in.rearrange("(b p) d -> p b d", p=P)).then_inc(s_boot, 16)
                sp.wait_ge(s_boot, 32)
                sp.wait_ge(s_zero, 1)
                for i in range(NROWS // CAP):
                    sp.dma_start(xbuf[CAP * i:CAP * i + CAP, :], hbuf[0:CAP, 0:D]).then_inc(s_xz, 16)
                for i in range(NE, NROWS // CAP):
                    sp.dma_start(ybuf[CAP * i:CAP * i + CAP, :], hbuf[0:CAP, 0:D]).then_inc(s_xz, 16)
                sp.wait_ge(s_xz, 16 * (NROWS // CAP + NOVER))

            @block.gpsimd
            def _(pool):
                nc.gpsimd.memset(hbuf[0:CAP, 0:D], 0.0).then_inc(s_zero, 1)
        nc.all_engine_barrier()

        s_dispatched = sem("tokens_dispatched")
        s_gathered = sem("expert_rows_gathered")
        PER_LAYER = 16 * 2 * NB

        names = dict(
            pack="parameters loaded", gain1="norm 1 gain row loaded", gain2="norm 2 gain row loaded",
            s5p="S5 parameters loaded", rstd="ACT: norm 1 scales", h="DVE: h rows of a block",
            pe="PE: h^T and projection groups", ev_d="DVE: groups evacuated", ev_a="ACT: groups evacuated",
            dve="DVE: own chain", act="ACT: own chain", pool="Pool: own chain",
            lb_e="ACT: lower bound exp", lb="DVE: lower bounds ready",
            sig_e="ACT: exp(-z) of a sigmoid job", sig_r="DVE: exp(-z) read", q_silu="DVE: silu(q) of a pair",
            q_copy="ACT: silu(q) copied to both halves", f_ready="DVE: forget gates of a head",
            f_split="Pool: scan operands of a head", head="DVE: decayed q, k of a head",
            r_sq="ACT: rope squares", r_y="DVE: rope gained tile", r_pe="PE: rope sums and swap",
            r_rs="ACT: rope rstd", r_done="DVE: rope tile done",
            ke_t="PE: k_end transposed", ke_e="ACT: k_end^T evacuated", hs_pe="PE: HGRN scores",
            hs_m="DVE: HGRN scores masked", vb="Pool: chunk-spread v", kv="PE: chunk k v of a block",
            kv_e="ACT: chunk k v evacuated", dec="Pool: decay rows", state="DVE: chunk states",
            ho="PE: HGRN outputs of a head", ho_b="ACT: backward output copied", ho_s="DVE: HGRN output of a pair",
            ho_q="ACT: HGRN squares", ho_m="PE: HGRN square sums", ho_r="ACT: HGRN rstd", o_a="DVE: o_a of a pair",
            k_dup="ACT: k^T halves duplicated", qk="PE: attention scores", mx="DVE: row maxima",
            ex="ACT: probabilities", pn="DVE: probabilities scaled", pt="PE: probabilities transposed",
            pt_e="ACT: transposed probabilities evacuated", pv="PE: attention output of a unit",
            o_b="ACT: o_b of a pair", u_out="u stored", u_in="u by chunk loaded",
            dt="ACT: S5 step sizes", ang="Pool: S5 angles", lam="ACT: S5 moduli, sines", den="Pool: S5 denominators",
            inv="DVE: S5 inverse denominators", bc="Pool: S5 Bt^T and Ct", tab="Pool: S5 rotations",
            kp="PE: S5 kernels of a bank", ke="S5 kernels evacuated", kdiag="DVE: S5 kernel diagonal",
            m5="S5 chunk matrix loaded", rho="Pool: S5 decay rows", bt="PE: Bt of a bank", bt_e="Bt evacuated",
            xin="PE: S5 chunk inputs of a quarter", rot="DVE: S5 inputs rotated", z="DVE: S5 scanned",
            zs="PE: S5 states swapped", xs="DVE: S5 states", y5="PE: S5 outputs", y5_e="S5 outputs evacuated",
            y_out="y stored", y_in="y loaded", ge="DVE: gelu argument", gx="ACT: gelu exp", z5="DVE: gelu",
            glu="PE: GLU products", glx="ACT: GLU exp", o_c="DVE: o_c of a tile",
            wo="PE: output projection groups", res="DVE: residual added", rstd2="ACT: norm 2 scales",
            h2="DVE: h rows", h2t="PE: h^T tiles", h2_d="DVE: h^T evacuated", h2_a="ACT: h^T evacuated",
            rl="PE: router logits", gs="DVE: group logits less maximum", gx2="ACT: group exp",
            sel="DVE: experts selected", sx="ACT: exp of the second's difference", cnt="PE: positions and counts",
            dest="DVE: destinations and weights", xt="PE: expert tokens transposed",
            xt_e="ACT: expert tokens evacuated", gu="PE: gate and up", ee="ACT: exp(-gate)", er="DVE: exp(-gate) read",
            ec="DVE: expert chain", hid="DVE: hidden rows", ht="PE: hidden transposed", ht_e="DVE: hidden^T evacuated",
            dn="PE: down", ye="ACT: expert rows evacuated", stored="ACT: every expert row stored",
            moe="DVE: MoE residual")
        s = {k: sem(f"s_{k}") for k in names}
        slot = [sem(f"slot{i}") for i in range(6)]
        xg_in = [sem(f"xg{i}") for i in range(2)]
        y_out = [sem(f"y_rows{i}_stored") for i in range(2)]

        def flat(ap):
            return ap.rearrange("p a b -> p (a b)")

        def linker(engine, semaphore):
            at = [0]

            def link(ins):
                at[0] += 1
                ins.then_inc(semaphore, 1)
                engine.wait_ge(semaphore, at[0])
            return link

        NG = KT + 18

        def wait_evacuated(engine, n):
            if n % 2 == 0:
                engine.wait_ge(s["ev_d"], n // 2 + 1)
            else:
                engine.wait_ge(s["ev_a"], n // 2 + 1)

        def weights(i):
            width = 512 if i < 4 else 256
            return ring[:, i, 0:8 * width].rearrange("p (k c) -> p k c", k=KT)

        w_o = [ring[:, 4 + i, :].rearrange("p (k c) -> p k c", k=KT) for i in range(2)]
        W_gate = [ring[:, 3 * i, :].rearrange("p (k c) -> p k c", k=KT) for i in range(2)]
        W_up = [ring[:, 3 * i + 1, :].rearrange("p (k c) -> p k c", k=KT) for i in range(2)]
        W_down = [ring[:, 3 * i + 2, :].rearrange("p (k c) -> p k c", k=FT) for i in range(2)]
        LOADS = [1, 1, 1, 1, 2, 1]
        NU = QH * NB
        RTI = [12, 13, 20, 21, 8, 9, 10, 11]
        target = {8: Z[0], 9: Z[1], 10: Z[2], 11: Z[3], 12: hq[0], 13: hq[1], 14: ak,
                  16: aq[0], 17: aq[1], 18: aq[2], 19: aq[3], 20: hg[0], 21: hg[1]}
        rope_x = [ak] + aq
        mixed = hq + aq + uT
        wg_f = wg.rearrange("e (p k) f -> e p (k f)", p=P)
        wu_f = wu.rearrange("e (p k) f -> e p (k f)", p=P)
        wd_f = wd.rearrange("e (p k) f -> e p (k f)", p=P)

        def evac_views(n):
            bank = pb[n % 4]
            if n < KT:
                return hT[:, n, :], bank[:, :]
            if n == 15:
                return flat(av), bank[:, :]
            if n in (22, 23):
                q = 2 * (n - 22)
                return flat(hv[:, q:q + 2, :]), bank[:, :]
            if n >= 24:
                return (uT[n - 24].rearrange("p (t k) -> p t k", t=SC),
                        bank[:, :].rearrange("p (k t) -> p t k", t=SC))
            return target[n], bank[:, :]

        def sync_program(sp, layer):
            for i in range(5):
                width = 4096 if i < 4 else 2048
                sp.dma_start(ring[:, i, 0:width], w_in[layer, :, 4096 * i:4096 * i + width]).then_inc(slot[i], 16)
            wait_evacuated(sp, 24)
            wait_evacuated(sp, 25)
            for i in range(2):
                sp.dma_start(u_dram[8 * i:8 * i + 8].rearrange("g c t k -> (g c) (t k)"), uT[i]).then_inc(s["u_out"], 16)
            sp.wait_ge(s["u_out"], 32)
            sp.wait_ge(s["ke_t"], HG)
            for t in range(SC):
                sp.dma_start(U5[C5 * t:C5 * t + C5], u_dram[:, :, t, :].rearrange("g c k -> c g k")).then_inc(s["u_in"], 16)
            sp.wait_ge(s["hs_pe"], HG)
            sp.wait_ge(s["head"], HG)
            sp.wait_ge(s["q_silu"], 4)
            for i in range(2):
                sp.dma_start(ring[:, 4 + i, :], w_out[layer, i]).then_inc(slot[4 + i], 16)
            sp.dma_start(gB[:, :], gains[layer, 1]).then_inc(s["gain2"], 16)
            sp.wait_ge(s["ho"], HG)
            sp.dma_start(s5, s5p[layer]).then_inc(s["s5p"], 16)
            sp.wait_ge(s["kdiag"], 1)
            for t in range(SC):
                rows = slice(C5 * t, C5 * t + C5)
                sp.dma_start(M5[rows, :, C5 * t:P].rearrange("p g (i c) -> p g i c", c=C5),
                             Kf[:, :, 0:SC - t, :]).then_inc(s["m5"], 16)
                if t:
                    sp.dma_start(M5[rows, :, 0:C5 * t].rearrange("p g (i c) -> p g i c", c=C5),
                                 Kb[:, :, SC - 1 - t:SC - 1, :]).then_inc(s["m5"], 16)
            sp.wait_ge(s["y5_e"], 2)
            for t in range(SC):
                sp.dma_start(y_dram[:, :, t, :].rearrange("g c k -> c g k"), Y5[C5 * t:C5 * t + C5]).then_inc(s["y_out"], 16)
            sp.wait_ge(s["y_out"], 16 * SC)
            for i in range(2):
                sp.dma_start(yT[i], y_dram[8 * i:8 * i + 8].rearrange("g c t k -> (g c) (t k)")).then_inc(s["y_in"], 16)
            first_e = sp.snap(layer * NE)
            second_e = sp.snap(layer * NE + 1)
            sp.dma_start(ring[:, 0, :], wg_f[first_e]).then_inc(slot[0], 16)
            sp.dma_start(ring[:, 1, :], wu_f[first_e]).then_inc(slot[1], 16)
            sp.dma_start(ring[:, 2, :], wd_f[first_e]).then_inc(slot[2], 16)
            sp.dma_start(ring[:, 3, :], wg_f[second_e]).then_inc(slot[3], 16)
            sp.wait_ge(s["wo"], 2 * NB)
            sp.dma_start(ring[:, 4, :], wu_f[second_e]).then_inc(slot[4], 16)
            sp.dma_start(ring[:, 5, :], wd_f[second_e]).then_inc(slot[5], 16)
            with sp.Fori(1, NE // 2) as j:
                for odd in range(2):
                    e = sp.snap(layer * NE + j * 2 + odd)
                    used = sp.snap(j * 2 + odd - 1)
                    sp.wait_ge(s["gu"], used)
                    sp.dma_start(ring[:, 3 * odd, :], wg_f[e]).then_inc(slot[3 * odd], 16)
                    sp.dma_start(ring[:, 3 * odd + 1, :], wu_f[e]).then_inc(slot[3 * odd + 1], 16)
                    sp.wait_ge(s["dn"], used)
                    sp.dma_start(ring[:, 3 * odd + 2, :], wd_f[e]).then_inc(slot[3 * odd + 2], 16)
            sp.wait_ge(s["dn"], NE)
            n_over = sp.value_load(over_i[0:1, NOVER:NOVER + 1], min_val=0, max_val=NOVER)
            with sp.If(n_over > 0):
                with sp.Fori(0, n_over) as i:
                    e_over = sp.value_load(over_i[0:1, bass.ds(i, 1)], min_val=0, max_val=NE - 1)
                    e = sp.snap(layer * NE + e_over)
                    used = sp.snap(i + NE)
                    sp.wait_ge(s["dn"], used)
                    sp.dma_start(ring[:, 0, :], wg_f[e]).then_inc(slot[0], 16)
                    sp.dma_start(ring[:, 1, :], wu_f[e]).then_inc(slot[1], 16)
                    sp.dma_start(ring[:, 2, :], wd_f[e]).then_inc(slot[2], 16)

        def tensor_program(pe, layer):
            mm, tr = nc.tensor.matmul, nc.tensor.transpose

            def rope(j):
                pe.wait_ge(s["r_sq"], j + 1)
                if j:
                    pe.wait_ge(s["r_rs"], j)
                    pe.wait_ge(s["r_done"], j)
                mm(pb[6][:, :], cst("head_ones"), rope_sq[j], start=True, stop=True)
                pe.wait_ge(s["r_y"], j + 1)
                mm(pb[7][:, :], cst("rope_swap"), rope_x[j], start=True, stop=True).then_inc(s["r_pe"], 1)

            pe.wait_ge(s["h"], NB)
            for n in range(KT):
                if n >= 4:
                    wait_evacuated(pe, n - 4)
                for b in range(NB):
                    last = tr(pb[n % 4][:, P * b:P * b + P], h[:, b, P * n:P * n + P], ident)
                last.then_inc(s["pe"], 1)
            wait_evacuated(pe, KT - 2)
            wait_evacuated(pe, KT - 1)
            for n in range(KT, NG):
                i, c = (n - KT) // 4, P * ((n - KT) % 4)
                w = weights(i)
                if c == 0:
                    pe.wait_ge(slot[i], 16)
                wait_evacuated(pe, n - 4)
                bank = pb[n % 4]
                if n == 15:
                    for b in range(NB):
                        for k in range(KT):
                            last = mm(bank[:, P * b:P * b + P], hT[:, k, P * b:P * b + P], w[:, k, c:c + P],
                                      start=(k == 0), stop=(k == KT - 1))
                elif n in (22, 23):
                    for half in range(2):
                        b = 2 * (n - 22) + half
                        for k in range(KT):
                            last = mm(bank[:, 256 * half:256 * half + 256], hT[:, k, P * b:P * b + P],
                                      w[:, k, 256:512], start=(k == 0), stop=(k == KT - 1))
                else:
                    for k in range(KT):
                        last = mm(bank[:, :], w[:, k, c:c + P], hT[:, k, :], start=(k == 0), stop=(k == KT - 1))
                last.then_inc(s["pe"], 1)
                for j, after in enumerate((18, 20, 22, 24, 25)):
                    if n == after:
                        rope(j)

            def hgrn_in(hh):
                pe.wait_ge(s["head"], hh + 1)
                if hh == 0:
                    wait_evacuated(pe, NG - 2)
                    wait_evacuated(pe, NG - 1)
                    pe.wait_ge(s["r_rs"], 5)
                else:
                    pe.wait_ge(s["kv_e"], NB * hh)
                    pe.wait_ge(s["hs_m"], hh)
                for b in range(NB):
                    last = tr(pb[0][:, P * b:P * b + P], k_end[hh][:, P * b:P * b + P], ident)
                last.then_inc(s["ke_t"], 1)
                for b in range(NB):
                    t = slice(P * b, P * b + P)
                    mm(pb[5][:, t], k_dec[hh][0:HD, t], q_dec[hh][0:HD, t], start=True, stop=True)
                    last = mm(pb[6][:, t], k_dec[hh][HD:P, t], q_dec[hh][HD:P, t], start=True, stop=True)
                last.then_inc(s["hs_pe"], 1)
                pe.wait_ge(s["ke_e"], hh + 1)
                kT = k_endT[hh % 2]
                for b in range(NB):
                    pe.wait_ge(s["vb"], NB * hh + b + 1)
                    v = v_blk[b % 2]
                    mm(pb[b][0:HD, :], kT[:, P * b:P * b + HD], v, start=True, stop=True)
                    rev = v.rearrange("p (c v) -> p c v", c=CB)[:, ::-1, :]
                    mm(pb[NB - 1 - b][HD:P, :].rearrange("p (c v) -> p c v", c=CB), kT[:, P * b + HD:P * b + P], rev,
                       start=True, stop=True).then_inc(s["kv"], 1)

            def hgrn_out(hh):
                pe.wait_ge(s["hs_m"], hh + 1)
                pe.wait_ge(s["state"], hh + 1)
                if hh == 0:
                    pe.wait_ge(s["r_done"], 5)
                if hh == 2:
                    pe.wait_ge(s["ho_s"], 1)
                rows = slice(HD * (hh % 2), HD * (hh % 2) + HD)
                q = q_dec[hh]
                for b in range(NB):
                    mm(pb[7][rows, P * b:P * b + P], hv[:, b, HD * hh:HD * hh + HD], sc_a[hh % 2][:, P * b:P * b + P],
                       start=True, stop=False)
                    for c in range(CB * b, CB * b + CB):
                        t = slice(CH * c, CH * c + CH)
                        if c < NCH - 1:
                            last = mm(pb[4][rows, t], st_sb[HD:P, :, NCH - 2 - c], q[HD:P, t], start=True, stop=True)
                        if c > 0:
                            last = mm(pb[7][rows, t], st_sb[0:HD, :, c - 1], q[0:HD, t],
                                      start=False, stop=(c % CB == CB - 1))
                last.then_inc(s["ho"], 1)

            hgrn_in(0)
            hgrn_in(1)
            hgrn_out(0)
            hgrn_in(2)
            hgrn_out(1)
            hgrn_in(3)
            hgrn_out(2)
            hgrn_out(3)
            pe.wait_ge(s["hs_m"], HG)
            for p in range(2):
                pe.wait_ge(s["ho_q"], p + 1)
                mm(pb[5 + p][:, :], cst("head_ones"), o_rs[p], start=True, stop=True).then_inc(s["ho_m"], 1)

            def scores(u):
                a, b = divmod(u, NB)
                if u == 0:
                    pe.wait_ge(s["kv_e"], NB * HG)
                    pe.wait_ge(s["k_dup"], 4)
                if u >= 2:
                    pe.wait_ge(s["ex"], u - 1)
                r = slice(HD * (a % 2), HD * (a % 2) + HD)
                mm(pb[u % 2][:, :], aq[a // 2][r, P * b:P * b + P], k_dup[a // 4][r, :],
                   start=True, stop=True).then_inc(s["qk"], 1)

            def values(u):
                a, b = divmod(u, NB)
                pe.wait_ge(s["pt_e"], u + 1)
                pair = a // 2
                if u == 0:
                    pe.wait_ge(s["ho_s"], 2)
                    pe.wait_ge(s["ho_r"], 2)
                if u % (2 * NB) == 0 and pair >= 2:
                    pe.wait_ge(s["o_b"], pair - 1)
                r = slice(HD * (a % 2), HD * (a % 2) + HD)
                kv = a // 4
                for j in range(NB):
                    last = mm(pb[4 + pair % 2][r, P * b:P * b + P], av[:, j, HD * kv:HD * kv + HD],
                              pT_sb[u % 2][:, P * j:P * j + P], start=(j == 0), stop=(j == NB - 1))
                last.then_inc(s["pv"], 1)

            scores(0)
            for u in range(NU):
                if u + 1 < NU:
                    scores(u + 1)
                pe.wait_ge(s["pn"], u + 1)
                if u >= 2:
                    pe.wait_ge(s["pt_e"], u - 1)
                for j in range(NB):
                    last = tr(pb[2 + u % 2][:, P * j:P * j + P], p_sb[u % 2][:, P * j:P * j + P], ident)
                last.then_inc(s["pt"], 1)
                if u >= 1:
                    values(u - 1)
            values(NU - 1)

            pe.wait_ge(s["bc"], 2)
            pe.wait_ge(s["ex"], NU)
            pe.wait_ge(s["pt_e"], NU)
            pe.wait_ge(s["o_b"], 4)
            for q in range(8):
                for dg in range(4 * q, 4 * q + 4):
                    zero_power, i0 = (SC - 1, 0) if dg < G5 else (0, 1)
                    last = mm(pb[q][0:C5, P * (dg % 4):P * (dg % 4) + P], BtT[:, dg, zero_power, :],
                              Ct[:, dg, i0:i0 + SC, :].rearrange("p i c -> p (i c)"), start=True, stop=True)
                last.then_inc(s["kp"], 1)
            for q in range(8):
                pe.wait_ge(s["ke"], q + 1)
                for dg in range(4 * q, 4 * q + 4):
                    last = tr(pb[q][:, P * (dg % 4):P * (dg % 4) + P],
                              BtT[:, dg, :, :].rearrange("p s c -> p (s c)"), ident)
                last.then_inc(s["bt"], 1)
            pe.wait_ge(s["u_in"], 16 * SC)
            for q in range(4):
                pe.wait_ge(s["bt_e"], 8)
                for i in range(8):
                    dg = 8 * q + i
                    u = U5[:, dg % G5, :] if dg < G5 else U5[:, dg % G5, ::-1]
                    mm(pb[2 * q][:, NK * i:NK * i + NK], Bt[:, dg, :], u, start=True, stop=True)
                    mm(pb[2 * q + 1][0:HD, NK * i:NK * i + NK], Bt[:, dg, HD:P], u, start=True, stop=True)
                    last = mm(pb[2 * q + 1][HD:P, NK * i:NK * i + NK], Bt[:, dg, 0:HD], u, start=True, stop=True)
                last.then_inc(s["xin"], 1)
            pe.wait_ge(s["z"], 1)
            for q in range(4):
                last = mm(pb[q][:, :], cst("half_swap"), flat(T2[:, 8 * q:8 * q + 8, :]), start=True, stop=True)
            last.then_inc(s["zs"], 1)
            pe.wait_ge(s["m5"], 16 * (2 * SC - 1))
            pe.wait_ge(s["xs"], 1)
            for g in range(G5):
                y = pb[4 + g // 8][:, NK * (g % 8):NK * (g % 8) + NK]
                mm(y, M5[:, g, :], U5[:, g, :], start=True, stop=False)
                mm(y[:, 1:NK], Ct[:, g, 1:NPOW, :].rearrange("p i c -> p (i c)"), T2[:, g, 0:NK - 1],
                   start=False, stop=False)
                last = mm(y[:, 0:NK - 1], Ct[:, G5 + g, 0:SC, :].rearrange("p i c -> p (i c)"),
                          T2[:, G5 + g, NK - 2::-1], start=False, stop=True)
            last.then_inc(s["y5"], 1)
            pe.wait_ge(s["z5"], 2)
            for m in range(2):
                for k in range(2):
                    last = mm(pb[m][:, :], pcol("w_glu")[:, 256 * k + P * m:256 * k + P * m + P], yT[k],
                              start=(k == 0), stop=(k == 1))
                last.then_inc(s["glu"], 1)

            pe.wait_ge(s["o_a"], 2)
            pe.wait_ge(s["o_c"], 2)
            pe.wait_ge(slot[4], 32)
            pe.wait_ge(slot[5], 16)
            pe.wait_ge(s["y5_e"], 2)
            for b in range(NB):
                for n in range(2):
                    for k in range(KT):
                        last = mm(pb[2 * b + n][:, :], mixed[k][:, P * b:P * b + P], w_o[n][:, k, :],
                                  start=(k == 0), stop=(k == KT - 1))
                    last.then_inc(s["wo"], 1)

            pe.wait_ge(s["h2"], NB)
            for k in range(KT):
                for b in range(NB):
                    last = tr(pb[k][:, P * b:P * b + P], h[:, b, P * k:P * k + P], ident)
                last.then_inc(s["h2t"], 1)
            pe.wait_ge(s["h2_d"], KT // 2)
            pe.wait_ge(s["h2_a"], KT // 2)
            for b in range(NB):
                for k in range(KT):
                    last = mm(pb[0][:, RW * b:RW * b + RW], hT[:, k, P * b:P * b + P],
                              pcol("router_w")[:, RW * k:RW * k + RW], start=(k == 0), stop=(k == KT - 1))
            last.then_inc(s["rl"], 1)
            pe.wait_ge(s["sel"], 1)
            chosen = rt[8][:, 0:NB * NE].rearrange("p (b e) -> p b e", b=NB)
            for b in range(NB):
                for c in range(b + 1):
                    mm(pb[1][:, NE * b:NE * b + NE], cst("before") if c == b else cst("ones"), chosen[:, c, :],
                       start=(c == 0), stop=(c == b))
            for c in range(NB):
                last = mm(pb[1][:, P:P + NE], cst("ones"), chosen[:, c, :], start=(c == 0), stop=(c == NB - 1))
            last.then_inc(s["cnt"], 1)

            def tokens(e, par, loads):
                free = pe.snap(e - 1) if not isinstance(e, int) or e >= 2 else None
                landed = pe.snap(loads * 16)
                pe.wait_ge(xg_in[par], landed)
                if free is not None:
                    pe.wait_ge(s["xt_e"], free)
                pe.wait_ge(s["dest"], 1)
                mm(pb[par][:, 0:CAP], xg[par][0:CAP, 0::KT], ident[0:CAP, 0:CAP], start=True, stop=True)
                for k in range(1, KT):
                    last = tr(pb[par][:, CAP * k:CAP * k + CAP], xg[par][0:CAP, k::KT], ident[0:CAP, 0:CAP])
                last.then_inc(s["xt"], 1)

            def gate_up(e, par, loads):
                done, free = pe.snap(e + 1), (pe.snap(e - 1) if not isinstance(e, int) or e >= 2 else None)
                lot = [pe.snap((LOADS[3 * par + i] + loads) * 16) for i in range(2)]
                pe.wait_ge(s["xt_e"], done)
                if free is not None:
                    pe.wait_ge(s["hid"], free)
                pe.wait_ge(slot[3 * par], lot[0])
                pe.wait_ge(slot[3 * par + 1], lot[1])
                for k in range(KT):
                    mm(pb[2 + par][0:CAP, :], xT[par][:, k, :], W_gate[par][:, k, :], start=(k == 0), stop=(k == KT - 1))
                    last = mm(pb[2 + par][CAP:P, :], xT[par][:, k, :], W_up[par][:, k, :],
                              start=(k == 0), stop=(k == KT - 1))
                last.then_inc(s["gu"], 1)

            def hidden(e, par):
                done, free = pe.snap(e + 1), (pe.snap(e) if not isinstance(e, int) or e >= 1 else None)
                pe.wait_ge(s["hid"], done)
                if free is not None:
                    pe.wait_ge(s["ht_e"], free)
                pe.wait_ge(s["res"], 2 * NB)
                mm(pb[4][:, 0:CAP], hid[par][0:CAP, 0::FT], ident[0:CAP, 0:CAP], start=True, stop=True)
                for k in range(1, FT):
                    last = tr(pb[4][:, CAP * k:CAP * k + CAP], hid[par][0:CAP, k::FT], ident[0:CAP, 0:CAP])
                last.then_inc(s["ht"], 1)

            def down(e, par, loads):
                done, free = pe.snap(e + 1), (pe.snap(e - 1) if not isinstance(e, int) or e >= 2 else None)
                lot = pe.snap((LOADS[3 * par + 2] + loads) * 16)
                pe.wait_ge(s["ht_e"], done)
                if free is not None:
                    pe.wait_ge(s["ye"], free)
                pe.wait_ge(slot[3 * par + 2], lot)
                for k in range(FT):
                    mm(pb[5 + par][0:CAP, :], hidT[par][:, k, :], W_down[par][:, k, 0:512],
                       start=(k == 0), stop=(k == FT - 1))
                    last = mm(pb[5 + par][CAP:P, :], hidT[par][:, k, :], W_down[par][:, k, 512:1024],
                              start=(k == 0), stop=(k == FT - 1))
                last.then_inc(s["dn"], 1)

            tokens(0, 0, 1)
            gate_up(0, 0, 1)
            tokens(1, 1, 1)

            def pair(j):
                gate_up(j * 2 + 1, 1, j + 1)
                hidden(j * 2, 0)
                tokens(j * 2 + 2, 0, j + 2)
                down(j * 2, 0, j + 1)
                gate_up(j * 2 + 2, 0, j + 2)
                hidden(j * 2 + 1, 1)
                tokens(j * 2 + 3, 1, j + 2)
                down(j * 2 + 1, 1, j + 1)

            pair(0)
            with pe.Fori(1, NE // 2 - 1) as j:
                pair(j)
            gate_up(NE - 1, 1, NE // 2)
            hidden(NE - 2, 0)
            down(NE - 2, 0, NE // 2)
            hidden(NE - 1, 1)
            down(NE - 1, 1, NE // 2)
            pe.wait_ge(s["ye"], NE)
            n_over = pe.value_load(over_i[0:1, NOVER:NOVER + 1], min_val=0, max_val=NOVER)
            with pe.If(n_over > 0):
                with pe.Fori(0, n_over) as i:
                    tokens(i + NE, 0, i + NE // 2 + 1)
                    gate_up(i + NE, 0, i + NE // 2 + 1)
                    hidden(i + NE, 0)
                    down(i + NE, 0, i + NE // 2 + 1)

        def scalar_program(act, layer):
            A = nc.scalar.activation
            link = linker(act, s["act"])
            eps = cst("eps")
            act.dma_start(pk[:, :], pack[layer]).then_inc(s["pack"], 16)
            act.dma_start(gB[:, :], gains[layer, 0]).then_inc(s["gain1"], 16)

            def norm_scales(done):
                for b in range(NB):
                    ins = A(h[:, b, :], x[:, b, :], ACT.Square, accum_out=small[:, 36 + b:37 + b])
                    if b == NB - 1:
                        link(ins)
                link(A(small[:, 44:48], small[:, 36:40], ACT.Ln, bias=eps, scale=1.0 / D))
                A(small[:, 40:44], small[:, 44:48], ACT.Exp, scale=-0.5).then_inc(done, 1)

            def evacuate(n):
                act.wait_ge(s["pe"], n + 1)
                to, of = evac_views(n)
                A(to, of, ACT.Copy).then_inc(s["ev_a"], 1)

            norm_scales(s["rstd"])
            act.wait_ge(s["pack"], 16)
            lb_raw = pcol("lb")
            act.wait_ge(s["lb"], 1)
            A(lbs[:, 0:8], lbs[:, 0:8], ACT.Exp).then_inc(s["lb_e"], 1)
            for n in range(1, 14, 2):
                evacuate(n)

            jobs = [hq[0], hq[1]] + Z + hg

            def sig_exp(j):
                n = {0: 12, 1: 13, 2: 8, 3: 9, 4: 10, 5: 11, 6: 20, 7: 21}[j]
                wait_evacuated(act, n)
                if j:
                    act.wait_ge(s["sig_r"], j)
                A(ht_e, jobs[j], ACT.Exp, scale=-1.0).then_inc(s["sig_e"], 1)

            def q_copies(p):
                act.wait_ge(s["q_silu"], p + 1)
                for i in range(2):
                    for half in range(2):
                        A(q_dec[2 * p + i][HD * half:HD * half + HD, :], hq[p][HD * i:HD * i + HD, :],
                          ACT.Copy).then_inc(s["q_copy"], 1)

            def rope_square(j):
                wait_evacuated(act, [14, 16, 17, 18, 19][j])
                if j == 0:
                    act.wait_ge(s["pe"], 16)
                A(rope_sq[j], rope_x[j], ACT.Square).then_inc(s["r_sq"], 1)

            def rope_rstd(j):
                act.wait_ge(s["r_pe"], j + 1)
                link(A(rope_sq[j], pb[6][:, :], ACT.Ln, bias=eps, scale=1.0 / HD))
                A(rope_sq[j], rope_sq[j], ACT.Exp, scale=-0.5).then_inc(s["r_rs"], 1)

            sig_exp(0)
            sig_exp(1)
            q_copies(0)
            q_copies(1)
            evacuate(15)
            sig_exp(2)
            rope_square(0)
            evacuate(17)
            sig_exp(3)
            rope_square(1)
            rope_square(2)
            evacuate(19)
            rope_square(3)
            rope_square(4)
            sig_exp(4)
            rope_rstd(0)
            evacuate(21)
            sig_exp(5)
            rope_rstd(1)
            evacuate(23)
            rope_rstd(2)
            sig_exp(6)
            evacuate(25)
            rope_rstd(3)
            sig_exp(7)
            rope_rstd(4)

            def hgrn_copies(hh):
                act.wait_ge(s["ke_t"], hh + 1)
                if hh == 0:
                    act.wait_ge(s["pe"], NG)
                if hh >= 2:
                    act.wait_ge(s["kv"], NB * (hh - 1))
                A(k_endT[hh % 2], pb[0][:, :], ACT.Copy).then_inc(s["ke_e"], 1)
                act.wait_ge(s["kv"], NB * hh + NB)
                if hh:
                    act.wait_ge(s["state"], hh)
                for b in range(NB):
                    A(kv_sb[:, :, CB * b:CB * b + CB], pb[b][:, :].rearrange("p (c v) -> p v c", c=CB),
                      ACT.Copy).then_inc(s["kv_e"], 1)

            def pair_copy(p):
                act.wait_ge(s["ho"], 2 * p + 2)
                A(o_sb[p][:, 0:T - CH], pb[4][:, 0:T - CH], ACT.Copy).then_inc(s["ho_b"], 1)

            hgrn_copies(0)
            hgrn_copies(1)
            hgrn_copies(2)
            pair_copy(0)
            hgrn_copies(3)
            act.wait_ge(s["ho_s"], 1)
            A(o_rs[0], o_sb[0], ACT.Square).then_inc(s["ho_q"], 1)
            pair_copy(1)
            act.wait_ge(s["ho_s"], 2)
            A(o_rs[1], o_sb[1], ACT.Square).then_inc(s["ho_q"], 1)
            act.wait_ge(s["r_done"], 5)
            for kv in range(2):
                for half in range(2):
                    A(k_dup[kv][HD * half:HD * half + HD, :], ak[HD * kv:HD * kv + HD, :],
                      ACT.Copy).then_inc(s["k_dup"], 1)
            for p in range(2):
                act.wait_ge(s["ho_m"], p + 1)
                link(A(o_rs[p], pb[5 + p][:, :], ACT.Ln, bias=eps, scale=1.0 / HD))
                A(o_rs[p], o_rs[p], ACT.Exp, scale=-0.5).then_inc(s["ho_r"], 1)

            def probs(u):
                act.wait_ge(s["mx"], u + 1)
                if u >= 2:
                    act.wait_ge(s["pt"], u - 1)
                A(p_sb[u % 2], pb[u % 2][:, :], ACT.Exp, bias=small[:, 52 + u % 2:53 + u % 2], scale=SCALE,
                  accum_out=small[:, 48 + u % 2:49 + u % 2]).then_inc(s["ex"], 1)

            probs(0)
            for u in range(NU):
                if u + 1 < NU:
                    probs(u + 1)
                act.wait_ge(s["pt"], u + 1)
                if u >= 2:
                    act.wait_ge(s["pv"], u - 1)
                A(pT_sb[u % 2], pb[2 + u % 2][:, :], ACT.Copy).then_inc(s["pt_e"], 1)
                if u == 0:
                    act.wait_ge(s["s5p"], 16)
                    a0 = S5P["log_dt"][0]
                    A(pv_dt, s5[:, a0:a0 + DG], ACT.Exp).then_inc(s["dt"], 1)
                if u == 3:
                    act.wait_ge(s["ang"], 1)
                    A(pv_rho, pv_lr, ACT.Exp)
                    A(pv_rho8, pv_lr, ACT.Exp, scale=float(SC))
                    A(pv_sin, pv_r, ACT.Sin)
                    A(pv_cos, pv_rc, ACT.Sin).then_inc(s["lam"], 1)
                if u % (2 * NB) == 1 and u > 1:
                    pair = u // (2 * NB) - 1
                    act.wait_ge(s["pv"], 2 * NB * (pair + 1))
                    A(aq[pair], pb[4 + pair % 2][:, :], ACT.Copy).then_inc(s["o_b"], 1)
            act.wait_ge(s["pv"], NU)
            A(aq[3], pb[5][:, :], ACT.Copy).then_inc(s["o_b"], 1)

            for q in range(8):
                act.wait_ge(s["kp"], q + 1)
                to = (Kf if q < 4 else Kb)[:, 4 * (q % 4):4 * (q % 4) + 4, :, :].rearrange("p g i c -> p (g i c)")
                A(to, pb[q][0:C5, :], ACT.Copy).then_inc(s["ke"], 1)
            act.wait_ge(s["m5"], 16 * (2 * SC - 1))
            for q in range(8):
                act.wait_ge(s["bt"], q + 1)
                A(flat(Bt[:, 4 * q:4 * q + 4, :]), pb[q][:, :], ACT.Copy).then_inc(s["bt_e"], 1)
            act.wait_ge(s["y5"], 1)
            for i in range(2):
                A(flat(Y5[:, 8 * i:8 * i + 8, :]), pb[4 + i][:, :], ACT.Copy).then_inc(s["y5_e"], 1)
            for i in range(2):
                act.wait_ge(s["ge"], i + 1)
                A(gt[i], gt[i], ACT.Exp, scale=-2.0 * float(np.sqrt(2.0 / np.pi))).then_inc(s["gx"], 1)
            for i in range(2):
                act.wait_ge(s["glu"], i + 1)
                A(gt[i], pb[i][:, :], ACT.Exp, scale=-1.0, bias=small[:, 56 + i:57 + i]).then_inc(s["glx"], 1)

            act.wait_ge(s["res"], 2 * NB)
            act.wait_ge(s["o_c"], 2)
            norm_scales(s["rstd2"])
            for k in range(1, KT, 2):
                act.wait_ge(s["h2t"], k + 1)
                A(hT[:, k, :], pb[k][:, :], ACT.Copy).then_inc(s["h2_a"], 1)
            act.wait_ge(s["gs"], 1)
            A(rt[1][:, 0:16], rt[1][:, 0:16], ACT.Exp).then_inc(s["gx2"], 1)
            act.wait_ge(s["sel"], 1)
            A(small[:, 32:36], small[:, 28:32], ACT.Exp).then_inc(s["sx"], 1)

            def load_tokens(e, par):
                row = act.snap(e * CAP)
                act.dma_start(xg[par][0:CAP, :], xbuf[bass.ds(row, CAP), :]).then_inc(xg_in[par], 16)

            def tokens(e, par, ahead=True):
                done, free = act.snap(e + 1), (act.snap(e - 1) if not isinstance(e, int) or e >= 2 else None)
                act.wait_ge(s["xt"], done)
                if ahead:
                    load_tokens(e + 2, par)
                if free is not None:
                    act.wait_ge(s["gu"], free)
                A(flat(xT[par]), pb[par][:, :], ACT.Copy).then_inc(s["xt_e"], 1)

            def gate_exp(e, par):
                done, free = act.snap(e + 1), (act.snap(e) if not isinstance(e, int) or e >= 1 else None)
                act.wait_ge(s["gu"], done)
                if free is not None:
                    act.wait_ge(s["er"], free)
                A(e_e[0:CAP, :], pb[2 + par][0:CAP, :], ACT.Exp, scale=-1.0).then_inc(s["ee"], 1)

            def rows(e, par, before):
                done, stored = act.snap(e + 1), act.snap(before * 32)
                row = act.snap(e * CAP)
                act.wait_ge(s["dn"], done)
                act.wait_ge(y_out[par], stored)
                A(y_sb[par], pb[5 + par][:, :], ACT.Copy).then_inc(s["ye"], 1)
                act.wait_ge(s["ye"], done)
                for n in range(2):
                    act.dma_start(ybuf[bass.ds(row, CAP), 512 * n:512 * n + 512],
                                  y_sb[par][CAP * n:CAP * n + CAP, :]).then_inc(y_out[par], 16)

            dispatched = act.snap(layer * PER_LAYER + PER_LAYER)
            act.wait_ge(s_dispatched, dispatched)
            load_tokens(0, 0)
            load_tokens(1, 1)
            tokens(0, 0)
            gate_exp(0, 0)
            tokens(1, 1)

            def pair(j):
                gate_exp(j * 2 + 1, 1)
                tokens(j * 2 + 2, 0)
                rows(j * 2, 0, j)
                gate_exp(j * 2 + 2, 0)
                tokens(j * 2 + 3, 1)
                rows(j * 2 + 1, 1, j)

            pair(0)
            with act.Fori(1, NE // 2 - 2) as j:
                pair(j)
            gate_exp(NE - 3, 1)
            tokens(NE - 2, 0, ahead=False)
            rows(NE - 4, 0, NE // 2 - 2)
            gate_exp(NE - 2, 0)
            tokens(NE - 1, 1, ahead=False)
            rows(NE - 3, 1, NE // 2 - 2)
            gate_exp(NE - 1, 1)
            rows(NE - 2, 0, NE // 2 - 1)
            rows(NE - 1, 1, NE // 2 - 1)
            n_over = act.value_load(over_i[0:1, NOVER:NOVER + 1], min_val=0, max_val=NOVER)
            all_even = act.snap((n_over + NE // 2) * 32)
            with act.If(n_over > 0):
                with act.Fori(0, n_over) as i:
                    load_tokens(i + NE, 0)
                    tokens(i + NE, 0, ahead=False)
                    gate_exp(i + NE, 0)
                    rows(i + NE, 0, i + NE // 2)
            act.wait_ge(y_out[1], 32 * (NE // 2))
            act.wait_ge(y_out[0], all_even)
            A(small[:, 63:64], eps, ACT.Copy).then_inc(s["stored"], 1)

        (pv_dt, pv_lr, pv_r, pv_rc, pv_rho, pv_rho8, pv_sin, pv_cos, pv_fr, pv_fi) = ss

        def vector_program(dve, layer):
            V = nc.vector
            TS, TT, STT = V.tensor_scalar, V.tensor_tensor, V.scalar_tensor_tensor
            link = linker(dve, s["dve"])

            def h_rows(scale_sem, done):
                dve.wait_ge(scale_sem, 1)
                for b in range(NB):
                    STT(out=h[:, b, :], in0=x[:, b, :], scalar=small[:, 40 + b:41 + b], in1=gB[:, :],
                        op0=ALU.mult, op1=ALU.mult).then_inc(done, 1)

            def evacuate(n):
                dve.wait_ge(s["pe"], n + 1)
                to, of = evac_views(n)
                V.tensor_copy(to, of).then_inc(s["ev_d"], 1)

            dve.wait_ge(s["pack"], 16)
            lb = pcol("lb").rearrange("p (l h) -> p l h", l=L)
            link(TT(lbs[:, 8:12], lb[:, 0, :], lb[:, 1, :], ALU.max))
            for j in range(L):
                ins = TT(lbs[:, 4 * j:4 * j + 4], lb[:, j, :], lbs[:, 8:12], ALU.subtract)
            ins.then_inc(s["lb"], 1)
            dve.wait_ge(s["gain1"], 16)
            h_rows(s["rstd"], s["h"])
            dve.wait_ge(s["lb_e"], 1)
            link(TT(lbs[:, 8:12], lbs[:, 0:4], lbs[:, 4:8], ALU.add))
            link(V.reciprocal(lbs[:, 8:12], lbs[:, 8:12]))
            ws = pcol("lb_sum")
            link(TS(lbs[:, 12:16], lbs[:, 0:4], ws[:, 0:1], None, ALU.mult))
            link(STT(out=lbs[:, 12:16], in0=lbs[:, 4:8], scalar=ws[:, 1:2], in1=lbs[:, 12:16], op0=ALU.mult, op1=ALU.add))
            link(TT(lbs[:, 12:16], lbs[:, 12:16], lbs[:, 8:12], ALU.mult))
            link(TS(lbs[:, 16:20], lbs[:, 12:16], -1.0, 1.0, ALU.mult, ALU.add))
            link(TS(small[:, 56:58], pcol("b_glu"), -1.0, None, ALU.mult))
            for n in range(0, 14, 2):
                evacuate(n)

            def sigmoid(j):
                dve.wait_ge(s["sig_e"], j + 1)
                link(TS(ht_s, ht_e, 1.0, None, ALU.add))
                link(V.reciprocal(ht_s, ht_s))

            def silu(j, z, count):
                sigmoid(j)
                ins = TT(z, z, ht_s, ALU.mult)
                ins.then_inc(s["q_silu"], 1)
                dve.wait_ge(s["q_silu"], count)
                V.memset(small[:, 60:61], 0.0).then_inc(s["sig_r"], 1)

            def gate_chain(hh):
                one_less = lbs[:, 16 + hh:17 + hh]
                bound = lbs[:, 12 + hh:13 + hh]
                dve.wait_ge(s["sig_e"], 3 + hh)
                link(TS(ht_e, ht_e, 1.0e30, None, ALU.min))
                sigmoid(2 + hh)
                if hh:
                    dve.wait_ge(s["f_split"], hh)
                link(TS(ht_f, ht_s, one_less, bound, ALU.mult, ALU.add))
                V.memset(small[:, 61:62], 0.0).then_inc(s["f_ready"], 1)
                link(STT(out=ht_k, in0=ht_e, scalar=one_less, in1=ht_s, op0=ALU.mult, op1=ALU.mult))
                V.memset(small[:, 60:61], 0.0).then_inc(s["sig_r"], 1)
                dve.wait_ge(s["f_split"], hh + 1)
                V.tensor_tensor_scan(out=ht_F[0:HD, :], data0=ht_d0[0:HD, :], data1=ht_d1[0:HD, :], initial=0.0,
                                     op0=ALU.mult, op1=ALU.add)
                link(V.tensor_tensor_scan(out=ht_F[HD:P, ::-1], data0=ht_d0[HD:P, ::-1], data1=ht_d1[HD:P, ::-1],
                                          initial=0.0, op0=ALU.mult, op1=ALU.add))
                V.tensor_copy(dec_n[0:HD, :], ht_F[0:HD, CH - 1::CH])
                V.tensor_copy(dec_n[HD:P, :], ht_F[HD:P, 0::CH])
                V.tensor_copy(dec_s[hh][0:HD, :], ht_F[0:HD, CH - 1::CH])
                V.tensor_copy(dec_s[hh][HD:P, :], ht_F[HD:P, T - CH::-CH])
                link(V.reciprocal(ht_R, ht_F))
                V.memset(dec_s[hh][:, 0:1], 0.0)
                if hh == 0:
                    dve.wait_ge(s["pe"], NG if False else KT + 1)
                link(TT(k_dec[hh], ht_k, ht_R, ALU.mult))
                TT(k_end[hh].rearrange("p (c t) -> p c t", t=CH), k_dec[hh].rearrange("p (c t) -> p c t", t=CH),
                   dec_n[:, :, None].broadcast_to([P, NCH, CH]), ALU.mult)
                dve.wait_ge(s["q_copy"], 8)
                TT(q_dec[hh], q_dec[hh], ht_F, ALU.mult).then_inc(s["head"], 1)
                dve.wait_ge(s["head"], hh + 1)

            def rope_gain(j):
                dve.wait_ge(s["r_sq"], j + 1)
                TS(rope_x[j], rope_x[j], pcol("k_g" if j == 0 else "q_g"), None, ALU.mult).then_inc(s["r_y"], 1)

            def rope_turn(j):
                dve.wait_ge(s["r_pe"], j + 1)
                TT(rope_t, pb[7][:, :], cst("sin"), ALU.mult)
                link(TT(rope_x[j], rope_x[j], cst("cos"), ALU.mult))
                link(TT(rope_x[j], rope_x[j], rope_t, ALU.add))
                dve.wait_ge(s["r_rs"], j + 1)
                TT(rope_x[j], rope_x[j], rope_sq[j], ALU.mult).then_inc(s["r_done"], 1)
                dve.wait_ge(s["r_done"], j + 1)

            silu(0, hq[0], 1)
            silu(1, hq[1], 2)
            evacuate(14)
            gate_chain(0)
            evacuate(16)
            rope_gain(0)
            rope_gain(1)
            gate_chain(1)
            evacuate(18)
            rope_gain(2)
            rope_gain(3)
            rope_turn(0)
            gate_chain(2)
            evacuate(20)
            rope_gain(4)
            rope_turn(1)
            gate_chain(3)
            evacuate(22)
            rope_turn(2)
            evacuate(24)
            silu(6, hg[0], 3)
            rope_turn(3)
            silu(7, hg[1], 4)
            rope_turn(4)

            def masked_scores(hh):
                dve.wait_ge(s["hs_pe"], hh + 1)
                if hh >= 2:
                    dve.wait_ge(s["ho"], hh - 1)
                if hh == 0:
                    dve.wait_ge(s["pe"], NG)
                mask = [cst(m)[:, None, :].broadcast_to([P, NB, P]) for m in ("mask_f", "mask_b")]
                b4 = lambda ap: ap.rearrange("p (b t) -> p b t", b=NB)
                TT(b4(sc_t), b4(pb[5][:, :]), mask[0], ALU.mult)
                link(TT(b4(sc_a[hh % 2]), b4(pb[6][:, :]), mask[1], ALU.mult))
                TT(sc_a[hh % 2], sc_a[hh % 2], sc_t, ALU.add).then_inc(s["hs_m"], 1)
                dve.wait_ge(s["hs_m"], hh + 1)

            def states(hh):
                dve.wait_ge(s["kv_e"], NB * hh + NB)
                dve.wait_ge(s["dec"], hh + 1)
                if hh:
                    dve.wait_ge(s["ho"], hh)
                V.tensor_tensor_scan(out=flat(st_sb), data0=flat(dec_sb), data1=flat(kv_sb), initial=0.0,
                                     op0=ALU.mult, op1=ALU.add).then_inc(s["state"], 1)

            def pair_sum(p):
                dve.wait_ge(s["ho_b"], p + 1)
                V.tensor_copy(o_sb[p][:, T - CH:T], pb[7][:, T - CH:T])
                TT(o_sb[p][:, 0:T - CH], o_sb[p][:, 0:T - CH], pb[7][:, 0:T - CH], ALU.add).then_inc(s["ho_s"], 1)

            masked_scores(0)
            states(0)
            masked_scores(1)
            states(1)
            masked_scores(2)
            states(2)
            pair_sum(0)
            masked_scores(3)
            states(3)
            pair_sum(1)

            def row_max(u):
                dve.wait_ge(s["qk"], u + 1)
                if u >= 2:
                    dve.wait_ge(s["ex"], u - 1)
                link(V.reduce_max(small[:, 50 + u % 2:51 + u % 2], pb[u % 2][:, :], AX.X))
                TS(small[:, 52 + u % 2:53 + u % 2], small[:, 50 + u % 2:51 + u % 2], -SCALE, None,
                   ALU.mult).then_inc(s["mx"], 1)

            def head_norm(p):
                dve.wait_ge(s["ho_r"], p + 1)
                link(STT(out=o_sb[p], in0=o_sb[p], scalar=pcol("hgrn_g"), in1=o_rs[p], op0=ALU.mult, op1=ALU.mult))
                TT(hq[p], o_sb[p], hg[p], ALU.mult).then_inc(s["o_a"], 1)

            row_max(0)
            for u in range(NU):
                if u + 1 < NU:
                    row_max(u + 1)
                dve.wait_ge(s["ex"], u + 1)
                link(V.reciprocal(small[:, 54 + u % 2:55 + u % 2], small[:, 48 + u % 2:49 + u % 2]))
                TS(p_sb[u % 2], p_sb[u % 2], small[:, 54 + u % 2:55 + u % 2], None, ALU.mult).then_inc(s["pn"], 1)
                if u < 2:
                    head_norm(u)
                if u == 5:
                    dve.wait_ge(s["den"], 1)
                    V.reciprocal(pv_rc, pv_dt).then_inc(s["inv"], 1)

            dve.wait_ge(s["ke"], 8)
            diag_f, diag_b = Kf[:, :, 0, :], Kb[:, :, SC - 1, :]
            TT(diag_f, diag_f, diag_b, ALU.add).then_inc(s["kdiag"], 1)
            dve.wait_ge(s["bt"], 8)
            for q in range(4):
                dve.wait_ge(s["xin"], q + 1)
                if q == 0:
                    dve.wait_ge(s["tab"], 1)
                r = slice(8 * q, 8 * q + 8)
                a = pb[2 * q][:, :].rearrange("p (d k) -> p d k", d=8)
                b = pb[2 * q + 1][:, :].rearrange("p (d k) -> p d k", d=8)
                TT(T1[:, r, :], a, cosT[:, r, :], ALU.mult)
                link(TT(T2[:, r, :], b, sinT[:, r, :], ALU.mult))
                link(TT(T1[:, r, :], T1[:, r, :], T2[:, r, :], ALU.add))
            dve.wait_ge(s["rho"], 1)
            V.tensor_tensor_scan(out=flat(T2), data0=flat(rho), data1=flat(T1), initial=0.0,
                                 op0=ALU.mult, op1=ALU.add).then_inc(s["z"], 1)
            dve.wait_ge(s["z"], 1)
            link(TT(flat(T1), flat(T2), flat(cosT), ALU.mult))
            dve.wait_ge(s["zs"], 1)
            for q in range(4):
                r = slice(8 * q, 8 * q + 8)
                link(TT(T2[:, r, :], pb[q][:, :].rearrange("p (d k) -> p d k", d=8), sinT[:, r, :], ALU.mult))
            TT(flat(T2), flat(T1), flat(T2), ALU.subtract).then_inc(s["xs"], 1)
            dve.wait_ge(s["y_in"], 32)
            dve.wait_ge(s["y5"], 1)
            for m in range(2):
                z, t, r = yT[m], gt[m], gt[2 + m]
                link(STT(out=z, in0=uT[m], scalar=pcol("s5_d")[:, m:m + 1], in1=z, op0=ALU.mult, op1=ALU.add))
                link(TT(t, z, z, ALU.mult))
                link(TS(t, t, 0.044715, 1.0, ALU.mult, ALU.add))
                link(TT(t, t, z, ALU.mult))
                TS(t, t, -50.0, None, ALU.max).then_inc(s["ge"], 1)
            for m in range(2):
                z, t, r = yT[m], gt[m], gt[2 + m]
                dve.wait_ge(s["gx"], m + 1)
                link(TS(r, t, 1.0, None, ALU.add))
                link(V.reciprocal(r, r))
                TT(z, z, r, ALU.mult).then_inc(s["z5"], 1)
            for m in range(2):
                z, t, r = yT[m], gt[m], gt[2 + m]
                dve.wait_ge(s["glx"], m + 1)
                dve.wait_ge(s["z5"], 2)
                link(TS(r, t, 1.0, None, ALU.add))
                link(V.reciprocal(r, r))
                TT(uT[m].rearrange("p (k t) -> p t k", t=SC), z.rearrange("p (t k) -> p t k", t=SC),
                   r.rearrange("p (t k) -> p t k", t=SC), ALU.mult).then_inc(s["o_c"], 1)
            for n in range(2 * NB):
                b, half = divmod(n, 2)
                dve.wait_ge(s["wo"], n + 1)
                xs = x[:, b, 512 * half:512 * half + 512]
                TT(xs, xs, pb[n][:, :], ALU.add).then_inc(s["res"], 1)
            dve.wait_ge(s["gain2"], 16)
            h_rows(s["rstd2"], s["h2"])
            for k in range(0, KT, 2):
                dve.wait_ge(s["h2t"], k + 1)
                V.tensor_copy(hT[:, k, :], pb[k][:, :]).then_inc(s["h2_d"], 1)

            def v3(i, n):
                return rt[i][:, 0:NB * n].rearrange("p (b e) -> p b e", b=NB)

            def bc(ap, n):
                return ap[:, :, None].broadcast_to([P, NB, n])

            def per_block(ap, n):
                return ap[:, None, :].broadcast_to([P, NB, n])

            logits = v3(0, RW)
            dve.wait_ge(s["rl"], 1)
            link(TT(logits, pb[0][:, 0:NB * RW].rearrange("p (b e) -> p b e", b=NB), per_block(pcol("router_b"), RW), ALU.add))
            g_log, e_log = logits[:, :, 0:EG], logits[:, :, EG:RW]
            g_rel, g_hot, e_in, hot1, hot2, e_tmp = v3(1, EG), v3(2, EG), v3(3, NE), v3(4, NE), v3(5, NE), v3(6, NE)
            chosen, e_msk = v3(8, NE), v3(7, NE)
            col = [rt[9][:, 4 * i:4 * i + 4] for i in range(10)]

            def first_of(hot, values, top, ids, n):
                link(TT(hot, values, bc(top, n), ALU.is_equal))
                link(TT(hot, hot, per_block(ids, n), ALU.mult))
                link(V.tensor_reduce(out=col[9], in_=hot, axis=AX.X, op=ALU.min))
                link(TT(hot, per_block(ids, n), bc(col[9], n), ALU.is_equal))

            link(V.reduce_max(col[0], g_log, AX.X))
            TT(g_rel, g_log, bc(col[0], EG), ALU.subtract).then_inc(s["gs"], 1)
            first_of(g_hot, g_log, col[0], cst("group_id"), EG)
            grp = lambda ap: ap.rearrange("p b (g e) -> p b g e", g=EG)
            for b in range(NB):
                link(TT(e_in[:, b, :].rearrange("p (g e) -> p g e", g=EG), e_log[:, b, :].rearrange("p (g e) -> p g e", g=EG),
                        g_hot[:, b, :, None].broadcast_to([P, EG, EPG]), ALU.mult))
                link(V.tensor_copy(e_tmp[:, b, :].rearrange("p (g e) -> p g e", g=EG),
                                   g_hot[:, b, :, None].broadcast_to([P, EG, EPG])))
            link(TS(rt[6][:, 0:NB * NE], rt[6][:, 0:NB * NE], 1.0, NEG, ALU.subtract, ALU.mult))
            link(TT(e_in, e_in, e_tmp, ALU.add))
            link(V.reduce_max(col[1], e_in, AX.X))
            first_of(hot1, e_in, col[1], cst("expert_id"), NE)
            link(STT(out=rt[7][:, 0:NB * NE], in0=rt[4][:, 0:NB * NE], scalar=-2.0 * NEG, in1=rt[3][:, 0:NB * NE],
                     op0=ALU.mult, op1=ALU.add))
            link(V.reduce_max(col[2], e_msk, AX.X))
            first_of(hot2, e_msk, col[2], cst("expert_id"), NE)
            link(TT(chosen, hot1, hot2, ALU.add))
            TT(small[:, 28:32], col[2], col[1], ALU.subtract).then_inc(s["sel"], 1)
            dve.wait_ge(s["gx2"], 1)
            link(V.tensor_reduce(out=col[3], in_=g_rel, axis=AX.X, op=ALU.add))
            link(V.reciprocal(col[3], col[3]))
            dve.wait_ge(s["sx"], 1)
            link(TS(col[4], small[:, 32:36], 1.0, None, ALU.add))
            link(V.reciprocal(col[4], col[4]))
            link(TT(gate_w[:, 0:NB], col[4], col[3], ALU.mult))
            link(TT(gate_w[:, NB:2 * NB], gate_w[:, 0:NB], small[:, 32:36], ALU.mult))
            dve.wait_ge(s["cnt"], 1)
            pos, cnt = v3(6, NE), rt[10][:, 0:NE]
            ext, run, base = rt[10][:, 32:64], rt[10][:, 64:96], rt[10][:, 96:128]
            link(V.tensor_copy(rt[6][:, 0:NB * NE], pb[1][:, 0:NB * NE]))
            link(V.tensor_copy(cnt, pb[1][:, P:P + NE]))
            many = qd[:, 1760:1760 + 7 * NE].rearrange("p (e m) -> p e m", m=7)
            link(TT(many, cnt[:, :, None].broadcast_to([P, NE, 7]), cst("chunk_end")[:, None, :].broadcast_to([P, NE, 7]),
                    ALU.is_gt))
            link(V.tensor_reduce(out=ext, in_=many, axis=AX.X, op=ALU.add))
            link(V.tensor_tensor_scan(out=run, data0=cst("ones")[:, 0:NE], data1=ext, initial=0.0,
                                      op0=ALU.mult, op1=ALU.add))
            link(TT(base, run, ext, ALU.subtract))
            link(TS(base, base, float(CAP), float((NE - 1) * CAP), ALU.mult, ALU.add))
            link(TT(base, base, cst("expert_row"), ALU.subtract))
            far = v3(7, NE)
            link(TS(rt[7][:, 0:NB * NE], rt[6][:, 0:NB * NE], float(CAP), None, ALU.is_ge))
            link(TT(far, far, per_block(base, NE), ALU.mult))
            link(TT(far, far, per_block(cst("expert_row"), NE), ALU.add))
            link(TT(far, far, pos, ALU.add))
            for j, hot in enumerate((hot1, hot2)):
                link(TT(pos, far, hot, ALU.mult))
                link(V.tensor_reduce(out=col[5 + j], in_=pos, axis=AX.X, op=ALU.add))
                link(V.tensor_copy(dest_i[:, NB * j:NB * j + NB], col[5 + j]))
            over = qd[:, 1760 - 0:1760 + 0 + 224]
            wide = hbuf[:, 4096:4096 + NOVER * NE].rearrange("p (i e) -> p i e", i=NOVER)
            link(TT(wide, run[:, None, :].broadcast_to([P, NOVER, NE]),
                    cst("over_id")[:, :, None].broadcast_to([P, NOVER, NE]), ALU.is_le))
            link(V.tensor_reduce(out=rt[9][:, 100:100 + NOVER], in_=wide, axis=AX.X, op=ALU.add))
            link(TS(rt[9][:, 100:100 + NOVER], rt[9][:, 100:100 + NOVER], float(NE - 1), None, ALU.min))
            link(V.tensor_copy(over_i[:, 0:NOVER], rt[9][:, 100:100 + NOVER]))
            V.tensor_copy(over_i[:, NOVER:NOVER + 1], run[:, NE - 1:NE]).then_inc(s["dest"], 1)

            def hidden_rows(e, par):
                done, free = dve.snap(e + 1), (dve.snap(e - 1) if not isinstance(e, int) or e >= 2 else None)
                steps = [dve.snap(e * 3 + 1 + i) for i in range(3)]
                dve.wait_ge(s["ee"], done)
                if free is not None:
                    dve.wait_ge(s["ht"], free)
                top, bottom = pb[2 + par][0:CAP, :], pb[2 + par][CAP:P, :]
                TS(e_s[0:CAP, :], e_e[0:CAP, :], 1.0, None, ALU.add).then_inc(s["ec"], 1)
                dve.wait_ge(s["ec"], steps[0])
                V.reciprocal(e_s[0:CAP, :], e_s[0:CAP, :]).then_inc(s["ec"], 1)
                dve.wait_ge(s["ec"], steps[1])
                V.memset(small[:, 62:63], 0.0).then_inc(s["er"], 1)
                TT(e_s[0:CAP, :], e_s[0:CAP, :], top, ALU.mult).then_inc(s["ec"], 1)
                dve.wait_ge(s["ec"], steps[2])
                TT(hid[par][0:CAP, :], e_s[0:CAP, :], bottom, ALU.mult).then_inc(s["hid"], 1)

            def hidden_t(e, par):
                done, free = dve.snap(e + 1), (dve.snap(e - 1) if not isinstance(e, int) or e >= 2 else None)
                dve.wait_ge(s["ht"], done)
                if free is not None:
                    dve.wait_ge(s["dn"], free)
                V.tensor_copy(flat(hidT[par]), pb[4][:, 0:FT * CAP]).then_inc(s["ht_e"], 1)

            hidden_rows(0, 0)

            def pair(j):
                hidden_t(j * 2, 0)
                hidden_rows(j * 2 + 1, 1)
                hidden_t(j * 2 + 1, 1)
                hidden_rows(j * 2 + 2, 0)

            pair(0)
            with dve.Fori(1, NE // 2 - 1) as j:
                pair(j)
            hidden_t(NE - 2, 0)
            hidden_rows(NE - 1, 1)
            hidden_t(NE - 1, 1)
            dve.wait_ge(s["dn"], NE)
            n_over = dve.value_load(over_i[0:1, NOVER:NOVER + 1], min_val=0, max_val=NOVER)
            with dve.If(n_over > 0):
                with dve.Fori(0, n_over) as i:
                    hidden_rows(i + NE, 0)
                    hidden_t(i + NE, 0)
            gathered = dve.snap(layer * PER_LAYER + PER_LAYER)
            dve.wait_ge(s_gathered, gathered)
            for j in range(2):
                for b in range(NB):
                    i = NB * j + b
                    if j:
                        dve.wait_ge(s["moe"], b + 1)
                    STT(out=x[:, b, :], in0=hbuf[:, D * i:D * i + D], scalar=gate_w[:, i:i + 1], in1=x[:, b, :],
                        op0=ALU.mult, op1=ALU.add).then_inc(s["moe"], 1)

        def pool_program(pool, layer):
            G = nc.gpsimd
            TS, TT = G.tensor_scalar, G.tensor_tensor
            link = linker(pool, s["pool"])
            for hh in range(HG):
                pool.wait_ge(s["f_ready"], hh + 1)
                if hh:
                    pool.wait_ge(s["head"], hh)
                link(TT(ht_d1, ht_f, cst("chunk_start"), ALU.mult))
                TT(ht_d0, ht_f, ht_d1, ALU.subtract).then_inc(s["f_split"], 1)
            wait_evacuated(pool, 22)
            wait_evacuated(pool, 23)
            pool.wait_ge(s["pe"], NG)
            for hh in range(HG):
                pool.wait_ge(s["head"], hh + 1)
                if hh:
                    pool.wait_ge(s["state"], hh)
                G.tensor_copy(dec_sb, dec_s[hh][:, None, :].broadcast_to([P, HD, NCH])).then_inc(s["dec"], 1)
                for b in range(NB):
                    n = NB * hh + b
                    if n >= 2:
                        pool.wait_ge(s["kv"], n - 1)
                    TT(v_blk[b % 2].rearrange("p (c v) -> p c v", c=CB),
                       hv[:, b, HD * hh:HD * hh + HD][:, None, :].broadcast_to([P, CB, HD]),
                       cst("chunk_of")[:, :, None].broadcast_to([P, CB, HD]), ALU.mult).then_inc(s["vb"], 1)

            def sp(name):
                a, n = S5P[name]
                return s5[:, a:a + n]

            pool.wait_ge(s["s5p"], 16)
            pool.wait_ge(s["o_a"], 2)
            pool.wait_ge(s["r_done"], 5)
            pool.wait_ge(s["dt"], 1)
            tmp = [Wr[:, i, :] for i in range(4)]
            link(TT(pv_lr, sp("a_re"), pv_dt, ALU.mult))
            link(TT(pv_sin, sp("a_im"), pv_dt, ALU.mult))
            link(TS(tmp[0], pv_sin, float(1.0 / TWO_PI), ROUND, ALU.mult, ALU.add))
            link(TS(tmp[0], tmp[0], ROUND, None, ALU.subtract))
            for part in TURN:
                link(TS(tmp[1], tmp[0], -part, None, ALU.mult))
                link(TT(pv_sin, pv_sin, tmp[1], ALU.add))
            link(TS(pv_r, pv_sin, PI_DOWN, -PI_DOWN, ALU.min, ALU.max))
            link(TS(tmp[1], pv_r, 0.0, 2.0, ALU.max, ALU.mult))
            link(TT(tmp[1], pv_r, tmp[1], ALU.subtract))
            TS(pv_rc, tmp[1], float(np.pi / 2), None, ALU.add).then_inc(s["ang"], 1)
            pool.wait_ge(s["lam"], 1)
            c1, s1, c2, s2 = Wi[:, 0, :], Wi[:, 1, :], Wi[:, 2, :], Wi[:, 3, :]
            link(G.tensor_copy(c1, pv_cos))
            link(G.tensor_copy(s1, pv_sin))

            def square(c, sn, t0, t1):
                link(TT(t0, c, c, ALU.mult))
                link(TT(t1, sn, sn, ALU.mult))
                link(TT(sn, sn, c, ALU.mult))
                link(TT(sn, sn, sn, ALU.add))
                link(TT(c, t0, t1, ALU.subtract))

            for _ in range(3):
                square(c1, s1, c2, s2)
            tm = s_tmp[:, 0:DG * NK // 2].rearrange("p (d k) -> p d k", d=DG)
            G.memset(cosT[:, :, 0], 1.0)
            link(G.memset(sinT[:, :, 0], 0.0))
            n = 1
            while n < NK:
                lo, hi = slice(0, n), slice(n, 2 * n)
                cb, sb_ = (a[:, :, None].broadcast_to([P, DG, n]) for a in (c1, s1))
                t = tm[:, :, 0:n]
                link(TT(cosT[:, :, hi], cosT[:, :, lo], cb, ALU.mult))
                link(TT(t, sinT[:, :, lo], sb_, ALU.mult))
                link(TT(cosT[:, :, hi], cosT[:, :, hi], t, ALU.subtract))
                link(TT(sinT[:, :, hi], sinT[:, :, lo], cb, ALU.mult))
                link(TT(t, cosT[:, :, lo], sb_, ALU.mult))
                link(TT(sinT[:, :, hi], sinT[:, :, hi], t, ALU.add))
                square(c1, s1, c2, s2)
                n *= 2
            TS(flat(sinT), flat(sinT), cst("sign"), None, ALU.mult).then_inc(s["tab"], 1)
            pool.wait_ge(s["tab"], 1)
            link(TT(pv_cos, pv_cos, pv_rho, ALU.mult))
            link(TT(pv_sin, pv_sin, pv_rho, ALU.mult))
            G.memset(Wr[:, 0, :], 1.0)
            link(G.memset(Wi[:, 0, :], 0.0))
            link(G.tensor_copy(Wr[:, 1, :], pv_cos))
            link(G.tensor_copy(Wi[:, 1, :], pv_sin))
            for n in (1, 2, 4):
                lo, hi = slice(1, n + 1), slice(n + 1, 2 * n + 1)
                br, bi = (a[:, n, :][:, None, :].broadcast_to([P, n, DG]) for a in (Wr, Wi))
                t = A1[:, 0:n, :]
                link(TT(Wr[:, hi, :], Wr[:, lo, :], br, ALU.mult))
                link(TT(t, Wi[:, lo, :], bi, ALU.mult))
                link(TT(Wr[:, hi, :], Wr[:, hi, :], t, ALU.subtract))
                link(TT(Wi[:, hi, :], Wr[:, lo, :], bi, ALU.mult))
                link(TT(t, Wi[:, lo, :], br, ALU.mult))
                link(TT(Wi[:, hi, :], Wi[:, hi, :], t, ALU.add))
            t0, t1, t2 = A1[:, 0, :], A1[:, 1, :], A1[:, 2, :]
            link(TT(t0, sp("a_re"), sp("a_re"), ALU.mult))
            link(TT(t1, sp("a_im"), sp("a_im"), ALU.mult))
            TT(pv_dt, t0, t1, ALU.add).then_inc(s["den"], 1)
            link(TS(t2, pv_cos, 1.0, None, ALU.subtract))
            link(TT(pv_fr, t2, sp("a_re"), ALU.mult))
            link(TT(t0, pv_sin, sp("a_im"), ALU.mult))
            link(TT(pv_fr, pv_fr, t0, ALU.add))
            link(TT(pv_fi, pv_sin, sp("a_re"), ALU.mult))
            link(TT(t0, t2, sp("a_im"), ALU.mult))
            link(TT(pv_fi, pv_fi, t0, ALU.subtract))
            pool.wait_ge(s["inv"], 1)
            link(TT(pv_fr, pv_fr, pv_rc, ALU.mult))
            link(TT(pv_fi, pv_fi, pv_rc, ALU.mult))
            d3 = lambda ap: ap.rearrange("p (d c) -> p d c", d=DG)
            b_re, b_im, c_re, c_im = (d3(sp(n)) for n in ("b_re", "b_im", "c_re", "c_im"))
            fr, fi = (a[:, :, None].broadcast_to([P, DG, C5]) for a in (pv_fr, pv_fi))
            q0, q1, q2 = (d3(s_tmp[:, 512 * i:512 * i + 512]) for i in range(3))
            link(TT(q0, b_re, fi, ALU.mult))
            link(TT(q1, b_im, fi, ALU.mult))
            link(TT(q2, b_im, fr, ALU.mult))
            link(TT(b_re, b_re, fr, ALU.mult))
            link(TT(b_re, b_re, q1, ALU.subtract))
            link(TT(b_im, q0, q2, ALU.add))
            w2 = lambda ap: ap.rearrange("p i d -> p (i d)")
            for to, a_, b_, sub in ((A1, ("is_re", Wr), ("is_im", Wi), False), (A2, ("is_im", Wr), ("is_re", Wi), True),
                                    (A3, ("is_re", Wr), ("is_im", Wi), True), (A4, ("is_im", Wr), ("is_re", Wi), False)):
                t = s_tmp[:, 0:NPOW * DG]
                link(TS(w2(to), w2(a_[1]), cst(a_[0]), None, ALU.mult))
                link(TS(t, w2(b_[1]), cst(b_[0]), None, ALU.mult))
                link(TT(w2(to), w2(to), t, ALU.subtract if sub else ALU.add))
            link(TS(w2(A4), w2(A4), -1.0, None, ALU.mult))
            for d in range(2):
                dg = slice(G5 * d, G5 * d + G5)

                def times(to, i0, n, down_, pr, pi, vr, vi, tmp_):
                    for k, (pwr, val) in enumerate(((pr, vr), (pi, vi))):
                        w = pwr[:, i0:i0 + n, dg]
                        if down_:
                            w = w[:, ::-1, :]
                        w = w.rearrange("p i d -> p d i")[:, :, :, None].broadcast_to([P, G5, n, C5])
                        v = val[:, dg, :][:, :, None, :].broadcast_to([P, G5, n, C5])
                        link(TT(tmp_ if k else to, w, v, ALU.mult))
                    return TT(to, to, tmp_, ALU.add)

                t8 = s_tmp[:, 0:G5 * SC * C5].rearrange("p (d i c) -> p d i c", d=G5, i=SC)
                t9 = s_tmp[:, 0:G5 * NPOW * C5].rearrange("p (d i c) -> p d i c", d=G5, i=NPOW)
                link(times(BtT[:, dg, :, :], 0, SC, d == 0, A1, A2, b_re, b_im, t8))
                times(Ct[:, dg, :, :], 0, NPOW, d == 1, A3, A4, c_re, c_im, t9).then_inc(s["bc"], 1)
                pool.wait_ge(s["bc"], d + 1)
            pool.wait_ge(s["m5"], 16 * (2 * SC - 1))
            link(G.tensor_copy(rho, pv_rho8[:, :, None].broadcast_to([P, DG, NK])))
            G.memset(rho[:, :, 0], 0.0).then_inc(s["rho"], 1)

            pool.wait_ge(s["dest"], 1)
            for i in range(2 * NB):
                G.indirect_dma_start(out=xbuf, out_offset=bass.IndirectOffsetOnAxis(ap=dest_i[:, i:i + 1], axis=0),
                                     in_=h[:, i % NB, :], in_offset=None).then_inc(s_dispatched, 16)
            pool.wait_ge(s["stored"], 1)
            for i in range(2 * NB):
                G.indirect_dma_start(out=hbuf[:, D * i:D * i + D], out_offset=None, in_=ybuf,
                                     in_offset=bass.IndirectOffsetOnAxis(ap=dest_i[:, i:i + 1], axis=0)).then_inc(s_gathered, 16)

        with nc.Fori(0, L) as layer:
            with nc.Block() as block:
                @block.sync
                def _(sp):
                    sync_program(sp, layer)

                @block.tensor
                def _(pe):
                    tensor_program(pe, layer)

                @block.scalar
                def _(act):
                    scalar_program(act, layer)

                @block.vector
                def _(dve):
                    vector_program(dve, layer)

                @block.gpsimd
                def _(pool):
                    pool_program(pool, layer)
            numbers = [q.num for q in [*s.values(), *slot, *xg_in, *y_out]]
            assert max(numbers) - min(numbers) + 1 == len(numbers)
            nc.multi_engine_barrier(list(nc.engines), sems_to_clear=range(min(numbers), max(numbers) + 1))

        with nc.Block() as block:
            @block.sync
            def _(sp):
                sp.dma_start(gB[:, :], final_g).then_inc(s_fin_g, 16)
                for b in range(NB):
                    sp.wait_ge(s_fd, b + 1)
                    sp.dma_start(out[P * b:P * b + P, :], h[:, b, :]).then_inc(s_out, 16)
                sp.wait_ge(s_out, 16 * NB)

            @block.scalar
            def _(act):
                A = nc.scalar.activation
                link = linker(act, s_fa)
                for b in range(NB):
                    link(A(h[:, b, :], x[:, b, :], ACT.Square, accum_out=small[:, 36 + b:37 + b]))
                link(A(small[:, 44:48], small[:, 36:40], ACT.Ln, bias=cst("eps"), scale=1.0 / D))
                A(small[:, 40:44], small[:, 44:48], ACT.Exp, scale=-0.5).then_inc(s_fa, 1)

            @block.vector
            def _(dve):
                dve.wait_ge(s_fin_g, 16)
                dve.wait_ge(s_fa, NB + 2)
                for b in range(NB):
                    nc.vector.scalar_tensor_tensor(out=h[:, b, :], in0=x[:, b, :], scalar=small[:, 40 + b:41 + b],
                                                   in1=gB[:, :], op0=ALU.mult, op1=ALU.mult).then_inc(s_fd, 1)


TURN = (6.28125, float(np.float32(TWO_PI - 6.28125)), float(TWO_PI - 6.28125 - np.float32(TWO_PI - 6.28125)))
PI_DOWN = 3.1415925


def constants():
    c = np.zeros((P, CONST_W), np.float32)

    def put(name, value):
        a, n = CONST[name]
        c[:, a:a + n] = value

    p = np.arange(P)[:, None]
    q = np.arange(P)[None, :]
    put("ident", p == q)
    same = (p // CH) == (q // CH)
    put("mask_f", same & (p <= q))
    put("mask_b", same & (p >= q))
    put("head_ones", (p // HD) == (q // HD))
    put("rope_swap", np.where((q % 2 == 0) & (p == q + 1), -1.0, 0.0) + np.where((q % 2 == 1) & (p == q - 1), 1.0, 0.0))
    put("half_swap", p == (q + HD) % P)
    put("before", p < q)
    put("ones", 1.0)
    pairs, grid = HD // 4, 64
    freqs = np.power(np.float32(10000.0), -np.arange(pairs, dtype=np.float32) / np.float32(pairs)).astype(np.float32)
    t = np.arange(T)
    ang = np.concatenate([(t // grid).astype(np.float32)[:, None] * freqs, (t % grid).astype(np.float32)[:, None] * freqs], 1)
    by_row = ang.astype(np.float32)[:, (np.arange(P) % HD) // 2].T
    put("cos", np.cos(by_row))
    put("sin", np.sin(by_row))
    put("chunk_start", np.where(p < HD, t[None, :] % CH == 0, t[None, :] % CH == CH - 1))
    put("chunk_of", (p // CH) == np.arange(CB)[None, :])
    put("group_id", np.arange(EG)[None, :] - BIG)
    put("expert_id", np.arange(NE)[None, :] - BIG)
    put("expert_row", np.arange(NE)[None, :] * CAP)
    put("chunk_end", np.arange(1, 8)[None, :] * CAP)
    put("over_id", np.arange(NOVER)[None, :])
    put("is_re", p < HD)
    put("is_im", p >= HD)
    put("sign", np.where(p < HD, 1.0, -1.0))
    put("eps", EPS)
    return c


def kernel(**inputs):
    import concourse.bacc as bacc
    from concourse.bass_utils import run_bass_kernel_spmd

    a = {k: np.asarray(v) for k, v in inputs.items()}
    f = np.ascontiguousarray

    w = a["w_in"].reshape(L, KT, P, 2304)
    head = lambda at, i: np.arange(at + HD * i, at + HD * i + HD)
    z = np.concatenate([np.concatenate([head(768, i), head(1024, i)]) for i in range(HG)])
    order = [z, np.concatenate([np.arange(0, 256), np.arange(1792, 2048)]), np.arange(1280, 1792),
             np.concatenate([np.arange(512, 768), np.arange(256, 512)]), np.arange(2048, 2304)]
    w_in = f(np.concatenate([w[..., o].transpose(0, 2, 1, 3).reshape(L, P, -1) for o in order], axis=2))
    w_out = f(a["w_out"].reshape(L, KT, P, 2, 512).transpose(0, 3, 2, 1, 4).reshape(L, 2, P, 4096))

    pack = np.zeros((L, P, PACK_W), np.float32)

    def put(name, value):
        at, n = PACK[name]
        pack[:, :, at:at + n] = value

    bounds = a["hgrn_lower_bounds"].reshape(L, 2, HG, HD).transpose(1, 3, 0, 2).reshape(P, L * HG)
    put("lb", bounds[None])
    put("lb_sum", np.array([[0.0] + [1.0 if 1 <= j <= l else 0.0 for j in range(1, L)] for l in range(L)])[:, None, :])
    twice = lambda v: np.concatenate([v, v], axis=1)[:, :, None]
    put("hgrn_g", twice(a["hgrn_norm_g"]))
    put("q_g", twice(a["attn_q_norm_g"]))
    put("k_g", twice(a["attn_k_norm_g"]))
    put("s5_d", a["s5_d"].reshape(L, 2, P).transpose(0, 2, 1))
    put("b_glu", a["s5_b_glu"].reshape(L, 2, P).transpose(0, 2, 1))
    put("router_b", np.concatenate([a["router_group_b"], a["router_expert_b"]], axis=1)[:, None, :])
    rw = np.concatenate([a["router_group_w"], a["router_expert_w"]], axis=2).reshape(L, KT, P, RW)
    put("router_w", rw.transpose(0, 2, 1, 3).reshape(L, P, KT * RW))
    put("w_glu", a["s5_w_glu"].reshape(L, 2, P, 256).transpose(0, 2, 1, 3).reshape(L, P, 512))

    s5p = np.zeros((L, P, S5P_W), np.float32)

    def put5(name, value):
        at, n = S5P[name]
        s5p[:, :, at:at + n] = np.concatenate([value, value], axis=1)

    put5("a_re", a["s5_a_re"].transpose(0, 3, 1, 2).reshape(L, HD, DG))
    put5("a_im", a["s5_a_im"].transpose(0, 3, 1, 2).reshape(L, HD, DG))
    put5("log_dt", np.broadcast_to(a["s5_log_dt"].reshape(L, 1, DG), (L, HD, DG)))
    for part in ("re", "im"):
        put5("b_" + part, a["s5_b_" + part].transpose(0, 3, 1, 2, 4).reshape(L, HD, DG * C5))
        put5("c_" + part, a["s5_c_" + part].transpose(0, 4, 1, 2, 3).reshape(L, HD, DG * C5))

    rows = np.stack([a["norm1_g"], a["norm2_g"]], axis=1)
    gains = f(np.broadcast_to(rows[:, :, None, :], (L, 2, P, D)))
    final_g = f(np.broadcast_to(a["final_norm_g"][None, :], (P, D)))

    arrays = {
        "x_in": f(a["x"].reshape(T, D)), "w_in": w_in, "w_out": w_out, "pack": pack, "s5p": s5p, "gains": gains,
        "final_g": final_g, "wg": f(a["expert_w_gate"].reshape(L * NE, D, FF)),
        "wu": f(a["expert_w_up"].reshape(L * NE, D, FF)), "wd": f(a["expert_w_down"].reshape(L * NE, FF, D)),
        "consts": constants(),
    }
    nc = bacc.Bacc("TRN2", target_bir_lowering=False, num_devices=1)
    args = [nc.dram_tensor(name, v.shape, F32, kind="ExternalInput").ap() for name, v in arrays.items()]
    out = nc.dram_tensor("out", (T, D), F32, kind="ExternalOutput").ap()
    trunk(nc, *args, out)
    r = run_bass_kernel_spmd(nc, [arrays], core_ids=[0])
    return np.asarray(r.results[0]["out"]).reshape(1, T, D)
```

```python
from contextlib import ExitStack

import numpy as np

import concourse.bass as bass
from concourse import mybir

F32 = mybir.dt.float32
I32 = mybir.dt.int32
ALU = mybir.AluOpType
ACT = mybir.ActivationFunctionType
AX = mybir.AxisListType

P = 128
D = 1024
T = 512
L = 2
NB = T // P
KT = D // P
HD = 64
HG = 4
CH = 16
NCH = T // CH
CB = P // CH
QH = 8
G5 = 16
C5 = 16
DG = 2 * G5
SC = 8
NK = T // SC
NPOW = SC + 1
NE = 32
EG = 4
EPG = NE // EG
FF = 512
FT = FF // P
CAP = 64
NOVER = (2 * T) // CAP - 1
NROWS = (NE + NOVER) * CAP
RW = EG + NE
EPS = 1e-6
SCALE = HD ** -0.5
BIG = 1000.0
NEG = 1.0e30
TWO_PI = 2.0 * np.pi
ROUND = 12582912.0

def _cols(spec):
    at, out = 0, {}
    for name, n in spec:
        out[name] = (at, n)
        at += n
    return out, at


CONST, CONST_W = _cols([
    ("ident", P), ("mask_f", P), ("mask_b", P), ("head_ones", P), ("rope_swap", P), ("half_swap", P),
    ("before", P), ("ones", P), ("cos", T), ("sin", T), ("chunk_start", T), ("chunk_of", CB),
    ("group_id", EG), ("expert_id", NE), ("expert_row", NE), ("chunk_end", 7), ("over_id", NOVER),
    ("is_re", 1), ("is_im", 1), ("sign", 1), ("eps", 1)])
PACK, PACK_W = _cols([
    ("lb", L * HG), ("lb_sum", L), ("hgrn_g", 1), ("q_g", 1), ("k_g", 1), ("s5_d", 2), ("b_glu", 2),
    ("router_b", RW), ("router_w", KT * RW), ("w_glu", 2 * 256), ("a_re", DG), ("a_im", DG), ("log_dt", DG)])
S5P, S5P_W = _cols([
    ("b_re", DG * C5), ("b_im", DG * C5),
    ("c_re", DG * C5), ("c_im", DG * C5)])


def trunk(nc, x_in, w_in, w_out, pack, s5p, gains, final_g, wg, wu, wd, consts, out):
    ctx = ExitStack()
    with ctx:
        def sb(name, shape, dt=F32):
            return ctx.enter_context(nc.sbuf_tensor(name, shape, dt))

        def sem(name):
            return ctx.enter_context(nc.semaphore(name))

        u_dram = nc.dram_tensor("u_scratch", (G5, C5, SC, NK), F32).ap()
        y_dram = nc.dram_tensor("y_scratch", (G5, C5, SC, NK), F32).ap()
        xbuf = nc.dram_tensor("dispatched_tokens", (NROWS, D), F32).ap()
        ybuf = nc.dram_tensor("expert_rows", (NROWS, D), F32).ap()

        ring = sb("ring", [P, 6, 4096])
        hbuf = sb("hbuf", [P, 8192])
        x = sb("x", [P, NB, D])
        raw = sb("raw", [P, 9216])
        qd = sb("qd", [P, 2048])
        C = sb("consts_sb", [P, CONST_W])
        gB = sb("gain_rows", [P, D])
        pk = sb("pack_sb", [P, PACK_W])
        small = sb("small", [P, 64])
        dec4 = sb("dec4", [P, HG * NCH])
        lbs = sb("lower_bounds", [P, 24])
        over_i = sb("over_i", [P, 16], I32)
        dest_i = sb("dest_i", [P, 2 * NB], I32)
        gate_w = sb("gate_w", [P, 2 * NB])

        def cst(name):
            a, n = CONST[name]
            return C[:, a:a + n]

        def pcol(name):
            a, n = PACK[name]
            return pk[:, a:a + n]

        ident = cst("ident")
        h = hbuf[:, 0:4096].rearrange("p (b d) -> p b d", b=NB)
        hT = hbuf[:, 4096:8192].rearrange("p (k t) -> p k t", k=KT)

        def tile(buf, at, n=T):
            return buf[:, at:at + n]

        Z = [tile(raw, 512 * i) for i in range(HG)]
        hq = [tile(raw, 2048 + 512 * i) for i in range(2)]
        ak = tile(raw, 3072)
        av = raw[:, 3584:4096].rearrange("p (b c) -> p b c", b=NB)
        aq = [tile(raw, 4096 + 512 * i) for i in range(4)]
        hg = [tile(raw, 6144 + 512 * i) for i in range(2)]
        hv = raw[:, 7168:8192].rearrange("p (b c) -> p b c", b=NB)
        uT = [tile(raw, 8192 + 512 * i) for i in range(2)]
        q_dec = [tile(qd, 512 * i) for i in range(HG)]
        k_dec = [ring[:, 4, 2048 + 512 * i:2560 + 512 * i] for i in range(HG)]
        k_end = Z
        ht_e, ht_s, ht_k, ht_f, ht_d0, ht_d1, ht_F, ht_R = (ring[:, 5, 512 * i:512 * i + 512] for i in range(8))
        dec_n = small[:, 0:NCH]
        dec_s = [dec4[:, NCH * i:NCH * i + NCH] for i in range(HG)]
        two = lambda a, c: [ap.rearrange("p (v c) -> p v c", c=NCH) for ap in (a, c)]
        kv_sb = two(hbuf[:, 0:2048], ring[:, 3, 0:2048])
        dec_sb = two(hbuf[:, 2048:4096], ring[:, 3, 2048:4096])
        st_sb = two(hbuf[:, 4096:6144], ring[:, 1, 0:2048])
        v_blk = [hbuf[:, 6144:6656], hbuf[:, 6656:7168], ring[:, 1, 2048:2560], ring[:, 1, 2560:3072]]
        k_endT = [hbuf[:, 7168 + 512 * i:7680 + 512 * i] for i in range(2)]
        sc_a = [ring[:, 2, 512 * i:512 * i + 512] for i in range(2)]
        sc_t = ring[:, 2, 1024:1536]
        o_sb = [ring[:, 2, 1536 + 512 * i:2048 + 512 * i] for i in range(2)]
        o_rs = [ring[:, 2, 2560 + 512 * i:3072 + 512 * i] for i in range(2)]
        rope_sq = [ring[:, 1, 512 * i:512 * i + 512] for i in range(5)]
        rope_t = ring[:, 1, 2560:3072]
        k_dup = [tile(qd, 1024 + 512 * i) for i in range(2)]
        p_sb = [ring[:, 3, 512 * i:512 * i + 512] for i in range(3)]
        pT_sb = [ring[:, 3, 1536 + 512 * i:2048 + 512 * i] for i in range(3)]
        p_sum, p_max, p_bias, p_inv = ([small[:, 4 * k + i:4 * k + i + 1] for i in range(3)] for k in range(4))
        s5 = hbuf[:, 4608:4608 + S5P_W]
        Bt = ring[:, 1, :].rearrange("p (d m) -> p d m", d=DG)
        cosT = ring[:, 0, 0:2048].rearrange("p (d k) -> p d k", d=DG)
        sinT = ring[:, 0, 2048:4096].rearrange("p (d k) -> p d k", d=DG)
        BtT = ring[:, 2, :].rearrange("p (d s c) -> p d s c", d=DG, s=SC)
        T1 = ring[:, 2, 0:2048].rearrange("p (d k) -> p d k", d=DG)
        T2 = ring[:, 2, 2048:4096].rearrange("p (d k) -> p d k", d=DG)
        rho = qd[:, 0:2048].rearrange("p (d k) -> p d k", d=DG)
        M5 = ring[:, 3, 2048:4096].rearrange("p (g m) -> p g m", g=G5)
        Kf = ring[0:C5, 3, 0:2048].rearrange("p (g i c) -> p g i c", g=G5, i=SC)
        Kb = raw[0:C5, 6144:8192].rearrange("p (g i c) -> p g i c", g=G5, i=SC)
        Ct = hbuf[:, 0:4608].rearrange("p (d i c) -> p d i c", d=DG, i=NPOW)
        U5 = raw[:, 0:1024].rearrange("p (g k) -> p g k", g=G5)
        Y5 = raw[:, 1024:2048].rearrange("p (g k) -> p g k", g=G5)
        s_tmp = ring[:, 1, :]
        gt = [hbuf[:, 512 * i:512 * i + 512] for i in range(4)]
        yT = [tile(raw, 512 * i) for i in range(2)]
        pw = raw[:, 6144:6144 + 2048]
        Wr = gB[:, 320:320 + NPOW * DG].rearrange("p (i d) -> p i d", i=NPOW)
        Wi = gB[:, 608:608 + NPOW * DG].rearrange("p (i d) -> p i d", i=NPOW)
        W_t = gB[:, 896:1024].rearrange("p (i d) -> p i d", i=4)
        A1 = pw[:, 576:864].rearrange("p (i d) -> p i d", i=NPOW)
        A2 = pw[:, 864:1152].rearrange("p (i d) -> p i d", i=NPOW)
        A3 = pw[:, 1152:1440].rearrange("p (i d) -> p i d", i=NPOW)
        A4 = pw[:, 1440:1728].rearrange("p (i d) -> p i d", i=NPOW)
        ss = [gB[:, 32 * i:32 * i + 32] for i in range(10)]
        pv_den = pcol("log_dt")
        rt = [qd[:, 160 * i:160 * i + 160] for i in range(12)]
        xg = [tile(raw, 1024 * i, 1024) for i in range(2)]
        xT = [raw[:, 2048 + 512 * i:2560 + 512 * i].rearrange("p (k c) -> p k c", k=KT) for i in range(2)]
        e_e = tile(raw, 3072)
        e_s = tile(raw, 3584)
        hid = [tile(raw, 4096 + 512 * i) for i in range(2)]
        hidT = [raw[:, 5120 + 256 * i:5376 + 256 * i].rearrange("p (k c) -> p k c", k=FT) for i in range(2)]
        y_sb = [tile(raw, 5632 + 512 * i) for i in range(2)]

        pb = [ctx.enter_context(nc.psum_tensor(f"bank{i}", [P, 512], F32)) for i in range(8)]

        s_boot = sem("boot_loads")
        s_zero = sem("zero_rows")
        s_zeroed = sem("unused_rows_zeroed")
        s_fin_g = sem("final_gain_loaded")
        s_fa = sem("final_act")
        s_fd = sem("final_dve")
        s_out = sem("out_stored")

        with nc.Block() as block:
            @block.sync
            def _(sp):
                sp.dma_start(C[:, :], consts).then_inc(s_boot, 16)
                sp.dma_start(x[:, :, :], x_in.rearrange("(b p) d -> p b d", p=P)).then_inc(s_boot, 16)
                sp.wait_ge(s_boot, 32)
                sp.wait_ge(s_zero, 1)

            @block.gpsimd
            def _(pool):
                nc.gpsimd.memset(raw[:, 8192:9216], 0.0).then_inc(s_zero, 1)
        nc.all_engine_barrier()

        s_dispatched = sem("tokens_dispatched")
        s_gathered = sem("expert_rows_gathered")
        PER_LAYER = 16 * 2 * NB
        ZEROINGS = -(-NROWS // P) + -(-(NROWS - NE * CAP) // P)

        names = dict(
            pack="parameters loaded", gain1="norm 1 gain row loaded", gain2="norm 2 gain row loaded",
            s5p="S5 parameters loaded", rstd="ACT: norm 1 scales", h="DVE: h rows of a block",
            pe="PE: h^T and projection groups", ev_d="DVE: groups evacuated", ev_a="ACT: groups evacuated",
            dve="DVE: own chain", act="ACT: own chain", pool="Pool: own chain",
            lb_e="ACT: lower bound exp", lb="DVE: lower bounds ready",
            sig_e="ACT: exp(-z) or tanh(z/2) of a gate job", sig_r="DVE: that read", q_silu="DVE: silu(q) of a pair",
            q_copy="ACT: silu(q) copied to both halves", f_ready="DVE: forget gates of a head",
            f_split="Pool: scan operands of a head", head="DVE: decayed q, k of a head",
            r_sq="ACT: rope squares", r_y="DVE: rope gained tile", r_pe="PE: rope sums and swap",
            r_rs="ACT: rope rstd", r_done="DVE: rope tile done",
            ke_t="PE: k_end transposed", ke_e="ACT: k_end^T evacuated", hs_pe="PE: HGRN scores",
            hs_m="DVE: HGRN scores masked", vb="Pool: chunk-spread v", kv="PE: chunk k v of a block",
            kv_e="ACT: chunk k v evacuated", dec="Pool: decay rows", state="DVE: chunk states",
            ho="PE: HGRN outputs of a head", ho_b="ACT: backward output copied", ho_s="DVE: HGRN output of a pair",
            ho_q="ACT: HGRN squares", ho_m="PE: HGRN square sums", ho_r="ACT: HGRN rstd", o_a="DVE: o_a of a pair",
            k_dup="ACT: k^T halves duplicated", qk="PE: attention scores", mx="DVE: row maxima",
            ex="ACT: probabilities", pn="DVE: probabilities scaled", pt="PE: probabilities transposed",
            pt_e="ACT: transposed probabilities evacuated", pv="PE: attention output of a unit",
            o_b="ACT: o_b of a pair", u_out="u stored", u_in="u by chunk loaded",
            dt="ACT: S5 step sizes", ang="Pool: S5 angles", lam="ACT: S5 moduli, sines", den="Pool: S5 denominators",
            inv="DVE: S5 inverse denominators", bc="Pool: S5 Bt^T, then forward Ct", ct="DVE: S5 backward Ct", tab="Pool: S5 rotations",
            kp="PE: S5 kernels of a bank", ke="S5 kernels evacuated", kdiag="DVE: S5 kernel diagonal",
            m5="S5 chunk matrix loaded", rho="Pool: S5 decay rows", bt="PE: Bt of a bank", bt_e="ACT: odd banks of Bt evacuated",
            bt_v="DVE: even banks of Bt evacuated",
            xin="PE: S5 chunk inputs of a quarter", rot="DVE: S5 inputs rotated", z="DVE: S5 quarters scanned",
            zs="PE: S5 states swapped", xs="DVE: S5 states", y5="PE: S5 outputs", y5_e="S5 outputs evacuated",
            y_out="y stored", y_in="y loaded", ge="DVE: gelu argument", gx="ACT: gelu tanh", z5="DVE: gelu",
            glu="PE: GLU products", glx="ACT: GLU tanh", o_c="DVE: o_c of a tile",
            wo="PE: output projection groups", res="DVE: residual added", rstd2="ACT: norm 2 scales",
            h2="DVE: h rows", h2t="PE: h^T tiles", h2_d="DVE: h^T evacuated", h2_a="ACT: h^T evacuated",
            rl="PE: router logits", gs="DVE: group logits less maximum", gx2="ACT: group exp",
            sel="DVE: experts selected", sx="ACT: exp of the second's difference", cnt="PE: positions and counts",
            dest="DVE: destinations and weights", xt="PE: expert tokens transposed",
            xt_e="ACT: expert tokens evacuated", gu="PE: gate and up", ee="ACT: tanh(gate/2)", er="DVE: tanh(gate/2) read",
            ec="DVE: expert chain", hid="DVE: hidden rows", ht="PE: hidden transposed", ht_e="DVE: hidden^T evacuated",
            dn="PE: down", ye="ACT: expert rows evacuated", stored="ACT: every expert row stored",
            moe="DVE: MoE residual")
        s = {k: sem(f"s_{k}") for k in names}
        slot = [sem(f"slot{i}") for i in range(6)]
        xg_in = [sem(f"xg{i}") for i in range(2)]
        y_out = [sem(f"y_rows{i}_stored") for i in range(2)]

        def flat(ap):
            return ap.rearrange("p a b -> p (a b)")

        def linker(engine, semaphore):
            at = [0]

            def link(ins):
                at[0] += 1
                ins.then_inc(semaphore, 1)
                engine.wait_ge(semaphore, at[0])
            return link

        NG = KT + 18

        def wait_evacuated(engine, n):
            if n % 2 == 0:
                engine.wait_ge(s["ev_d"], n // 2 + 1)
            else:
                engine.wait_ge(s["ev_a"], n // 2 + 1)

        def weights(i):
            width = 512 if i < 4 else 256
            return ring[:, i, 0:8 * width].rearrange("p (k c) -> p k c", k=KT)

        w_o = [ring[:, 4 + i, :].rearrange("p (k c) -> p k c", k=KT) for i in range(2)]
        W_gate = [ring[:, 3 * i, :].rearrange("p (k c) -> p k c", k=KT) for i in range(2)]
        W_up = [ring[:, 3 * i + 1, :].rearrange("p (k c) -> p k c", k=KT) for i in range(2)]
        W_down = [ring[:, 3 * i + 2, :].rearrange("p (k c) -> p k c", k=FT) for i in range(2)]
        LOADS = [1, 1, 1, 1, 2, 1]
        NU = QH * NB
        RTI = [12, 13, 20, 21, 8, 9, 10, 11]
        target = {8: Z[0], 9: Z[1], 10: Z[2], 11: Z[3], 12: hq[0], 13: hq[1], 14: ak,
                  16: aq[0], 17: aq[1], 18: aq[2], 19: aq[3], 20: hg[0], 21: hg[1]}
        rope_x = [ak] + aq
        mixed = hq + aq + uT
        wg_f = wg.rearrange("e (p k) f -> e p (k f)", p=P)
        wu_f = wu.rearrange("e (p k) f -> e p (k f)", p=P)
        wd_f = wd.rearrange("e (p k) f -> e p (k f)", p=P)

        def evac_views(n):
            bank = pb[n % 4]
            if n < KT:
                return hT[:, n, :], bank[:, :]
            if n == 15:
                return flat(av), bank[:, :]
            if n in (22, 23):
                q = 2 * (n - 22)
                return flat(hv[:, q:q + 2, :]), bank[:, :]
            if n >= 24:
                return (uT[n - 24].rearrange("p (t k) -> p t k", t=SC),
                        bank[:, :].rearrange("p (k t) -> p t k", t=SC))
            return target[n], bank[:, :]

        X_BANK = [(pb[4], pb[5]), (pb[0], pb[1]), (pb[2], pb[3]), (pb[4], pb[5])]
        S_BANK, T_BANK = (0, 1, 6), (2, 3, 7)

        def sync_program(sp, layer):
            for i in range(5):
                width = 4096 if i < 4 else 2048
                sp.dma_start(ring[:, i, 0:width], w_in[layer, :, 4096 * i:4096 * i + width]).then_inc(slot[i], 16)
            with sp.If(layer < 1):
                for buf, first in ((xbuf, 0), (ybuf, NE * CAP)):
                    for r in range(first, NROWS, P):
                        n = min(P, NROWS - r)
                        sp.dma_start(buf[r:r + n], raw[0:n, 8192:9216]).then_inc(s_zeroed, 16)
            wait_evacuated(sp, 24)
            wait_evacuated(sp, 25)
            for i in range(2):
                sp.dma_start(u_dram[8 * i:8 * i + 8].rearrange("g c t k -> (g c) (t k)"), uT[i]).then_inc(s["u_out"], 16)
            sp.wait_ge(s["u_out"], 32)
            sp.wait_ge(s["ke_t"], HG)
            for t in range(SC):
                sp.dma_start(U5[C5 * t:C5 * t + C5], u_dram[:, :, t, :].rearrange("g c k -> c g k")).then_inc(s["u_in"], 16)
            sp.wait_ge(s["hs_pe"], HG)
            sp.wait_ge(s["head"], HG)
            sp.wait_ge(s["q_silu"], 4)
            for i in range(2):
                sp.dma_start(ring[:, 4 + i, :], w_out[layer, i]).then_inc(slot[4 + i], 16)
            sp.wait_ge(s["ho"], HG)
            sp.dma_start(s5, s5p[layer]).then_inc(s["s5p"], 16)
            sp.wait_ge(s["kdiag"], 1)
            for t in range(SC):
                rows = slice(C5 * t, C5 * t + C5)
                sp.dma_start(M5[rows, :, C5 * t:P].rearrange("p g (i c) -> p g i c", c=C5),
                             Kf[:, :, 0:SC - t, :]).then_inc(s["m5"], 16)
                if t:
                    sp.dma_start(M5[rows, :, 0:C5 * t].rearrange("p g (i c) -> p g i c", c=C5),
                                 Kb[:, :, SC - 1 - t:SC - 1, :]).then_inc(s["m5"], 16)
            sp.wait_ge(s["rho"], 1)
            sp.dma_start(gB[:, :], gains[layer, 1]).then_inc(s["gain2"], 16)
            sp.wait_ge(s["y5_e"], 2)
            for t in range(SC):
                sp.dma_start(y_dram[:, :, t, :].rearrange("g c k -> c g k"), Y5[C5 * t:C5 * t + C5]).then_inc(s["y_out"], 16)
            sp.wait_ge(s["y_out"], 16 * SC)
            for i in range(2):
                sp.dma_start(yT[i], y_dram[8 * i:8 * i + 8].rearrange("g c t k -> (g c) (t k)")).then_inc(s["y_in"], 16)
            first_e = sp.snap(layer * NE)
            second_e = sp.snap(layer * NE + 1)
            sp.dma_start(ring[:, 0, :], wg_f[first_e]).then_inc(slot[0], 16)
            sp.dma_start(ring[:, 1, :], wu_f[first_e]).then_inc(slot[1], 16)
            sp.dma_start(ring[:, 2, :], wd_f[first_e]).then_inc(slot[2], 16)
            sp.dma_start(ring[:, 3, :], wg_f[second_e]).then_inc(slot[3], 16)
            sp.wait_ge(s["wo"], 4 * NB)
            sp.dma_start(ring[:, 4, :], wu_f[second_e]).then_inc(slot[4], 16)
            sp.dma_start(ring[:, 5, :], wd_f[second_e]).then_inc(slot[5], 16)
            with sp.Fori(1, NE // 2) as j:
                for odd in range(2):
                    e = sp.snap(layer * NE + j * 2 + odd)
                    used = sp.snap(j * 2 + odd - 1)
                    sp.wait_ge(s["gu"], used)
                    sp.dma_start(ring[:, 3 * odd, :], wg_f[e]).then_inc(slot[3 * odd], 16)
                    sp.dma_start(ring[:, 3 * odd + 1, :], wu_f[e]).then_inc(slot[3 * odd + 1], 16)
                    sp.wait_ge(s["dn"], used)
                    sp.dma_start(ring[:, 3 * odd + 2, :], wd_f[e]).then_inc(slot[3 * odd + 2], 16)
            sp.wait_ge(s["dn"], NE)
            n_over = sp.value_load(over_i[0:1, NOVER:NOVER + 1], min_val=0, max_val=NOVER)
            with sp.If(n_over > 0):
                with sp.Fori(0, n_over) as i:
                    e_over = sp.value_load(over_i[0:1, bass.ds(i, 1)], min_val=0, max_val=NE - 1)
                    e = sp.snap(layer * NE + e_over)
                    used = sp.snap(i + NE)
                    sp.wait_ge(s["dn"], used)
                    sp.dma_start(ring[:, 0, :], wg_f[e]).then_inc(slot[0], 16)
                    sp.dma_start(ring[:, 1, :], wu_f[e]).then_inc(slot[1], 16)
                    sp.dma_start(ring[:, 2, :], wd_f[e]).then_inc(slot[2], 16)

        def tensor_program(pe, layer):
            mm, tr = nc.tensor.matmul, nc.tensor.transpose

            def rope(j):
                pe.wait_ge(s["r_sq"], j + 1)
                if j:
                    pe.wait_ge(s["r_rs"], j)
                    pe.wait_ge(s["r_done"], j)
                mm(pb[6][:, :], cst("head_ones"), rope_sq[j], start=True, stop=True)
                pe.wait_ge(s["r_y"], j + 1)
                mm(pb[7][:, :], cst("rope_swap"), rope_x[j], start=True, stop=True).then_inc(s["r_pe"], 1)

            pe.wait_ge(s["h"], NB)
            for n in range(KT):
                if n >= 4:
                    wait_evacuated(pe, n - 4)
                for b in range(NB):
                    last = tr(pb[n % 4][:, P * b:P * b + P], h[:, b, P * n:P * n + P], ident)
                last.then_inc(s["pe"], 1)
            wait_evacuated(pe, KT - 2)
            wait_evacuated(pe, KT - 1)
            for n in range(KT, NG):
                i, c = (n - KT) // 4, P * ((n - KT) % 4)
                w = weights(i)
                if c == 0:
                    pe.wait_ge(slot[i], 16)
                wait_evacuated(pe, n - 4)
                bank = pb[n % 4]
                if n == 15:
                    for b in range(NB):
                        for k in range(KT):
                            last = mm(bank[:, P * b:P * b + P], hT[:, k, P * b:P * b + P], w[:, k, c:c + P],
                                      start=(k == 0), stop=(k == KT - 1))
                elif n in (22, 23):
                    for half in range(2):
                        b = 2 * (n - 22) + half
                        for k in range(KT):
                            last = mm(bank[:, 256 * half:256 * half + 256], hT[:, k, P * b:P * b + P],
                                      w[:, k, 256:512], start=(k == 0), stop=(k == KT - 1))
                else:
                    for k in range(KT):
                        last = mm(bank[:, :], w[:, k, c:c + P], hT[:, k, :], start=(k == 0), stop=(k == KT - 1))
                last.then_inc(s["pe"], 1)
                for j, after in enumerate((18, 20, 22, 24, 25)):
                    if n == after:
                        rope(j)

            def hgrn_in(hh):
                pe.wait_ge(s["head"], hh + 1)
                if hh == 0:
                    wait_evacuated(pe, NG - 2)
                    wait_evacuated(pe, NG - 1)
                    pe.wait_ge(s["r_rs"], 5)
                else:
                    pe.wait_ge(s["kv_e"], NB * hh)
                    pe.wait_ge(s["hs_m"], hh)
                for b in range(NB):
                    last = tr(pb[0][:, P * b:P * b + P], k_end[hh][:, P * b:P * b + P], ident)
                last.then_inc(s["ke_t"], 1)
                for b in range(NB):
                    t = slice(P * b, P * b + P)
                    mm(pb[5][:, t], k_dec[hh][0:HD, t], q_dec[hh][0:HD, t], start=True, stop=True)
                    last = mm(pb[6][:, t], k_dec[hh][HD:P, t], q_dec[hh][HD:P, t], start=True, stop=True)
                last.then_inc(s["hs_pe"], 1)
                pe.wait_ge(s["ke_e"], hh + 1)
                kT = k_endT[hh % 2]
                for b in range(NB):
                    pe.wait_ge(s["vb"], NB * hh + b + 1)
                    v = v_blk[b]
                    mm(pb[b][0:HD, :], kT[:, P * b:P * b + HD], v, start=True, stop=True)
                    rev = v.rearrange("p (c v) -> p c v", c=CB)[:, ::-1, :]
                    mm(pb[NB - 1 - b][HD:P, :].rearrange("p (c v) -> p c v", c=CB), kT[:, P * b + HD:P * b + P], rev,
                       start=True, stop=True).then_inc(s["kv"], 1)

            def hgrn_out(hh):
                pe.wait_ge(s["hs_m"], hh + 1)
                pe.wait_ge(s["state"], hh + 1)
                if hh == 0:
                    pe.wait_ge(s["r_done"], 5)
                if hh == 2:
                    pe.wait_ge(s["ho_s"], 1)
                rows = slice(HD * (hh % 2), HD * (hh % 2) + HD)
                q, st = q_dec[hh], st_sb[hh % 2]
                for b in range(NB):
                    mm(pb[7][rows, P * b:P * b + P], hv[:, b, HD * hh:HD * hh + HD], sc_a[hh % 2][:, P * b:P * b + P],
                       start=True, stop=False)
                    for c in range(CB * b, CB * b + CB):
                        t = slice(CH * c, CH * c + CH)
                        if c < NCH - 1:
                            last = mm(pb[4][rows, t], st[HD:P, :, NCH - 2 - c], q[HD:P, t], start=True, stop=True)
                        if c > 0:
                            last = mm(pb[7][rows, t], st[0:HD, :, c - 1], q[0:HD, t],
                                      start=False, stop=(c % CB == CB - 1))
                last.then_inc(s["ho"], 1)

            hgrn_in(0)
            hgrn_in(1)
            hgrn_out(0)
            hgrn_in(2)
            hgrn_out(1)
            hgrn_in(3)
            hgrn_out(2)
            hgrn_out(3)
            pe.wait_ge(s["hs_m"], HG)
            for p in range(2):
                pe.wait_ge(s["ho_q"], p + 1)
                mm(pb[5 + p][:, :], cst("head_ones"), o_rs[p], start=True, stop=True).then_inc(s["ho_m"], 1)

            def scores(u):
                a, b = divmod(u, NB)
                if u == 0:
                    pe.wait_ge(s["kv_e"], NB * HG)
                    pe.wait_ge(s["k_dup"], 4)
                if u == 2:
                    pe.wait_ge(s["ho_r"], 2)
                if u >= 3:
                    pe.wait_ge(s["ex"], u - 2)
                r = slice(HD * (a % 2), HD * (a % 2) + HD)
                mm(pb[S_BANK[u % 3]][:, :], aq[a // 2][r, P * b:P * b + P], k_dup[a // 4][r, :],
                   start=True, stop=True).then_inc(s["qk"], 1)

            def values(u):
                a, b = divmod(u, NB)
                pe.wait_ge(s["pt_e"], u + 1)
                pair = a // 2
                if u == 0:
                    pe.wait_ge(s["ho_s"], 2)
                    pe.wait_ge(s["ho_r"], 2)
                if u % (2 * NB) == 0 and pair >= 2:
                    pe.wait_ge(s["o_b"], pair - 1)
                r = slice(HD * (a % 2), HD * (a % 2) + HD)
                kv = a // 4
                for j in range(NB):
                    last = mm(pb[4 + pair % 2][r, P * b:P * b + P], av[:, j, HD * kv:HD * kv + HD],
                              pT_sb[u % 3][:, P * j:P * j + P], start=(j == 0), stop=(j == NB - 1))
                last.then_inc(s["pv"], 1)

            scores(0)
            scores(1)
            for u in range(NU):
                if u + 2 < NU:
                    scores(u + 2)
                pe.wait_ge(s["pn"], u + 1)
                if u == 2:
                    pe.wait_ge(s["ho_s"], 2)
                if u >= 3:
                    pe.wait_ge(s["pt_e"], u - 2)
                for j in range(NB):
                    last = tr(pb[T_BANK[u % 3]][:, P * j:P * j + P], p_sb[u % 3][:, P * j:P * j + P], ident)
                last.then_inc(s["pt"], 1)
                if u >= 1:
                    values(u - 1)
            values(NU - 1)

            def projected(n, tiles, bank):
                b, half = divmod(n, 2)
                for k in tiles:
                    last = mm(bank[:, :], mixed[k][:, P * b:P * b + P], w_o[half][:, k, :],
                              start=(k == tiles[0]), stop=(k == tiles[-1]))
                last.then_inc(s["wo"], 1)

            def early(n):
                if n >= 2:
                    pe.wait_ge(s["res"], n - 1)
                projected(n, range(6), pb[6 + n % 2])

            pe.wait_ge(s["o_a"], 2)
            pe.wait_ge(s["o_b"], 4)
            pe.wait_ge(s["ex"], NU)
            pe.wait_ge(s["pt_e"], NU)
            pe.wait_ge(slot[4], 32)
            pe.wait_ge(slot[5], 16)
            for n in range(4):
                early(n)

            def bt_left(q):
                if q % 2:
                    pe.wait_ge(s["bt_e"], q // 2 + 1)
                else:
                    pe.wait_ge(s["bt_v"], q // 2 + 1)

            pe.wait_ge(s["bc"], 2)
            for q in range(8):
                if q >= 6:
                    bt_left(q - 6)
                for dg in range(4 * q, 4 * q + 4):
                    last = tr(pb[q % 6][:, P * (dg % 4):P * (dg % 4) + P],
                              BtT[:, dg, :, :].rearrange("p s c -> p (s c)"), ident)
                last.then_inc(s["bt"], 1)
            pe.wait_ge(s["ct"], 1)
            for q in range(8):
                if q < 6:
                    bt_left(q + 2)
                else:
                    pe.wait_ge(s["ke"], q - 5)
                for dg in range(4 * q, 4 * q + 4):
                    zero_power, i0 = (SC - 1, 0) if dg < G5 else (0, 1)
                    last = mm(pb[(q + 2) % 6][0:C5, P * (dg % 4):P * (dg % 4) + P], BtT[:, dg, zero_power, :],
                              Ct[:, dg, i0:i0 + SC, :].rearrange("p i c -> p (i c)"), start=True, stop=True)
                last.then_inc(s["kp"], 1)
            pe.wait_ge(s["u_in"], 16 * SC)
            for q in range(4):
                if q < 3:
                    pe.wait_ge(s["ke"], 4 + 2 * q)
                else:
                    pe.wait_ge(s["z"], 1)
                for i in range(8):
                    dg = 8 * q + i
                    u = U5[:, dg % G5, :] if dg < G5 else U5[:, dg % G5, ::-1]
                    c = slice(NK * i, NK * i + NK)
                    mm(X_BANK[q][0][:, c], Bt[:, dg, :], u, start=True, stop=True)
                    mm(X_BANK[q][1][0:HD, c], Bt[:, dg, HD:P], u, start=True, stop=True)
                    last = mm(X_BANK[q][1][HD:P, c], Bt[:, dg, 0:HD], u, start=True, stop=True)
                last.then_inc(s["xin"], 1)
            early(4)
            early(5)
            for q in range(4):
                pe.wait_ge(s["z"], max(q + 1, 2))
                mm(pb[q][:, :], cst("half_swap"), flat(T2[:, 8 * q:8 * q + 8, :]),
                   start=True, stop=True).then_inc(s["zs"], 1)
            pe.wait_ge(s["m5"], 16 * (2 * SC - 1))
            pe.wait_ge(s["xs"], 1)
            for g in range(G5):
                y = pb[4 + g // 8][:, NK * (g % 8):NK * (g % 8) + NK]
                mm(y, M5[:, g, :], U5[:, g, :], start=True, stop=False)
                mm(y[:, 1:NK], Ct[:, g, 1:NPOW, :].rearrange("p i c -> p (i c)"), T2[:, g, 0:NK - 1],
                   start=False, stop=False)
                last = mm(y[:, 0:NK - 1], Ct[:, G5 + g, 0:SC, :].rearrange("p i c -> p (i c)"),
                          T2[:, G5 + g, NK - 2::-1], start=False, stop=True)
            last.then_inc(s["y5"], 1)
            early(6)
            early(7)
            pe.wait_ge(s["z5"], 2)
            for m in range(2):
                for k in range(2):
                    last = mm(pb[m][:, :], pcol("w_glu")[:, 256 * k + P * m:256 * k + P * m + P], yT[k],
                              start=(k == 0), stop=(k == 1))
                last.then_inc(s["glu"], 1)
            pe.wait_ge(s["o_c"], 2)
            pe.wait_ge(s["y5_e"], 2)
            pe.wait_ge(s["res"], 2 * NB)
            for n in range(2 * NB):
                projected(n, range(6, KT), pb[n])

            pe.wait_ge(s["h2"], NB)
            for k in range(KT):
                for b in range(NB):
                    last = tr(pb[k][:, P * b:P * b + P], h[:, b, P * k:P * k + P], ident)
                last.then_inc(s["h2t"], 1)
            pe.wait_ge(s["h2_d"], KT // 2)
            pe.wait_ge(s["h2_a"], KT // 2)
            for b in range(NB):
                for k in range(KT):
                    last = mm(pb[0][:, RW * b:RW * b + RW], hT[:, k, P * b:P * b + P],
                              pcol("router_w")[:, RW * k:RW * k + RW], start=(k == 0), stop=(k == KT - 1))
            last.then_inc(s["rl"], 1)
            pe.wait_ge(s["sel"], 1)
            chosen = rt[8][:, 0:NB * NE].rearrange("p (b e) -> p b e", b=NB)
            for b in range(NB):
                for c in range(b + 1):
                    mm(pb[1][:, NE * b:NE * b + NE], cst("before") if c == b else cst("ones"), chosen[:, c, :],
                       start=(c == 0), stop=(c == b))
            for c in range(NB):
                last = mm(pb[1][:, P:P + NE], cst("ones"), chosen[:, c, :], start=(c == 0), stop=(c == NB - 1))
            last.then_inc(s["cnt"], 1)

            def tokens(e, par, loads):
                free = pe.snap(e - 1) if not isinstance(e, int) or e >= 2 else None
                landed = pe.snap(loads * 16)
                pe.wait_ge(xg_in[par], landed)
                if free is not None:
                    pe.wait_ge(s["xt_e"], free)
                pe.wait_ge(s["dest"], 1)
                mm(pb[par][:, 0:CAP], xg[par][0:CAP, 0::KT], ident[0:CAP, 0:CAP], start=True, stop=True)
                for k in range(1, KT):
                    last = tr(pb[par][:, CAP * k:CAP * k + CAP], xg[par][0:CAP, k::KT], ident[0:CAP, 0:CAP])
                last.then_inc(s["xt"], 1)

            def gate_up(e, par, loads):
                done, free = pe.snap(e + 1), (pe.snap(e - 1) if not isinstance(e, int) or e >= 2 else None)
                lot = [pe.snap((LOADS[3 * par + i] + loads) * 16) for i in range(2)]
                pe.wait_ge(s["xt_e"], done)
                if free is not None:
                    pe.wait_ge(s["hid"], free)
                pe.wait_ge(slot[3 * par], lot[0])
                pe.wait_ge(slot[3 * par + 1], lot[1])
                for k in range(KT):
                    mm(pb[2 + par][0:CAP, :], xT[par][:, k, :], W_gate[par][:, k, :], start=(k == 0), stop=(k == KT - 1))
                    last = mm(pb[2 + par][CAP:P, :], xT[par][:, k, :], W_up[par][:, k, :],
                              start=(k == 0), stop=(k == KT - 1))
                last.then_inc(s["gu"], 1)

            def hidden(e, par):
                done, free = pe.snap(e + 1), (pe.snap(e) if not isinstance(e, int) or e >= 1 else None)
                pe.wait_ge(s["hid"], done)
                if free is not None:
                    pe.wait_ge(s["ht_e"], free)
                pe.wait_ge(s["res"], 4 * NB)
                mm(pb[4][:, 0:CAP], hid[par][0:CAP, 0::FT], ident[0:CAP, 0:CAP], start=True, stop=True)
                for k in range(1, FT):
                    last = tr(pb[4][:, CAP * k:CAP * k + CAP], hid[par][0:CAP, k::FT], ident[0:CAP, 0:CAP])
                last.then_inc(s["ht"], 1)

            def down(e, par, loads):
                done, free = pe.snap(e + 1), (pe.snap(e - 1) if not isinstance(e, int) or e >= 2 else None)
                lot = pe.snap((LOADS[3 * par + 2] + loads) * 16)
                pe.wait_ge(s["ht_e"], done)
                if free is not None:
                    pe.wait_ge(s["ye"], free)
                pe.wait_ge(slot[3 * par + 2], lot)
                for k in range(FT):
                    mm(pb[5 + par][0:CAP, :], hidT[par][:, k, :], W_down[par][:, k, 0:512],
                       start=(k == 0), stop=(k == FT - 1))
                    last = mm(pb[5 + par][CAP:P, :], hidT[par][:, k, :], W_down[par][:, k, 512:1024],
                              start=(k == 0), stop=(k == FT - 1))
                last.then_inc(s["dn"], 1)

            tokens(0, 0, 1)
            gate_up(0, 0, 1)
            tokens(1, 1, 1)

            def pair(j):
                gate_up(j * 2 + 1, 1, j + 1)
                hidden(j * 2, 0)
                tokens(j * 2 + 2, 0, j + 2)
                down(j * 2, 0, j + 1)
                gate_up(j * 2 + 2, 0, j + 2)
                hidden(j * 2 + 1, 1)
                tokens(j * 2 + 3, 1, j + 2)
                down(j * 2 + 1, 1, j + 1)

            pair(0)
            with pe.Fori(1, NE // 2 - 1) as j:
                pair(j)
            gate_up(NE - 1, 1, NE // 2)
            hidden(NE - 2, 0)
            down(NE - 2, 0, NE // 2)
            hidden(NE - 1, 1)
            down(NE - 1, 1, NE // 2)
            pe.wait_ge(s["ye"], NE)
            n_over = pe.value_load(over_i[0:1, NOVER:NOVER + 1], min_val=0, max_val=NOVER)
            with pe.If(n_over > 0):
                with pe.Fori(0, n_over) as i:
                    tokens(i + NE, 0, i + NE // 2 + 1)
                    gate_up(i + NE, 0, i + NE // 2 + 1)
                    hidden(i + NE, 0)
                    down(i + NE, 0, i + NE // 2 + 1)

        def scalar_program(act, layer):
            A = nc.scalar.activation
            link = linker(act, s["act"])
            eps = cst("eps")
            act.dma_start(pk[:, :], pack[layer]).then_inc(s["pack"], 16)
            act.dma_start(gB[:, :], gains[layer, 0]).then_inc(s["gain1"], 16)

            def norm_scales(done):
                for b in range(NB):
                    ins = A(h[:, b, :], x[:, b, :], ACT.Square, accum_out=small[:, 36 + b:37 + b])
                    if b == NB - 1:
                        link(ins)
                link(A(small[:, 44:48], small[:, 36:40], ACT.Ln, bias=eps, scale=1.0 / D))
                A(small[:, 40:44], small[:, 44:48], ACT.Exp, scale=-0.5).then_inc(done, 1)

            def evacuate(n):
                act.wait_ge(s["pe"], n + 1)
                if n == 25:
                    act.wait_ge(s_zeroed, ZEROINGS * 16)
                to, of = evac_views(n)
                A(to, of, ACT.Copy).then_inc(s["ev_a"], 1)

            norm_scales(s["rstd"])
            act.wait_ge(s["pack"], 16)
            lb_raw = pcol("lb")
            act.wait_ge(s["lb"], 1)
            A(lbs[:, 0:8], lbs[:, 0:8], ACT.Exp).then_inc(s["lb_e"], 1)
            act.wait_ge(s["h"], NB)
            A(pv_dt, pcol("log_dt"), ACT.Exp).then_inc(s["dt"], 1)
            for n in range(1, 8, 2):
                evacuate(n)
            act.wait_ge(s["ang"], 1)
            A(pv_rho, pv_lr, ACT.Exp)
            A(pv_rho8, pv_lr, ACT.Exp, scale=float(SC))
            A(pv_sin, pv_r, ACT.Sin)
            A(pv_cos, pv_rc, ACT.Sin).then_inc(s["lam"], 1)
            for n in range(9, 14, 2):
                evacuate(n)

            jobs = [hq[0], hq[1]] + Z + hg

            def sig_exp(j):
                n = {0: 12, 1: 13, 2: 8, 3: 9, 4: 10, 5: 11, 6: 20, 7: 21}[j]
                wait_evacuated(act, n)
                if j:
                    act.wait_ge(s["sig_r"], j)
                if 2 <= j < 6:
                    A(ht_e, jobs[j], ACT.Exp, scale=-1.0).then_inc(s["sig_e"], 1)
                else:
                    A(ht_e, jobs[j], ACT.Tanh, scale=0.5).then_inc(s["sig_e"], 1)

            def q_copies(p):
                act.wait_ge(s["q_silu"], p + 1)
                for i in range(2):
                    for half in range(2):
                        A(q_dec[2 * p + i][HD * half:HD * half + HD, :], hq[p][HD * i:HD * i + HD, :],
                          ACT.Copy, scale=0.5).then_inc(s["q_copy"], 1)

            def rope_square(j):
                wait_evacuated(act, [14, 16, 17, 18, 19][j])
                if j == 0:
                    act.wait_ge(s["pe"], 16)
                A(rope_sq[j], rope_x[j], ACT.Square).then_inc(s["r_sq"], 1)

            def rope_rstd(j):
                act.wait_ge(s["r_pe"], j + 1)
                link(A(rope_sq[j], pb[6][:, :], ACT.Ln, bias=eps, scale=1.0 / HD))
                A(rope_sq[j], rope_sq[j], ACT.Exp, scale=-0.5).then_inc(s["r_rs"], 1)

            sig_exp(0)
            sig_exp(1)
            q_copies(0)
            q_copies(1)
            evacuate(15)
            sig_exp(2)
            rope_square(0)
            evacuate(17)
            sig_exp(3)
            rope_square(1)
            rope_square(2)
            evacuate(19)
            rope_square(3)
            rope_square(4)
            sig_exp(4)
            rope_rstd(0)
            evacuate(21)
            sig_exp(5)
            rope_rstd(1)
            evacuate(23)
            rope_rstd(2)
            sig_exp(6)
            evacuate(25)
            rope_rstd(3)
            sig_exp(7)
            rope_rstd(4)

            def hgrn_copies(hh):
                act.wait_ge(s["ke_t"], hh + 1)
                if hh == 0:
                    act.wait_ge(s["pe"], NG)
                if hh >= 2:
                    act.wait_ge(s["kv"], NB * (hh - 1))
                A(k_endT[hh % 2], pb[0][:, :], ACT.Copy).then_inc(s["ke_e"], 1)
                if hh >= 2:
                    act.wait_ge(s["state"], hh - 1)
                A(dec_sb[hh % 2], dec_s[hh][:, None, :].broadcast_to([P, HD, NCH]), ACT.Copy).then_inc(s["dec"], 1)
                act.wait_ge(s["kv"], NB * hh + NB)
                for b in range(NB):
                    A(kv_sb[hh % 2][:, :, CB * b:CB * b + CB], pb[b][:, :].rearrange("p (c v) -> p v c", c=CB),
                      ACT.Copy).then_inc(s["kv_e"], 1)

            def pair_copy(p):
                act.wait_ge(s["ho"], 2 * p + 2)
                A(o_sb[p][:, 0:T - CH], pb[4][:, 0:T - CH], ACT.Copy).then_inc(s["ho_b"], 1)

            hgrn_copies(0)
            hgrn_copies(1)
            hgrn_copies(2)
            pair_copy(0)
            hgrn_copies(3)
            act.wait_ge(s["ho_s"], 1)
            A(o_rs[0], o_sb[0], ACT.Square).then_inc(s["ho_q"], 1)
            pair_copy(1)
            act.wait_ge(s["ho_s"], 2)
            A(o_rs[1], o_sb[1], ACT.Square).then_inc(s["ho_q"], 1)
            act.wait_ge(s["r_done"], 5)
            for kv in range(2):
                for half in range(2):
                    A(k_dup[kv][HD * half:HD * half + HD, :], ak[HD * kv:HD * kv + HD, :],
                      ACT.Copy).then_inc(s["k_dup"], 1)
            for p in range(2):
                act.wait_ge(s["ho_m"], p + 1)
                link(A(o_rs[p], pb[5 + p][:, :], ACT.Ln, bias=eps, scale=1.0 / HD))
                A(o_rs[p], o_rs[p], ACT.Exp, scale=-0.5).then_inc(s["ho_r"], 1)

            def probs(u):
                act.wait_ge(s["mx"], u + 1)
                if u >= 3:
                    act.wait_ge(s["pt"], u - 2)
                A(p_sb[u % 3], pb[S_BANK[u % 3]][:, :], ACT.Exp, bias=p_bias[u % 3], scale=SCALE,
                  accum_out=p_sum[u % 3]).then_inc(s["ex"], 1)

            probs(0)
            probs(1)
            for u in range(NU):
                act.wait_ge(s["pt"], u + 1)
                if u >= 3:
                    act.wait_ge(s["pv"], u - 2)
                A(pT_sb[u % 3], pb[T_BANK[u % 3]][:, :], ACT.Copy).then_inc(s["pt_e"], 1)
                if u + 2 < NU:
                    probs(u + 2)
                if u % (2 * NB) == 1 and u > 1:
                    pair = u // (2 * NB) - 1
                    act.wait_ge(s["pv"], 2 * NB * (pair + 1))
                    A(aq[pair], pb[4 + pair % 2][:, :], ACT.Copy).then_inc(s["o_b"], 1)
            act.wait_ge(s["pv"], NU)
            A(aq[3], pb[5][:, :], ACT.Copy).then_inc(s["o_b"], 1)

            for q in range(1, 8, 2):
                act.wait_ge(s["bt"], q + 1)
                A(flat(Bt[:, 4 * q:4 * q + 4, :]), pb[q % 6][:, :], ACT.Copy).then_inc(s["bt_e"], 1)
            for q in range(8):
                act.wait_ge(s["kp"], q + 1)
                to = (Kf if q < 4 else Kb)[:, 4 * (q % 4):4 * (q % 4) + 4, :, :].rearrange("p g i c -> p (g i c)")
                A(to, pb[(q + 2) % 6][0:C5, :], ACT.Copy).then_inc(s["ke"], 1)
            act.wait_ge(s["y5"], 1)
            for i in range(2):
                A(flat(Y5[:, 8 * i:8 * i + 8, :]), pb[4 + i][:, :], ACT.Copy).then_inc(s["y5_e"], 1)
            for i in range(2):
                act.wait_ge(s["ge"], i + 1)
                A(gt[i], gt[i], ACT.Tanh, scale=float(np.sqrt(2.0 / np.pi))).then_inc(s["gx"], 1)
            for i in range(2):
                act.wait_ge(s["glu"], i + 1)
                A(gt[i], pb[i][:, :], ACT.Tanh, scale=0.25, bias=small[:, 56 + i:57 + i]).then_inc(s["glx"], 1)

            act.wait_ge(s["res"], 4 * NB)
            act.wait_ge(s["o_c"], 2)
            norm_scales(s["rstd2"])
            for k in range(1, KT, 2):
                act.wait_ge(s["h2t"], k + 1)
                A(hT[:, k, :], pb[k][:, :], ACT.Copy).then_inc(s["h2_a"], 1)
            act.wait_ge(s["gs"], 1)
            A(rt[1][:, 0:16], rt[1][:, 0:16], ACT.Exp).then_inc(s["gx2"], 1)
            act.wait_ge(s["sel"], 1)
            A(small[:, 32:36], small[:, 28:32], ACT.Exp).then_inc(s["sx"], 1)

            def load_tokens(e, par):
                row = act.snap(e * CAP)
                act.dma_start(xg[par][0:CAP, :], xbuf[bass.ds(row, CAP), :]).then_inc(xg_in[par], 16)

            def tokens(e, par, ahead=True):
                done, free = act.snap(e + 1), (act.snap(e - 1) if not isinstance(e, int) or e >= 2 else None)
                act.wait_ge(s["xt"], done)
                if ahead:
                    load_tokens(e + 2, par)
                if free is not None:
                    act.wait_ge(s["gu"], free)
                A(flat(xT[par]), pb[par][:, :], ACT.Copy).then_inc(s["xt_e"], 1)

            def gate_exp(e, par):
                done, free = act.snap(e + 1), (act.snap(e) if not isinstance(e, int) or e >= 1 else None)
                act.wait_ge(s["gu"], done)
                if free is not None:
                    act.wait_ge(s["er"], free)
                A(e_e[0:CAP, :], pb[2 + par][0:CAP, :], ACT.Tanh, scale=0.5).then_inc(s["ee"], 1)

            def rows(e, par, before):
                done, stored = act.snap(e + 1), act.snap(before * 32)
                row = act.snap(e * CAP)
                act.wait_ge(s["dn"], done)
                act.wait_ge(y_out[par], stored)
                A(y_sb[par], pb[5 + par][:, :], ACT.Copy, scale=0.5).then_inc(s["ye"], 1)
                act.wait_ge(s["ye"], done)
                for n in range(2):
                    act.dma_start(ybuf[bass.ds(row, CAP), 512 * n:512 * n + 512],
                                  y_sb[par][CAP * n:CAP * n + CAP, :]).then_inc(y_out[par], 16)

            dispatched = act.snap(layer * PER_LAYER + PER_LAYER)
            act.wait_ge(s_dispatched, dispatched)
            load_tokens(0, 0)
            load_tokens(1, 1)
            tokens(0, 0)
            gate_exp(0, 0)
            tokens(1, 1)

            def pair(j):
                gate_exp(j * 2 + 1, 1)
                tokens(j * 2 + 2, 0)
                rows(j * 2, 0, j)
                gate_exp(j * 2 + 2, 0)
                tokens(j * 2 + 3, 1)
                rows(j * 2 + 1, 1, j)

            pair(0)
            with act.Fori(1, NE // 2 - 2) as j:
                pair(j)
            gate_exp(NE - 3, 1)
            tokens(NE - 2, 0, ahead=False)
            rows(NE - 4, 0, NE // 2 - 2)
            gate_exp(NE - 2, 0)
            tokens(NE - 1, 1, ahead=False)
            rows(NE - 3, 1, NE // 2 - 2)
            gate_exp(NE - 1, 1)
            rows(NE - 2, 0, NE // 2 - 1)
            rows(NE - 1, 1, NE // 2 - 1)
            n_over = act.value_load(over_i[0:1, NOVER:NOVER + 1], min_val=0, max_val=NOVER)
            all_even = act.snap((n_over + NE // 2) * 32)
            with act.If(n_over > 0):
                with act.Fori(0, n_over) as i:
                    load_tokens(i + NE, 0)
                    tokens(i + NE, 0, ahead=False)
                    gate_exp(i + NE, 0)
                    rows(i + NE, 0, i + NE // 2)
            act.wait_ge(y_out[1], 32 * (NE // 2))
            act.wait_ge(y_out[0], all_even)
            A(small[:, 63:64], eps, ACT.Copy).then_inc(s["stored"], 1)

        (pv_dt, pv_lr, pv_r, pv_rc, pv_rho, pv_rho8, pv_sin, pv_cos, pv_fr, pv_fi) = ss

        def vector_program(dve, layer):
            V = nc.vector
            TS, TT, STT = V.tensor_scalar, V.tensor_tensor, V.scalar_tensor_tensor
            link = linker(dve, s["dve"])

            def h_rows(scale_sem, done):
                dve.wait_ge(scale_sem, 1)
                for b in range(NB):
                    STT(out=h[:, b, :], in0=x[:, b, :], scalar=small[:, 40 + b:41 + b], in1=gB[:, :],
                        op0=ALU.mult, op1=ALU.mult).then_inc(done, 1)

            def evacuate(n):
                dve.wait_ge(s["pe"], n + 1)
                if n == 24:
                    dve.wait_ge(s_zeroed, ZEROINGS * 16)
                to, of = evac_views(n)
                V.tensor_copy(to, of).then_inc(s["ev_d"], 1)

            dve.wait_ge(s["pack"], 16)
            lb = pcol("lb").rearrange("p (l h) -> p l h", l=L)
            link(TT(lbs[:, 8:12], lb[:, 0, :], lb[:, 1, :], ALU.max))
            for j in range(L):
                ins = TT(lbs[:, 4 * j:4 * j + 4], lb[:, j, :], lbs[:, 8:12], ALU.subtract)
            ins.then_inc(s["lb"], 1)
            dve.wait_ge(s["gain1"], 16)
            h_rows(s["rstd"], s["h"])
            dve.wait_ge(s["lb_e"], 1)
            link(TT(lbs[:, 8:12], lbs[:, 0:4], lbs[:, 4:8], ALU.add))
            link(V.reciprocal(lbs[:, 8:12], lbs[:, 8:12]))
            ws = pcol("lb_sum")
            link(TS(lbs[:, 12:16], lbs[:, 0:4], ws[:, 0:1], None, ALU.mult))
            link(STT(out=lbs[:, 12:16], in0=lbs[:, 4:8], scalar=ws[:, 1:2], in1=lbs[:, 12:16], op0=ALU.mult, op1=ALU.add))
            link(TT(lbs[:, 12:16], lbs[:, 12:16], lbs[:, 8:12], ALU.mult))
            link(TS(lbs[:, 16:20], lbs[:, 12:16], -1.0, 1.0, ALU.mult, ALU.add))
            link(TS(small[:, 56:58], pcol("b_glu"), 0.5, None, ALU.mult))
            for n in range(0, 14, 2):
                evacuate(n)
                if n == 8:
                    dve.wait_ge(s["den"], 1)
                    V.reciprocal(pv_den, pv_den).then_inc(s["inv"], 1)

            def sigmoid(j):
                dve.wait_ge(s["sig_e"], j + 1)
                link(TS(ht_s, ht_e, 1.0, None, ALU.add))
                link(V.reciprocal(ht_s, ht_s))

            def silu(j, z, count):
                dve.wait_ge(s["sig_e"], j + 1)
                STT(out=z, in0=ht_e, scalar=1.0, in1=z, op0=ALU.add, op1=ALU.mult).then_inc(s["q_silu"], 1)
                dve.wait_ge(s["q_silu"], count)
                V.memset(small[:, 60:61], 0.0).then_inc(s["sig_r"], 1)

            def gate_chain(hh):
                one_less = lbs[:, 16 + hh:17 + hh]
                bound = lbs[:, 12 + hh:13 + hh]
                dve.wait_ge(s["sig_e"], 3 + hh)
                link(TS(ht_e, ht_e, 1.0e30, None, ALU.min))
                sigmoid(2 + hh)
                if hh:
                    dve.wait_ge(s["f_split"], hh)
                link(TS(ht_f, ht_s, one_less, bound, ALU.mult, ALU.add))
                V.memset(small[:, 61:62], 0.0).then_inc(s["f_ready"], 1)
                link(STT(out=ht_k, in0=ht_e, scalar=one_less, in1=ht_s, op0=ALU.mult, op1=ALU.mult))
                V.memset(small[:, 60:61], 0.0).then_inc(s["sig_r"], 1)
                dve.wait_ge(s["f_split"], hh + 1)
                V.tensor_tensor_scan(out=ht_F[0:HD, :], data0=ht_d0[0:HD, :], data1=ht_d1[0:HD, :], initial=0.0,
                                     op0=ALU.mult, op1=ALU.add)
                link(V.tensor_tensor_scan(out=ht_F[HD:P, ::-1], data0=ht_d0[HD:P, ::-1], data1=ht_d1[HD:P, ::-1],
                                          initial=0.0, op0=ALU.mult, op1=ALU.add))
                V.tensor_copy(dec_n[0:HD, :], ht_F[0:HD, CH - 1::CH])
                V.tensor_copy(dec_n[HD:P, :], ht_F[HD:P, 0::CH])
                V.tensor_copy(dec_s[hh][0:HD, :], ht_F[0:HD, CH - 1::CH])
                V.tensor_copy(dec_s[hh][HD:P, :], ht_F[HD:P, T - CH::-CH])
                link(V.reciprocal(ht_R, ht_F))
                V.memset(dec_s[hh][:, 0:1], 0.0)
                if hh == 0:
                    dve.wait_ge(s["pe"], NG if False else KT + 1)
                link(TT(k_dec[hh], ht_k, ht_R, ALU.mult))
                TT(k_end[hh].rearrange("p (c t) -> p c t", t=CH), k_dec[hh].rearrange("p (c t) -> p c t", t=CH),
                   dec_n[:, :, None].broadcast_to([P, NCH, CH]), ALU.mult)
                dve.wait_ge(s["q_copy"], 8)
                TT(q_dec[hh], q_dec[hh], ht_F, ALU.mult).then_inc(s["head"], 1)
                dve.wait_ge(s["head"], hh + 1)

            def rope_gain(j):
                dve.wait_ge(s["r_sq"], j + 1)
                TS(rope_x[j], rope_x[j], pcol("k_g" if j == 0 else "q_g"), None, ALU.mult).then_inc(s["r_y"], 1)

            def rope_turn(j):
                dve.wait_ge(s["r_pe"], j + 1)
                TT(rope_t, pb[7][:, :], cst("sin"), ALU.mult)
                link(TT(rope_x[j], rope_x[j], cst("cos"), ALU.mult))
                link(TT(rope_x[j], rope_x[j], rope_t, ALU.add))
                dve.wait_ge(s["r_rs"], j + 1)
                TT(rope_x[j], rope_x[j], rope_sq[j], ALU.mult).then_inc(s["r_done"], 1)
                dve.wait_ge(s["r_done"], j + 1)

            silu(0, hq[0], 1)
            silu(1, hq[1], 2)
            evacuate(14)
            gate_chain(0)
            evacuate(16)
            rope_gain(0)
            rope_gain(1)
            gate_chain(1)
            evacuate(18)
            rope_gain(2)
            rope_gain(3)
            rope_turn(0)
            gate_chain(2)
            evacuate(20)
            rope_gain(4)
            rope_turn(1)
            gate_chain(3)
            evacuate(22)
            rope_turn(2)
            evacuate(24)
            silu(6, hg[0], 3)
            rope_turn(3)
            silu(7, hg[1], 4)
            rope_turn(4)

            def masked_scores(hh):
                dve.wait_ge(s["hs_pe"], hh + 1)
                if hh >= 2:
                    dve.wait_ge(s["ho"], hh - 1)
                if hh == 0:
                    dve.wait_ge(s["pe"], NG)
                mask = [cst(m)[:, None, :].broadcast_to([P, NB, P]) for m in ("mask_f", "mask_b")]
                b4 = lambda ap: ap.rearrange("p (b t) -> p b t", b=NB)
                TT(b4(sc_t), b4(pb[5][:, :]), mask[0], ALU.mult)
                link(TT(b4(sc_a[hh % 2]), b4(pb[6][:, :]), mask[1], ALU.mult))
                TT(sc_a[hh % 2], sc_a[hh % 2], sc_t, ALU.add).then_inc(s["hs_m"], 1)
                dve.wait_ge(s["hs_m"], hh + 1)

            def states(hh):
                dve.wait_ge(s["kv_e"], NB * hh + NB)
                dve.wait_ge(s["dec"], hh + 1)
                if hh >= 2:
                    dve.wait_ge(s["ho"], hh - 1)
                i = hh % 2
                V.tensor_tensor_scan(out=flat(st_sb[i]), data0=flat(dec_sb[i]), data1=flat(kv_sb[i]), initial=0.0,
                                     op0=ALU.mult, op1=ALU.add).then_inc(s["state"], 1)

            def pair_sum(p):
                dve.wait_ge(s["ho_b"], p + 1)
                V.tensor_copy(o_sb[p][:, T - CH:T], pb[7][:, T - CH:T])
                TT(o_sb[p][:, 0:T - CH], o_sb[p][:, 0:T - CH], pb[7][:, 0:T - CH], ALU.add).then_inc(s["ho_s"], 1)

            masked_scores(0)
            states(0)
            masked_scores(1)
            states(1)
            masked_scores(2)
            states(2)
            pair_sum(0)
            masked_scores(3)
            states(3)
            pair_sum(1)

            def row_max(u):
                dve.wait_ge(s["qk"], u + 1)
                if u >= 3:
                    dve.wait_ge(s["ex"], u - 2)
                link(V.reduce_max(p_max[u % 3], pb[S_BANK[u % 3]][:, :], AX.X))
                TS(p_bias[u % 3], p_max[u % 3], -SCALE, None, ALU.mult).then_inc(s["mx"], 1)

            def head_norm(p):
                dve.wait_ge(s["ho_r"], p + 1)
                link(STT(out=o_sb[p], in0=o_sb[p], scalar=pcol("hgrn_g"), in1=o_rs[p], op0=ALU.mult, op1=ALU.mult))
                STT(out=hq[p], in0=o_sb[p], scalar=0.5, in1=hg[p], op0=ALU.mult, op1=ALU.mult).then_inc(s["o_a"], 1)

            row_max(0)
            row_max(1)
            for u in range(NU):
                dve.wait_ge(s["ex"], u + 1)
                link(V.reciprocal(p_inv[u % 3], p_sum[u % 3]))
                TS(p_sb[u % 3], p_sb[u % 3], p_inv[u % 3], None, ALU.mult).then_inc(s["pn"], 1)
                if u + 2 < NU:
                    row_max(u + 2)
                if u < 2:
                    head_norm(u)

            def residual(n, bank, done):
                b, half = divmod(n, 2)
                dve.wait_ge(s["wo"], done)
                xs = x[:, b, 512 * half:512 * half + 512]
                TT(xs, xs, bank[:, :], ALU.add).then_inc(s["res"], 1)

            def early(n):
                residual(n, pb[6 + n % 2], n + 1)

            dve.wait_ge(s["pv"], NU)
            dve.wait_ge(s["bc"], 1)
            back = slice(G5, DG)
            ct_b = Ct[:, back, :, :]
            ct_t = ring[:, 3, 0:G5 * NPOW * C5].rearrange("p (d i c) -> p d i c", d=G5, i=NPOW)
            c_re, c_im = (s5[:, S5P[n][0]:S5P[n][0] + DG * C5].rearrange("p (d c) -> p d c", d=DG) for n in ("c_re", "c_im"))

            def power(w):
                return w[:, ::-1, back].rearrange("p i d -> p d i")[:, :, :, None].broadcast_to([P, G5, NPOW, C5])

            def value(v):
                return v[:, back, :][:, :, None, :].broadcast_to([P, G5, NPOW, C5])

            TT(ct_b, power(A3), value(c_re), ALU.mult)
            early(0)
            link(TT(ct_t, power(A4), value(c_im), ALU.mult))
            early(1)
            TT(ct_b, ct_b, ct_t, ALU.add).then_inc(s["ct"], 1)
            early(2)
            early(3)
            for q in range(0, 8, 2):
                dve.wait_ge(s["bt"], q + 1)
                V.tensor_copy(flat(Bt[:, 4 * q:4 * q + 4, :]), pb[q % 6][:, :]).then_inc(s["bt_v"], 1)
            dve.wait_ge(s["kp"], 8)
            dve.wait_ge(s["tab"], 1)
            for q in range(4):
                dve.wait_ge(s["xin"], q + 1)
                r = slice(8 * q, 8 * q + 8)
                a, b = (bank[:, :].rearrange("p (d k) -> p d k", d=8) for bank in X_BANK[q])
                TT(T1[:, r, :], a, cosT[:, r, :], ALU.mult)
                link(TT(T2[:, r, :], b, sinT[:, r, :], ALU.mult))
                link(TT(T1[:, r, :], T1[:, r, :], T2[:, r, :], ALU.add))
                if q == 0:
                    dve.wait_ge(s["rho"], 1)
                V.tensor_tensor_scan(out=flat(T2[:, r, :]), data0=flat(rho[:, r, :]), data1=flat(T1[:, r, :]), initial=0.0,
                                     op0=ALU.mult, op1=ALU.add).then_inc(s["z"], 1)
                if q == 0:
                    dve.wait_ge(s["ke"], 8)
                    diag_f, diag_b = Kf[:, :, 0, :], Kb[:, :, SC - 1, :]
                    TT(diag_f, diag_f, diag_b, ALU.add).then_inc(s["kdiag"], 1)
                dve.wait_ge(s["z"], q + 1)
                link(TT(T1[:, r, :], T2[:, r, :], cosT[:, r, :], ALU.mult))
            early(4)
            early(5)
            for q in range(4):
                r = slice(8 * q, 8 * q + 8)
                dve.wait_ge(s["zs"], q + 1)
                link(TT(T2[:, r, :], pb[q][:, :].rearrange("p (d k) -> p d k", d=8), sinT[:, r, :], ALU.mult))
                ins = TT(T2[:, r, :], T1[:, r, :], T2[:, r, :], ALU.subtract)
            ins.then_inc(s["xs"], 1)
            early(6)
            early(7)
            dve.wait_ge(s["y_in"], 32)
            dve.wait_ge(s["y5"], 1)
            for m in range(2):
                z, t = yT[m], gt[m]
                link(STT(out=z, in0=uT[m], scalar=pcol("s5_d")[:, m:m + 1], in1=z, op0=ALU.mult, op1=ALU.add))
                link(TT(t, z, z, ALU.mult))
                link(TS(t, t, 0.044715, 1.0, ALU.mult, ALU.add))
                TT(t, t, z, ALU.mult).then_inc(s["ge"], 1)
            for m in range(2):
                dve.wait_ge(s["gx"], m + 1)
                STT(out=yT[m], in0=gt[m], scalar=1.0, in1=yT[m], op0=ALU.add, op1=ALU.mult).then_inc(s["z5"], 1)
            for m in range(2):
                z, t, r = yT[m], gt[m], gt[2 + m]
                dve.wait_ge(s["glx"], m + 1)
                dve.wait_ge(s["z5"], 2)
                link(TS(r, t, 0.25, 0.25, ALU.mult, ALU.add))
                TT(uT[m].rearrange("p (k t) -> p t k", t=SC), z.rearrange("p (t k) -> p t k", t=SC),
                   r.rearrange("p (t k) -> p t k", t=SC), ALU.mult).then_inc(s["o_c"], 1)
            for n in range(2 * NB):
                residual(n, pb[n], 2 * NB + n + 1)
            dve.wait_ge(s["gain2"], 16)
            h_rows(s["rstd2"], s["h2"])
            for k in range(0, KT, 2):
                dve.wait_ge(s["h2t"], k + 1)
                V.tensor_copy(hT[:, k, :], pb[k][:, :]).then_inc(s["h2_d"], 1)

            def v3(i, n):
                return rt[i][:, 0:NB * n].rearrange("p (b e) -> p b e", b=NB)

            def bc(ap, n):
                return ap[:, :, None].broadcast_to([P, NB, n])

            def per_block(ap, n):
                return ap[:, None, :].broadcast_to([P, NB, n])

            logits = v3(0, RW)
            dve.wait_ge(s["rl"], 1)
            link(TT(logits, pb[0][:, 0:NB * RW].rearrange("p (b e) -> p b e", b=NB), per_block(pcol("router_b"), RW), ALU.add))
            g_log, e_log = logits[:, :, 0:EG], logits[:, :, EG:RW]
            g_rel, g_hot, e_in, hot1, hot2, e_tmp = v3(1, EG), v3(2, EG), v3(3, NE), v3(4, NE), v3(5, NE), v3(6, NE)
            chosen, e_msk = v3(8, NE), v3(7, NE)
            col = [rt[9][:, 4 * i:4 * i + 4] for i in range(10)]

            def first_of(hot, values, top, ids, n):
                link(TT(hot, values, bc(top, n), ALU.is_equal))
                link(TT(hot, hot, per_block(ids, n), ALU.mult))
                link(V.tensor_reduce(out=col[9], in_=hot, axis=AX.X, op=ALU.min))
                link(TT(hot, per_block(ids, n), bc(col[9], n), ALU.is_equal))

            link(V.reduce_max(col[0], g_log, AX.X))
            TT(g_rel, g_log, bc(col[0], EG), ALU.subtract).then_inc(s["gs"], 1)
            first_of(g_hot, g_log, col[0], cst("group_id"), EG)
            grp = lambda ap: ap.rearrange("p b (g e) -> p b g e", g=EG)
            for b in range(NB):
                link(TT(e_in[:, b, :].rearrange("p (g e) -> p g e", g=EG), e_log[:, b, :].rearrange("p (g e) -> p g e", g=EG),
                        g_hot[:, b, :, None].broadcast_to([P, EG, EPG]), ALU.mult))
                link(V.tensor_copy(e_tmp[:, b, :].rearrange("p (g e) -> p g e", g=EG),
                                   g_hot[:, b, :, None].broadcast_to([P, EG, EPG])))
            link(TS(rt[6][:, 0:NB * NE], rt[6][:, 0:NB * NE], 1.0, NEG, ALU.subtract, ALU.mult))
            link(TT(e_in, e_in, e_tmp, ALU.add))
            link(V.reduce_max(col[1], e_in, AX.X))
            first_of(hot1, e_in, col[1], cst("expert_id"), NE)
            link(STT(out=rt[7][:, 0:NB * NE], in0=rt[4][:, 0:NB * NE], scalar=-2.0 * NEG, in1=rt[3][:, 0:NB * NE],
                     op0=ALU.mult, op1=ALU.add))
            link(V.reduce_max(col[2], e_msk, AX.X))
            first_of(hot2, e_msk, col[2], cst("expert_id"), NE)
            link(TT(chosen, hot1, hot2, ALU.add))
            TT(small[:, 28:32], col[2], col[1], ALU.subtract).then_inc(s["sel"], 1)
            dve.wait_ge(s["gx2"], 1)
            link(V.tensor_reduce(out=col[3], in_=g_rel, axis=AX.X, op=ALU.add))
            link(V.reciprocal(col[3], col[3]))
            dve.wait_ge(s["sx"], 1)
            link(TS(col[4], small[:, 32:36], 1.0, None, ALU.add))
            link(V.reciprocal(col[4], col[4]))
            link(TT(gate_w[:, 0:NB], col[4], col[3], ALU.mult))
            link(TT(gate_w[:, NB:2 * NB], gate_w[:, 0:NB], small[:, 32:36], ALU.mult))
            dve.wait_ge(s["cnt"], 1)
            pos, cnt = v3(6, NE), rt[10][:, 0:NE]
            ext, run, base = rt[10][:, 32:64], rt[10][:, 64:96], rt[10][:, 96:128]
            link(V.tensor_copy(rt[6][:, 0:NB * NE], pb[1][:, 0:NB * NE]))
            link(V.tensor_copy(cnt, pb[1][:, P:P + NE]))
            many = qd[:, 1760:1760 + 7 * NE].rearrange("p (e m) -> p e m", m=7)
            link(TT(many, cnt[:, :, None].broadcast_to([P, NE, 7]), cst("chunk_end")[:, None, :].broadcast_to([P, NE, 7]),
                    ALU.is_gt))
            link(V.tensor_reduce(out=ext, in_=many, axis=AX.X, op=ALU.add))
            link(V.tensor_tensor_scan(out=run, data0=cst("ones")[:, 0:NE], data1=ext, initial=0.0,
                                      op0=ALU.mult, op1=ALU.add))
            link(TT(base, run, ext, ALU.subtract))
            link(TS(base, base, float(CAP), float((NE - 1) * CAP), ALU.mult, ALU.add))
            link(TT(base, base, cst("expert_row"), ALU.subtract))
            far = v3(7, NE)
            link(TS(rt[7][:, 0:NB * NE], rt[6][:, 0:NB * NE], float(CAP), None, ALU.is_ge))
            link(TT(far, far, per_block(base, NE), ALU.mult))
            link(TT(far, far, per_block(cst("expert_row"), NE), ALU.add))
            link(TT(far, far, pos, ALU.add))
            for j, hot in enumerate((hot1, hot2)):
                link(TT(pos, far, hot, ALU.mult))
                link(V.tensor_reduce(out=col[5 + j], in_=pos, axis=AX.X, op=ALU.add))
                link(V.tensor_copy(dest_i[:, NB * j:NB * j + NB], col[5 + j]))
            over = qd[:, 1760 - 0:1760 + 0 + 224]
            wide = hbuf[:, 4096:4096 + NOVER * NE].rearrange("p (i e) -> p i e", i=NOVER)
            link(TT(wide, run[:, None, :].broadcast_to([P, NOVER, NE]),
                    cst("over_id")[:, :, None].broadcast_to([P, NOVER, NE]), ALU.is_le))
            link(V.tensor_reduce(out=rt[9][:, 100:100 + NOVER], in_=wide, axis=AX.X, op=ALU.add))
            link(TS(rt[9][:, 100:100 + NOVER], rt[9][:, 100:100 + NOVER], float(NE - 1), None, ALU.min))
            link(V.tensor_copy(over_i[:, 0:NOVER], rt[9][:, 100:100 + NOVER]))
            V.tensor_copy(over_i[:, NOVER:NOVER + 1], run[:, NE - 1:NE]).then_inc(s["dest"], 1)

            def hidden_rows(e, par):
                done, free = dve.snap(e + 1), (dve.snap(e - 1) if not isinstance(e, int) or e >= 2 else None)
                dve.wait_ge(s["ee"], done)
                if free is not None:
                    dve.wait_ge(s["ht"], free)
                top, bottom = pb[2 + par][0:CAP, :], pb[2 + par][CAP:P, :]
                STT(out=e_s[0:CAP, :], in0=e_e[0:CAP, :], scalar=1.0, in1=top, op0=ALU.add, op1=ALU.mult).then_inc(s["ec"], 1)
                dve.wait_ge(s["ec"], done)
                V.memset(small[:, 62:63], 0.0).then_inc(s["er"], 1)
                TT(hid[par][0:CAP, :], e_s[0:CAP, :], bottom, ALU.mult).then_inc(s["hid"], 1)

            def hidden_t(e, par):
                done, free = dve.snap(e + 1), (dve.snap(e - 1) if not isinstance(e, int) or e >= 2 else None)
                dve.wait_ge(s["ht"], done)
                if free is not None:
                    dve.wait_ge(s["dn"], free)
                V.tensor_copy(flat(hidT[par]), pb[4][:, 0:FT * CAP]).then_inc(s["ht_e"], 1)

            hidden_rows(0, 0)

            def pair(j):
                hidden_t(j * 2, 0)
                hidden_rows(j * 2 + 1, 1)
                hidden_t(j * 2 + 1, 1)
                hidden_rows(j * 2 + 2, 0)

            pair(0)
            with dve.Fori(1, NE // 2 - 1) as j:
                pair(j)
            hidden_t(NE - 2, 0)
            hidden_rows(NE - 1, 1)
            hidden_t(NE - 1, 1)
            dve.wait_ge(s["dn"], NE)
            n_over = dve.value_load(over_i[0:1, NOVER:NOVER + 1], min_val=0, max_val=NOVER)
            with dve.If(n_over > 0):
                with dve.Fori(0, n_over) as i:
                    hidden_rows(i + NE, 0)
                    hidden_t(i + NE, 0)
            gathered = dve.snap(layer * PER_LAYER + PER_LAYER)
            dve.wait_ge(s_gathered, gathered)
            for j in range(2):
                for b in range(NB):
                    i = NB * j + b
                    if j:
                        dve.wait_ge(s["moe"], b + 1)
                    STT(out=x[:, b, :], in0=hbuf[:, D * i:D * i + D], scalar=gate_w[:, i:i + 1], in1=x[:, b, :],
                        op0=ALU.mult, op1=ALU.add).then_inc(s["moe"], 1)

        def pool_program(pool, layer):
            G = nc.gpsimd
            TS, TT = G.tensor_scalar, G.tensor_tensor
            link = linker(pool, s["pool"])

            def scan_operands(hh):
                pool.wait_ge(s["f_ready"], hh + 1)
                if hh:
                    pool.wait_ge(s["head"], hh)
                link(TT(ht_d1, ht_f, cst("chunk_start"), ALU.mult))
                TT(ht_d0, ht_f, ht_d1, ALU.subtract).then_inc(s["f_split"], 1)

            def square(c, sn, t0, t1):
                link(TT(t0, c, c, ALU.mult))
                link(TT(t1, sn, sn, ALU.mult))
                link(TT(sn, sn, c, ALU.mult))
                link(TT(sn, sn, sn, ALU.add))
                link(TT(c, t0, t1, ALU.subtract))

            a_re, a_im = pcol("a_re"), pcol("a_im")
            pool.wait_ge(s["dt"], 1)
            tmp = [Wr[:, i, :] for i in range(4)]
            link(TT(pv_lr, a_re, pv_dt, ALU.mult))
            link(TT(pv_sin, a_im, pv_dt, ALU.mult))
            link(TS(tmp[0], pv_sin, float(1.0 / TWO_PI), ROUND, ALU.mult, ALU.add))
            link(TS(tmp[0], tmp[0], ROUND, None, ALU.subtract))
            for part in TURN:
                link(TS(tmp[1], tmp[0], -part, None, ALU.mult))
                link(TT(pv_sin, pv_sin, tmp[1], ALU.add))
            link(TS(pv_r, pv_sin, PI_DOWN, -PI_DOWN, ALU.min, ALU.max))
            link(TS(tmp[1], pv_r, 0.0, 2.0, ALU.max, ALU.mult))
            link(TT(tmp[1], pv_r, tmp[1], ALU.subtract))
            TS(pv_rc, tmp[1], float(np.pi / 2), None, ALU.add).then_inc(s["ang"], 1)
            link(TT(tmp[2], a_re, a_re, ALU.mult))
            link(TT(tmp[3], a_im, a_im, ALU.mult))
            TT(pv_den, tmp[2], tmp[3], ALU.add).then_inc(s["den"], 1)
            pool.wait_ge(s["lam"], 1)
            c1, s1, c2, s2 = Wi[:, 0, :], Wi[:, 1, :], Wi[:, 2, :], Wi[:, 3, :]
            link(G.tensor_copy(c1, pv_cos))
            link(G.tensor_copy(s1, pv_sin))
            for _ in range(3):
                square(c1, s1, c2, s2)
            tm = ring[:, 1, 3072:4096].rearrange("p (d k) -> p d k", d=DG)

            def turns(n):
                lo, hi = slice(0, n), slice(n, 2 * n)
                cb, sb_ = (a[:, :, None].broadcast_to([P, DG, n]) for a in (c1, s1))
                t = tm[:, :, 0:n]
                link(TT(cosT[:, :, hi], cosT[:, :, lo], cb, ALU.mult))
                link(TT(t, sinT[:, :, lo], sb_, ALU.mult))
                link(TT(cosT[:, :, hi], cosT[:, :, hi], t, ALU.subtract))
                link(TT(sinT[:, :, hi], sinT[:, :, lo], cb, ALU.mult))
                link(TT(t, cosT[:, :, lo], sb_, ALU.mult))
                link(TT(sinT[:, :, hi], sinT[:, :, hi], t, ALU.add))
                square(c1, s1, c2, s2)

            scan_operands(0)
            pool.wait_ge(s["pe"], 16)
            G.memset(cosT[:, :, 0], 1.0)
            link(G.memset(sinT[:, :, 0], 0.0))
            for n in (1, 2, 4):
                turns(n)
            scan_operands(1)
            turns(8)
            turns(16)
            scan_operands(2)
            turns(32)
            scan_operands(3)
            TS(flat(sinT), flat(sinT), cst("sign"), None, ALU.mult).then_inc(s["tab"], 1)
            pool.wait_ge(s["tab"], 1)
            link(TT(pv_cos, pv_cos, pv_rho, ALU.mult))
            link(TT(pv_sin, pv_sin, pv_rho, ALU.mult))
            G.memset(Wr[:, 0, :], 1.0)
            link(G.memset(Wi[:, 0, :], 0.0))
            link(G.tensor_copy(Wr[:, 1, :], pv_cos))
            link(G.tensor_copy(Wi[:, 1, :], pv_sin))
            for n in (1, 2, 4):
                lo, hi = slice(1, n + 1), slice(n + 1, 2 * n + 1)
                br, bi = (a[:, n, :][:, None, :].broadcast_to([P, n, DG]) for a in (Wr, Wi))
                t = W_t[:, 0:n, :]
                link(TT(Wr[:, hi, :], Wr[:, lo, :], br, ALU.mult))
                link(TT(t, Wi[:, lo, :], bi, ALU.mult))
                link(TT(Wr[:, hi, :], Wr[:, hi, :], t, ALU.subtract))
                link(TT(Wi[:, hi, :], Wr[:, lo, :], bi, ALU.mult))
                link(TT(t, Wi[:, lo, :], br, ALU.mult))
                link(TT(Wi[:, hi, :], Wi[:, hi, :], t, ALU.add))
            t0, t2 = W_t[:, 0, :], W_t[:, 2, :]
            link(TS(t2, pv_cos, 1.0, None, ALU.subtract))
            link(TT(pv_fr, t2, a_re, ALU.mult))
            link(TT(t0, pv_sin, a_im, ALU.mult))
            link(TT(pv_fr, pv_fr, t0, ALU.add))
            link(TT(pv_fi, pv_sin, a_re, ALU.mult))
            link(TT(t0, t2, a_im, ALU.mult))
            link(TT(pv_fi, pv_fi, t0, ALU.subtract))
            pool.wait_ge(s["inv"], 1)
            link(TT(pv_fr, pv_fr, pv_den, ALU.mult))
            link(TT(pv_fi, pv_fi, pv_den, ALU.mult))

            wait_evacuated(pool, 22)
            wait_evacuated(pool, 23)
            pool.wait_ge(s["pe"], NG)
            pool.wait_ge(s["r_done"], 5)
            for n in range(NB * HG):
                hh, b = divmod(n, NB)
                if n >= 4:
                    pool.wait_ge(s["kv"], n - 3)
                TT(v_blk[b].rearrange("p (c v) -> p c v", c=CB),
                   hv[:, b, HD * hh:HD * hh + HD][:, None, :].broadcast_to([P, CB, HD]),
                   cst("chunk_of")[:, :, None].broadcast_to([P, CB, HD]), ALU.mult).then_inc(s["vb"], 1)

            def sp(name):
                a, n = S5P[name]
                return s5[:, a:a + n]

            pool.wait_ge(s["s5p"], 16)
            pool.wait_ge(s["o_a"], 2)
            d3 = lambda ap: ap.rearrange("p (d c) -> p d c", d=DG)
            b_re, b_im, c_re, c_im = (d3(sp(n)) for n in ("b_re", "b_im", "c_re", "c_im"))
            fr, fi = (a[:, :, None].broadcast_to([P, DG, C5]) for a in (pv_fr, pv_fi))
            q0, q1, q2 = (d3(s_tmp[:, 512 * i:512 * i + 512]) for i in range(3))
            link(TT(q0, b_re, fi, ALU.mult))
            link(TT(q1, b_im, fi, ALU.mult))
            link(TT(q2, b_im, fr, ALU.mult))
            link(TT(b_re, b_re, fr, ALU.mult))
            link(TT(b_re, b_re, q1, ALU.subtract))
            link(TT(b_im, q0, q2, ALU.add))
            w2 = lambda ap: ap.rearrange("p i d -> p (i d)")
            for to, a_, b_, sub in ((A1, ("is_re", Wr), ("is_im", Wi), False), (A2, ("is_im", Wr), ("is_re", Wi), True),
                                    (A3, ("is_re", Wr), ("is_im", Wi), True), (A4, ("is_im", Wr), ("is_re", Wi), False)):
                t = s_tmp[:, 0:NPOW * DG]
                link(TS(w2(to), w2(a_[1]), cst(a_[0]), None, ALU.mult))
                link(TS(t, w2(b_[1]), cst(b_[0]), None, ALU.mult))
                link(TT(w2(to), w2(to), t, ALU.subtract if sub else ALU.add))
            link(TS(w2(A4), w2(A4), -1.0, None, ALU.mult))
            def times(to, dg, i0, n, down_, pr, pi, vr, vi, tmp_):
                for k, (pwr, val) in enumerate(((pr, vr), (pi, vi))):
                    w = pwr[:, i0:i0 + n, dg]
                    if down_:
                        w = w[:, ::-1, :]
                    w = w.rearrange("p i d -> p d i")[:, :, :, None].broadcast_to([P, G5, n, C5])
                    v = val[:, dg, :][:, :, None, :].broadcast_to([P, G5, n, C5])
                    link(TT(tmp_ if k else to, w, v, ALU.mult))
                return TT(to, to, tmp_, ALU.add)

            forward, backward = slice(0, G5), slice(G5, DG)
            t8 = s_tmp[:, 0:G5 * SC * C5].rearrange("p (d i c) -> p d i c", d=G5, i=SC)
            t9 = s_tmp[:, 0:G5 * NPOW * C5].rearrange("p (d i c) -> p d i c", d=G5, i=NPOW)
            link(times(BtT[:, forward, :, :], forward, 0, SC, True, A1, A2, b_re, b_im, t8))
            times(BtT[:, backward, :, :], backward, 0, SC, False, A1, A2, b_re, b_im, t8).then_inc(s["bc"], 1)
            pool.wait_ge(s["bc"], 1)
            times(Ct[:, forward, :, :], forward, 0, NPOW, False, A3, A4, c_re, c_im, t9).then_inc(s["bc"], 1)
            pool.wait_ge(s["qk"], NU)
            link(G.tensor_copy(rho, pv_rho8[:, :, None].broadcast_to([P, DG, NK])))
            G.memset(rho[:, :, 0], 0.0).then_inc(s["rho"], 1)

            pool.wait_ge(s["dest"], 1)
            pool.wait_ge(s_zeroed, ZEROINGS * 16)
            for i in range(2 * NB):
                G.indirect_dma_start(out=xbuf, out_offset=bass.IndirectOffsetOnAxis(ap=dest_i[:, i:i + 1], axis=0),
                                     in_=h[:, i % NB, :], in_offset=None).then_inc(s_dispatched, 16)
            pool.wait_ge(s["stored"], 1)
            for i in range(2 * NB):
                G.indirect_dma_start(out=hbuf[:, D * i:D * i + D], out_offset=None, in_=ybuf,
                                     in_offset=bass.IndirectOffsetOnAxis(ap=dest_i[:, i:i + 1], axis=0)).then_inc(s_gathered, 16)

        with nc.Fori(0, L) as layer:
            with nc.Block() as block:
                @block.sync
                def _(sp):
                    sync_program(sp, layer)

                @block.tensor
                def _(pe):
                    tensor_program(pe, layer)

                @block.scalar
                def _(act):
                    scalar_program(act, layer)

                @block.vector
                def _(dve):
                    vector_program(dve, layer)

                @block.gpsimd
                def _(pool):
                    pool_program(pool, layer)
            numbers = [q.num for q in [*s.values(), *slot, *xg_in, *y_out]]
            assert max(numbers) - min(numbers) + 1 == len(numbers)
            nc.multi_engine_barrier(list(nc.engines), sems_to_clear=range(min(numbers), max(numbers) + 1))

        with nc.Block() as block:
            @block.sync
            def _(sp):
                sp.dma_start(gB[:, :], final_g).then_inc(s_fin_g, 16)
                for b in range(NB):
                    sp.wait_ge(s_fd, b + 1)
                    sp.dma_start(out[P * b:P * b + P, :], h[:, b, :]).then_inc(s_out, 16)
                sp.wait_ge(s_out, 16 * NB)

            @block.scalar
            def _(act):
                A = nc.scalar.activation
                link = linker(act, s_fa)
                for b in range(NB):
                    link(A(h[:, b, :], x[:, b, :], ACT.Square, accum_out=small[:, 36 + b:37 + b]))
                link(A(small[:, 44:48], small[:, 36:40], ACT.Ln, bias=cst("eps"), scale=1.0 / D))
                A(small[:, 40:44], small[:, 44:48], ACT.Exp, scale=-0.5).then_inc(s_fa, 1)

            @block.vector
            def _(dve):
                dve.wait_ge(s_fin_g, 16)
                dve.wait_ge(s_fa, NB + 2)
                for b in range(NB):
                    nc.vector.scalar_tensor_tensor(out=h[:, b, :], in0=x[:, b, :], scalar=small[:, 40 + b:41 + b],
                                                   in1=gB[:, :], op0=ALU.mult, op1=ALU.mult).then_inc(s_fd, 1)


TURN = (6.28125, float(np.float32(TWO_PI - 6.28125)), float(TWO_PI - 6.28125 - np.float32(TWO_PI - 6.28125)))
PI_DOWN = 3.1415925


def constants():
    c = np.zeros((P, CONST_W), np.float32)

    def put(name, value):
        a, n = CONST[name]
        c[:, a:a + n] = value

    p = np.arange(P)[:, None]
    q = np.arange(P)[None, :]
    put("ident", p == q)
    same = (p // CH) == (q // CH)
    put("mask_f", same & (p <= q))
    put("mask_b", same & (p >= q))
    put("head_ones", (p // HD) == (q // HD))
    put("rope_swap", np.where((q % 2 == 0) & (p == q + 1), -1.0, 0.0) + np.where((q % 2 == 1) & (p == q - 1), 1.0, 0.0))
    put("half_swap", p == (q + HD) % P)
    put("before", p < q)
    put("ones", 1.0)
    pairs, grid = HD // 4, 64
    freqs = np.power(np.float32(10000.0), -np.arange(pairs, dtype=np.float32) / np.float32(pairs)).astype(np.float32)
    t = np.arange(T)
    ang = np.concatenate([(t // grid).astype(np.float32)[:, None] * freqs, (t % grid).astype(np.float32)[:, None] * freqs], 1)
    by_row = ang.astype(np.float32)[:, (np.arange(P) % HD) // 2].T
    put("cos", np.cos(by_row))
    put("sin", np.sin(by_row))
    put("chunk_start", np.where(p < HD, t[None, :] % CH == 0, t[None, :] % CH == CH - 1))
    put("chunk_of", (p // CH) == np.arange(CB)[None, :])
    put("group_id", np.arange(EG)[None, :] - BIG)
    put("expert_id", np.arange(NE)[None, :] - BIG)
    put("expert_row", np.arange(NE)[None, :] * CAP)
    put("chunk_end", np.arange(1, 8)[None, :] * CAP)
    put("over_id", np.arange(NOVER)[None, :])
    put("is_re", p < HD)
    put("is_im", p >= HD)
    put("sign", np.where(p < HD, 1.0, -1.0))
    put("eps", EPS)
    return c


def kernel(**inputs):
    import concourse.bacc as bacc
    from concourse.bass_utils import run_bass_kernel_spmd

    a = {k: np.asarray(v) for k, v in inputs.items()}
    f = np.ascontiguousarray

    w = a["w_in"].reshape(L, KT, P, 2304)
    head = lambda at, i: np.arange(at + HD * i, at + HD * i + HD)
    z = np.concatenate([np.concatenate([head(768, i), head(1024, i)]) for i in range(HG)])
    order = [z, np.concatenate([np.arange(0, 256), np.arange(1792, 2048)]), np.arange(1280, 1792),
             np.concatenate([np.arange(512, 768), np.arange(256, 512)]), np.arange(2048, 2304)]
    w_in = f(np.concatenate([w[..., o].transpose(0, 2, 1, 3).reshape(L, P, -1) for o in order], axis=2))
    w_out = f(a["w_out"].reshape(L, KT, P, 2, 512).transpose(0, 3, 2, 1, 4).reshape(L, 2, P, 4096))

    pack = np.zeros((L, P, PACK_W), np.float32)

    def put(name, value):
        at, n = PACK[name]
        pack[:, :, at:at + n] = value

    bounds = a["hgrn_lower_bounds"].reshape(L, 2, HG, HD).transpose(1, 3, 0, 2).reshape(P, L * HG)
    put("lb", bounds[None])
    put("lb_sum", np.array([[0.0] + [1.0 if 1 <= j <= l else 0.0 for j in range(1, L)] for l in range(L)])[:, None, :])
    twice = lambda v: np.concatenate([v, v], axis=1)[:, :, None]
    put("hgrn_g", twice(a["hgrn_norm_g"]))
    put("q_g", twice(a["attn_q_norm_g"]))
    put("k_g", twice(a["attn_k_norm_g"]))
    put("s5_d", a["s5_d"].reshape(L, 2, P).transpose(0, 2, 1))
    put("b_glu", a["s5_b_glu"].reshape(L, 2, P).transpose(0, 2, 1))
    put("router_b", np.concatenate([a["router_group_b"], a["router_expert_b"]], axis=1)[:, None, :])
    rw = np.concatenate([a["router_group_w"], a["router_expert_w"]], axis=2).reshape(L, KT, P, RW)
    put("router_w", rw.transpose(0, 2, 1, 3).reshape(L, P, KT * RW))
    put("w_glu", a["s5_w_glu"].reshape(L, 2, P, 256).transpose(0, 2, 1, 3).reshape(L, P, 512))

    both = lambda v: np.concatenate([v, v], axis=1)
    put("a_re", both(a["s5_a_re"].transpose(0, 3, 1, 2).reshape(L, HD, DG)))
    put("a_im", both(a["s5_a_im"].transpose(0, 3, 1, 2).reshape(L, HD, DG)))
    put("log_dt", a["s5_log_dt"].reshape(L, 1, DG))

    s5p = np.zeros((L, P, S5P_W), np.float32)

    def put5(name, value):
        at, n = S5P[name]
        s5p[:, :, at:at + n] = np.concatenate([value, value], axis=1)

    for part in ("re", "im"):
        put5("b_" + part, a["s5_b_" + part].transpose(0, 3, 1, 2, 4).reshape(L, HD, DG * C5))
        put5("c_" + part, a["s5_c_" + part].transpose(0, 4, 1, 2, 3).reshape(L, HD, DG * C5))

    rows = np.stack([a["norm1_g"], a["norm2_g"]], axis=1)
    gains = f(np.broadcast_to(rows[:, :, None, :], (L, 2, P, D)))
    final_g = f(np.broadcast_to(a["final_norm_g"][None, :], (P, D)))

    arrays = {
        "x_in": f(a["x"].reshape(T, D)), "w_in": w_in, "w_out": w_out, "pack": pack, "s5p": s5p, "gains": gains,
        "final_g": final_g, "wg": f(a["expert_w_gate"].reshape(L * NE, D, FF)),
        "wu": f(a["expert_w_up"].reshape(L * NE, D, FF)), "wd": f(a["expert_w_down"].reshape(L * NE, FF, D)),
        "consts": constants(),
    }
    nc = bacc.Bacc("TRN2", target_bir_lowering=False, num_devices=1)
    args = [nc.dram_tensor(name, v.shape, F32, kind="ExternalInput").ap() for name, v in arrays.items()]
    out = nc.dram_tensor("out", (T, D), F32, kind="ExternalOutput").ap()
    trunk(nc, *args, out)
    r = run_bass_kernel_spmd(nc, [arrays], core_ids=[0])
    return np.asarray(r.results[0]["out"]).reshape(1, T, D)
```

```python
from contextlib import ExitStack

import numpy as np

import concourse.bass as bass
from concourse import mybir

F32 = mybir.dt.float32
I32 = mybir.dt.int32
ALU = mybir.AluOpType
ACT = mybir.ActivationFunctionType
AX = mybir.AxisListType

P = 128
D = 1024
T = 512
L = 2
NB = T // P
KT = D // P
HD = 64
HG = 4
CH = 16
NCH = T // CH
CB = P // CH
QH = 8
G5 = 16
C5 = 16
DG = 2 * G5
SC = 8
NK = T // SC
NPOW = SC + 1
NE = 32
EG = 4
EPG = NE // EG
FF = 512
FT = FF // P
CAP = 64
NOVER = (2 * T) // CAP - 1
NROWS = (NE + NOVER) * CAP
RW = EG + NE
EPS = 1e-6
SCALE = HD ** -0.5
BIG = 1000.0
NEG = 1.0e30
TWO_PI = 2.0 * np.pi
ROUND = 12582912.0

def _cols(spec):
    at, out = 0, {}
    for name, n in spec:
        out[name] = (at, n)
        at += n
    return out, at


CONST, CONST_W = _cols([
    ("ident", P), ("mask_f", P), ("mask_b", P), ("head_ones", P), ("rope_swap", P), ("half_swap", P),
    ("before", P), ("ones", P), ("cos", T), ("sin", T), ("chunk_start", T), ("chunk_of", CB),
    ("group_id", EG), ("expert_id", NE), ("expert_row", NE), ("far_row", NE), ("chunk_end", 7), ("over_id", NOVER), ("slot_id", CAP),
    ("is_re", 1), ("is_im", 1), ("sign", 1), ("eps", 1)])
PACK, PACK_W = _cols([
    ("lb", L * HG), ("lb_sum", L), ("hgrn_g", 1), ("q_g", 1), ("k_g", 1), ("s5_d", 2), ("b_glu", 2),
    ("router_b", RW), ("router_w", KT * RW), ("w_glu", 2 * 256), ("a_re", DG), ("a_im", DG), ("log_dt", DG)])
S5P, S5P_W = _cols([
    ("b_re", DG * C5), ("b_im", DG * C5),
    ("c_re", DG * C5), ("c_im", DG * C5)])


def trunk(nc, x_in, w_in, w_out, pack, s5p, gains, wg, wu, wd, consts, out):
    ctx = ExitStack()
    with ctx:
        def sb(name, shape, dt=F32):
            return ctx.enter_context(nc.sbuf_tensor(name, shape, dt))

        def sem(name):
            return ctx.enter_context(nc.semaphore(name))

        u_dram = nc.dram_tensor("u_scratch", (G5, C5, SC, NK), F32).ap()
        ybuf = nc.dram_tensor("expert_rows", (NROWS, D), F32).ap()

        ring = sb("ring", [P, 6, 4096])
        hbuf = sb("hbuf", [P, 8192])
        x = sb("x", [P, NB, D])
        raw = sb("raw", [P, 9216])
        qd = sb("qd", [P, 2048])
        C = sb("consts_sb", [P, CONST_W])
        gB = sb("gain_rows", [P, D])
        pk = sb("pack_sb", [P, PACK_W])
        small = sb("small", [P, 64])
        dec4 = sb("dec4", [P, HG * NCH])
        lbs = sb("lower_bounds", [P, 24])
        over_i = sb("over_i", [P, 16], I32)
        dest_i = sb("dest_i", [P, 2 * NB], I32)
        gate_w = sb("gate_w", [P, 2 * NB])

        def cst(name):
            a, n = CONST[name]
            return C[:, a:a + n]

        def pcol(name):
            a, n = PACK[name]
            return pk[:, a:a + n]

        ident = cst("ident")
        h = hbuf[:, 0:4096].rearrange("p (b d) -> p b d", b=NB)
        hT = hbuf[:, 4096:8192].rearrange("p (k t) -> p k t", k=KT)

        def tile(buf, at, n=T):
            return buf[:, at:at + n]

        Z = [tile(raw, 512 * i) for i in range(HG)]
        hq = [tile(raw, 2048 + 512 * i) for i in range(2)]
        ak = tile(raw, 3072)
        av = raw[:, 3584:4096].rearrange("p (b c) -> p b c", b=NB)
        aq = [tile(raw, 4096 + 512 * i) for i in range(4)]
        hg = [tile(raw, 6144 + 512 * i) for i in range(2)]
        hv = raw[:, 7168:8192].rearrange("p (b c) -> p b c", b=NB)
        uT = [tile(raw, 8192 + 512 * i) for i in range(2)]
        q_dec = [tile(qd, 512 * i) for i in range(HG)]
        k_dec = [ring[:, 4, 2048 + 512 * i:2560 + 512 * i] for i in range(HG)]
        k_end = Z
        ht_e, ht_s, ht_k, ht_f, ht_d0, ht_d1, ht_F, ht_R = (ring[:, 5, 512 * i:512 * i + 512] for i in range(8))
        dec_n = small[:, 0:NCH]
        dec_s = [dec4[:, NCH * i:NCH * i + NCH] for i in range(HG)]
        two = lambda a, c: [ap.rearrange("p (v c) -> p v c", c=NCH) for ap in (a, c)]
        kv_sb = two(hbuf[:, 0:2048], ring[:, 3, 0:2048])
        dec_sb = two(hbuf[:, 2048:4096], ring[:, 3, 2048:4096])
        st_sb = [hbuf[:, 4096:6146], ring[:, 1, 0:2050]]
        v_blk = [hbuf[:, 6400:6912]] + [ring[:, 1, 2050 + 512 * i:2562 + 512 * i] for i in range(3)]
        k_endT = [hbuf[:, 7168 + 512 * i:7680 + 512 * i] for i in range(2)]
        sc_a = [ring[:, 2, 512 * i:512 * i + 512] for i in range(2)]
        sc_t = ring[:, 2, 1024:1536]
        o_sb = [ring[:, 2, 1536 + 512 * i:2048 + 512 * i] for i in range(2)]
        o_rs = [ring[:, 2, 2560 + 512 * i:3072 + 512 * i] for i in range(2)]
        rope_sq = [ring[:, 1, 512 * i:512 * i + 512] for i in range(5)]
        rope_t = ring[:, 1, 2560:3072]
        p_sb = [ring[:, 3, 512 * i:512 * i + 512] for i in range(3)]
        pT_sb = [ring[:, 3, 1536 + 512 * i:2048 + 512 * i] for i in range(3)]
        p_sum, p_max, p_bias, p_inv = ([small[:, 4 * k + i:4 * k + i + 1] for i in range(3)] for k in range(4))
        s5 = hbuf[:, 4608:4608 + S5P_W]
        Bt = ring[:, 1, :].rearrange("p (d m) -> p d m", d=DG)
        cosT = ring[:, 0, 0:2048].rearrange("p (d k) -> p d k", d=DG)
        sinT = ring[:, 0, 2048:4096].rearrange("p (d k) -> p d k", d=DG)
        BtT = ring[:, 2, :].rearrange("p (d s c) -> p d s c", d=DG, s=SC)
        T1 = ring[:, 2, 0:2048].rearrange("p (d k) -> p d k", d=DG)
        T2 = ring[:, 2, 2048:4096].rearrange("p (d k) -> p d k", d=DG)
        rho = qd[:, 0:2048].rearrange("p (d k) -> p d k", d=DG)
        M5 = ring[:, 3, 2048:4096].rearrange("p (g m) -> p g m", g=G5)
        Kf = ring[0:C5, 3, 0:2048].rearrange("p (g i c) -> p g i c", g=G5, i=SC)
        Kb = raw[0:C5, 6144:8192].rearrange("p (g i c) -> p g i c", g=G5, i=SC)
        Ct = hbuf[:, 0:4608].rearrange("p (d i c) -> p d i c", d=DG, i=NPOW)
        U5 = raw[:, 0:1024].rearrange("p (g k) -> p g k", g=G5)
        S5 = ring[:, 1, 0:DG * NK].rearrange("p (d k) -> p d k", d=DG)
        Y5 = raw[:, 1024:2048].rearrange("p (t g c) -> p t g c", t=SC, g=G5 // 2)
        s_tmp = ring[:, 1, :]
        gt = [hbuf[:, 512 * i:512 * i + 512] for i in range(4)]
        yT = [tile(raw, 512 * i) for i in range(2)]
        pw = raw[:, 6144:6144 + 2048]
        Wr = gB[:, 320:320 + NPOW * DG].rearrange("p (i d) -> p i d", i=NPOW)
        Wi = gB[:, 608:608 + NPOW * DG].rearrange("p (i d) -> p i d", i=NPOW)
        W_t = gB[:, 896:1024].rearrange("p (i d) -> p i d", i=4)
        A1 = pw[:, 1024:1312].rearrange("p (i d) -> p i d", i=NPOW)
        A2 = pw[:, 1312:1600].rearrange("p (i d) -> p i d", i=NPOW)
        A3 = pw[:, 1600:1888].rearrange("p (i d) -> p i d", i=NPOW)
        A4 = hbuf[:, 6656:6944].rearrange("p (i d) -> p i d", i=NPOW)
        ss = [gB[:, 32 * i:32 * i + 32] for i in range(10)]
        pv_den = pcol("log_dt")
        rt = [qd[:, 160 * i:160 * i + 160] for i in range(12)]
        pick = [raw[:, 256 * i:256 * i + 256].rearrange("p (b s) -> p b s", b=NB) for i in range(2)]
        pick_t = raw[:, 512:768].rearrange("p (b s) -> p b s", b=NB)
        x_rows = [raw[:, 1024 + 512 * i:1536 + 512 * i] for i in range(2)]
        rel = [small[:, NB * i:NB * i + NB] for i in range(2)]
        xT = [raw[:, 2048 + 512 * i:2560 + 512 * i].rearrange("p (k c) -> p k c", k=KT) for i in range(2)]
        e_e = tile(raw, 3072)
        e_s = tile(raw, 3584)
        hid = [tile(raw, 4096 + 512 * i) for i in range(2)]
        hidT = [raw[:, 5120 + 256 * i:5376 + 256 * i].rearrange("p (k c) -> p k c", k=FT) for i in range(2)]
        y_sb = [tile(raw, 5632 + 512 * i) for i in range(2)]

        pb = [ctx.enter_context(nc.psum_tensor(f"bank{i}", [P, 512], F32)) for i in range(8)]

        s_x = sem("x_loaded")
        s_consts = sem("constants_loaded")
        s_zero = sem("zero_rows")
        s_zeroed = sem("unused_rows_zeroed")
        s_first = sem("first_norm")
        s_fd = sem("final_rows")
        s_out = sem("out_stored")
        s_win = [sem(f"w_in{i}_loaded") for i in range(5)]
        s_gain1 = sem("norm1_or_final_gain_loaded")
        s_gathered = [sem(f"expert_rows_of_block{i}_gathered") for i in range(NB)]
        ZEROINGS = -(-(NROWS - NE * CAP) // P)
        sum_sq, rms, rstd = small[:, 36:40], small[:, 44:48], small[:, 40:44]

        def load_w_in(sp, layer, i):
            width = 4096 if i < 4 else 2048
            sp.dma_start(ring[:, i, 0:width], w_in[layer, :, 4096 * i:4096 * i + width]).then_inc(s_win[i], 16)

        with nc.Block() as block:
            @block.sync
            def _(sp):
                sp.dma_start(x[:, :, :], x_in.rearrange("(b p) d -> p b d", p=P)).then_inc(s_x, 16)
                sp.dma_start(C[:, :], consts).then_inc(s_consts, 16)
                sp.dma_start(gB[:, :], gains[0]).then_inc(s_gain1, 16)
                for i in range(5):
                    load_w_in(sp, 0, i)
                sp.wait_ge(s_zero, 1)

            @block.gpsimd
            def _(pool):
                nc.gpsimd.memset(raw[:, 8192:9216], 0.0).then_inc(s_zero, 1)

            @block.scalar
            def _(act):
                act.wait_ge(s_x, 16)
                for b in range(NB):
                    nc.scalar.activation(hbuf[:, D * b:D * b + D], x[:, b, :], ACT.Square,
                                         accum_out=sum_sq[:, b:b + 1]).then_inc(s_first, 1)
                act.wait_ge(s_first, NB)
                act.wait_ge(s_consts, 16)
                nc.scalar.activation(rms, sum_sq, ACT.Sqrt, bias=cst("eps"), scale=1.0 / D).then_inc(s_first, 1)

            @block.vector
            def _(dve):
                dve.wait_ge(s_first, NB + 1)
                nc.vector.reciprocal(rstd, rms).then_inc(s_first, 1)
        nc.all_engine_barrier()

        names = dict(
            pack="parameters loaded", gain2="norm 2 gain row loaded",
            s5p="S5 parameters loaded", h="DVE: h rows of a block",
            pe="PE: h^T and projection groups", ev_d="DVE: groups evacuated", ev_a="ACT: groups evacuated",
            dve="DVE: own chain", act="ACT: own chain", pool="Pool: own chain",
            lb_e="ACT: lower bound exp", lb="DVE: lower bounds ready",
            sig_e="ACT: exp(-z) or tanh(z/2) of a gate job", sig_r="DVE: that read", q_silu="DVE: silu(q) of a pair",
            q_copy="ACT: silu(q) copied to both halves", f_ready="DVE: forget gates of a head",
            f_split="Pool: scan operands of a head", head="DVE: decayed q, k of a head",
            r_sq="ACT: rope squares", r_y="DVE: rope gained tile", r_pe="PE: rope sums and swap",
            r_rs="ACT: rope rstd", r_done="DVE: rope tile done",
            ke_t="PE: k_end transposed", ke_e="ACT: k_end^T evacuated", hs_pe="PE: HGRN scores",
            hs_m="DVE: HGRN scores masked", vb="Pool: chunk-spread v", kv="PE: chunk k v of a block",
            kv_e="ACT: chunk k v evacuated", dec="Pool: decay rows", state="DVE: chunk states",
            ho="PE: HGRN outputs of a head", ho_s="ACT: HGRN output of a pair",
            ho_q="ACT: HGRN squares", ho_m="PE: HGRN square sums", ho_r="ACT: HGRN rstd", o_a="DVE: o_a of a pair",
            qk="PE: attention scores", mx="DVE: row maxima",
            ex="ACT: probabilities", pn="DVE: probabilities scaled", pt="PE: probabilities transposed",
            pt_e="ACT: transposed probabilities evacuated", pv="PE: attention output of a unit",
            o_b="ACT: o_b of a pair", u_out="u stored", u_in="u by chunk loaded",
            dt="ACT: S5 step sizes", ang="Pool: S5 angles", lam="ACT: S5 moduli, sines", den="Pool: S5 denominators",
            inv="DVE: S5 inverse denominators", bc="Pool: S5 Bt^T, then forward Ct", ct="DVE: S5 backward Ct", tab="Pool: S5 rotations",
            kp="PE: S5 kernels of a bank", ke="S5 kernels evacuated", kdiag="DVE: S5 kernel diagonal",
            m5="S5 chunk matrix loaded", rho="Pool: S5 decay rows", bt="PE: Bt of a bank", bt_e="ACT: odd banks of Bt evacuated",
            bt_v="DVE: even banks of Bt evacuated",
            xin="PE: S5 chunk inputs of a quarter", z="DVE: S5 quarters scanned",
            zs="PE: S5 states swapped", xs="DVE: S5 states", y5="PE: S5 outputs", y5_e="ACT: S5 outputs, first half",
            y5_v="DVE: S5 outputs, second half", yt="PE: S5 outputs feature-major", ge="DVE: gelu argument", gx="ACT: gelu tanh", z5="DVE: gelu",
            glu="PE: GLU products", glx="ACT: GLU tanh", o_c="DVE: o_c of a tile",
            wo="PE: output projection groups", res="DVE: residual added", rms2="ACT: norm 2 root mean squares",
            h2="DVE: h rows", h2t="PE: h^T tiles", h2_d="DVE: h^T evacuated", h2_a="ACT: h^T evacuated",
            rl="PE: router logits", gs="DVE: group logits less maximum", gx2="ACT: group exp",
            sel="DVE: experts selected", sx="ACT: exp of the second's difference", cnt="PE: positions and counts",
            dest="DVE: destinations", oc="DVE: selection chain",
            oh="DVE: selection matrix of a block", over="DVE: weights, overflow blocks", xp="PE: token rows of a block selected",
            xp_e="ACT: token rows evacuated", xt="PE: token rows transposed", xt_e="ACT: transposed rows evacuated",
            gu="PE: gate and up", ee="ACT: tanh(gate/2)", er="DVE: tanh(gate/2) read",
            ec="DVE: expert chain", hid="DVE: hidden rows", ht="PE: hidden transposed", ht_e="DVE: hidden^T evacuated",
            dn="PE: down", ye="ACT: expert rows evacuated", stored="ACT: every expert row stored",
            moe="DVE: MoE residual", rms3="ACT: root mean squares of the next norm")
        s = {k: sem(f"s_{k}") for k in names}
        slot = [sem(f"slot{i}") for i in range(6)]
        y_out = [sem(f"y_rows{i}_stored") for i in range(2)]

        def flat(ap):
            return ap.rearrange("p a b -> p (a b)")

        def linker(engine, semaphore):
            at = [0]

            def link(ins):
                at[0] += 1
                ins.then_inc(semaphore, 1)
                engine.wait_ge(semaphore, at[0])
            return link

        NG = KT + 18

        def wait_evacuated(engine, n):
            if n % 2 == 0:
                engine.wait_ge(s["ev_d"], n // 2 + 1)
            else:
                engine.wait_ge(s["ev_a"], n // 2 + 1)

        def weights(i):
            width = 512 if i < 4 else 256
            return ring[:, i, 0:8 * width].rearrange("p (k c) -> p k c", k=KT)

        w_o = [ring[:, 4 + i, :].rearrange("p (k c) -> p k c", k=KT) for i in range(2)]
        W_gate = [ring[:, 3 * i, :].rearrange("p (k c) -> p k c", k=KT) for i in range(2)]
        W_up = [ring[:, 3 * i + 1, :].rearrange("p (k c) -> p k c", k=KT) for i in range(2)]
        W_down = [ring[:, 3 * i + 2, :].rearrange("p (k c) -> p k c", k=FT) for i in range(2)]
        LOADS = [0, 0, 0, 0, 1, 1]
        NU = QH * NB
        target = {8: Z[0], 9: Z[1], 10: Z[2], 11: Z[3], 12: hq[0], 13: hq[1], 14: ak,
                  16: aq[0], 17: aq[1], 18: aq[2], 19: aq[3], 20: hg[0], 21: hg[1]}
        rope_x = [ak] + aq
        mixed = hq + aq + uT
        wg_f = wg.rearrange("e (p k) f -> e p (k f)", p=P)
        wu_f = wu.rearrange("e (p k) f -> e p (k f)", p=P)
        wd_f = wd.rearrange("e (p k) f -> e p (k f)", p=P)

        def evac_views(n):
            bank = pb[n % 4 if n >= KT else n]
            if n < KT:
                return hT[:, n, :], bank[:, :]
            if n == 15:
                return flat(av), bank[:, :]
            if n in (22, 23):
                q = 2 * (n - 22)
                return flat(hv[:, q:q + 2, :]), bank[:, :]
            if n >= 24:
                return (uT[n - 24].rearrange("p (t k) -> p t k", t=SC),
                        bank[:, :].rearrange("p (k t) -> p t k", t=SC))
            return target[n], bank[:, :]

        X_BANK = [(pb[4], pb[5]), (pb[0], pb[1]), (pb[2], pb[3]), (pb[4], pb[5])]
        R_BANK = ((pb[6], pb[7]), (pb[4], pb[5]))
        O_BANK, M_BANK = (pb[7], pb[4]), (pb[7], pb[5])
        S_BANK, T_BANK = (0, 1, 6), (2, 3, 7)

        def sync_program(sp, layer):
            with sp.If(layer < 1):
                for r in range(NE * CAP, NROWS, P):
                    n = min(P, NROWS - r)
                    sp.dma_start(ybuf[r:r + n], raw[0:n, 8192:9216]).then_inc(s_zeroed, 16)
            wait_evacuated(sp, 24)
            wait_evacuated(sp, 25)
            for i in range(2):
                sp.dma_start(u_dram[8 * i:8 * i + 8].rearrange("g c t k -> (g c) (t k)"), uT[i]).then_inc(s["u_out"], 16)
            sp.wait_ge(s["u_out"], 32)
            sp.wait_ge(s["ke_t"], HG)
            for t in range(SC):
                sp.dma_start(U5[C5 * t:C5 * t + C5], u_dram[:, :, t, :].rearrange("g c k -> c g k")).then_inc(s["u_in"], 16)
            sp.wait_ge(s["hs_pe"], HG)
            sp.wait_ge(s["head"], HG)
            sp.wait_ge(s["q_silu"], 4)
            for i in range(2):
                sp.dma_start(ring[:, 4 + i, :], w_out[layer, i]).then_inc(slot[4 + i], 16)
            sp.wait_ge(s["ho"], HG)
            sp.dma_start(s5, s5p[layer]).then_inc(s["s5p"], 16)
            sp.wait_ge(s["kdiag"], 1)
            for t in range(SC):
                rows = slice(C5 * t, C5 * t + C5)
                sp.dma_start(M5[rows, :, C5 * t:P].rearrange("p g (i c) -> p g i c", c=C5),
                             Kf[:, :, 0:SC - t, :]).then_inc(s["m5"], 16)
                if t:
                    sp.dma_start(M5[rows, :, 0:C5 * t].rearrange("p g (i c) -> p g i c", c=C5),
                                 Kb[:, :, SC - 1 - t:SC - 1, :]).then_inc(s["m5"], 16)
            sp.wait_ge(s["rho"], 1)
            sp.dma_start(gB[:, :], gains[layer * 2 + 1]).then_inc(s["gain2"], 16)
            sp.wait_ge(s["y5"], 1)
            first_e = sp.snap(layer * NE)
            second_e = sp.snap(layer * NE + 1)
            sp.dma_start(ring[:, 0, :], wg_f[first_e]).then_inc(slot[0], 16)
            sp.dma_start(ring[:, 1, :], wu_f[first_e]).then_inc(slot[1], 16)
            sp.dma_start(ring[:, 2, :], wd_f[first_e]).then_inc(slot[2], 16)
            sp.dma_start(ring[:, 3, :], wg_f[second_e]).then_inc(slot[3], 16)
            sp.wait_ge(s["wo"], 4 * NB)
            sp.dma_start(ring[:, 4, :], wu_f[second_e]).then_inc(slot[4], 16)
            sp.dma_start(ring[:, 5, :], wd_f[second_e]).then_inc(slot[5], 16)

            def gate_up(e, used, par):
                sp.wait_ge(s["gu"], used)
                sp.dma_start(ring[:, 3 * par, :], wg_f[e]).then_inc(slot[3 * par], 16)
                sp.dma_start(ring[:, 3 * par + 1, :], wu_f[e]).then_inc(slot[3 * par + 1], 16)

            def down(e, used, par):
                sp.wait_ge(s["dn"], used)
                sp.dma_start(ring[:, 3 * par + 2, :], wd_f[e]).then_inc(slot[3 * par + 2], 16)

            gate_up(sp.snap(layer * NE + 2), 1, 0)
            gate_up(sp.snap(layer * NE + 3), 2, 1)
            down(sp.snap(layer * NE + 2), 1, 0)
            with sp.Fori(2, NE // 2) as j:
                e = [sp.snap(layer * NE + j * 2 + i) for i in (-1, 0, 1)]
                used = [sp.snap(j * 2 + i) for i in (-2, -1, 0)]
                gate_up(e[1], used[1], 0)
                down(e[0], used[0], 1)
                gate_up(e[2], used[2], 1)
                down(e[1], used[1], 0)
            down(sp.snap(layer * NE + NE - 1), NE - 2, 1)
            next_layer = nc.s_assert_within(sp.snap(layer + 1), 0, L - 1,
                                            skip_runtime_bounds_check_because="used only where layer < L - 1")
            next_gain = sp.snap(layer * 2 + 2)
            sp.wait_ge(s["h2"], NB)
            sp.dma_start(gB[:, :], gains[next_gain]).then_inc(s_gain1, 16)
            with sp.If(layer < L - 1):
                sp.wait_ge(s["gu"], NE - 1)
                load_w_in(sp, next_layer, 0)
                load_w_in(sp, next_layer, 1)
            sp.wait_ge(s["dn"], NE)
            sp.wait_ge(s["over"], 1)
            n_over = sp.value_load(over_i[0:1, NOVER:NOVER + 1], min_val=0, max_val=NOVER)
            all_done = sp.snap(n_over + NE)
            with sp.If(n_over > 0):
                with sp.Fori(0, n_over) as i:
                    e_over = sp.value_load(over_i[0:1, bass.ds(i, 1)], min_val=0, max_val=NE - 1)
                    e = sp.snap(layer * NE + e_over)
                    used = sp.snap(i + NE)
                    sp.wait_ge(s["dn"], used)
                    sp.dma_start(ring[:, 3, :], wg_f[e]).then_inc(slot[3], 16)
                    sp.dma_start(ring[:, 4, :], wu_f[e]).then_inc(slot[4], 16)
                    sp.dma_start(ring[:, 5, :], wd_f[e]).then_inc(slot[5], 16)
            with sp.If(layer < L - 1):
                sp.wait_ge(s["dn"], all_done)
                sp.wait_ge(s["moe"], 2 * NB - 1)
                load_w_in(sp, next_layer, 2)
                load_w_in(sp, next_layer, 3)
                load_w_in(sp, next_layer, 4)

        def tensor_program(pe, layer):
            mm, tr = nc.tensor.matmul, nc.tensor.transpose

            def rope(j):
                pe.wait_ge(s["r_sq"], j + 1)
                if j >= 2:
                    pe.wait_ge(s["r_rs"], j - 1)
                    pe.wait_ge(s["r_done"], j - 1)
                mm(R_BANK[j % 2][0][:, :], cst("head_ones"), rope_sq[j], start=True, stop=True)
                pe.wait_ge(s["r_y"], j + 1)
                mm(R_BANK[j % 2][1][:, :], cst("rope_swap"), rope_x[j], start=True, stop=True).then_inc(s["r_pe"], 1)

            for b in range(NB):
                pe.wait_ge(s["h"], b + 1)
                for n in range(KT):
                    last = tr(pb[n][:, P * b:P * b + P], h[:, b, P * n:P * n + P], ident)
                    if b == NB - 1:
                        last.then_inc(s["pe"], 1)
            wait_evacuated(pe, KT - 2)
            wait_evacuated(pe, KT - 1)
            loaded = pe.snap(layer * 16 + 16)
            for n in range(KT, NG):
                i, c = (n - KT) // 4, P * ((n - KT) % 4)
                w = weights(i)
                if c == 0:
                    pe.wait_ge(s_win[i], loaded)
                if n >= KT + 4:
                    wait_evacuated(pe, n - 4)
                bank = pb[n % 4]
                if n == 15:
                    for b in range(NB):
                        for k in range(KT):
                            last = mm(bank[:, P * b:P * b + P], hT[:, k, P * b:P * b + P], w[:, k, c:c + P],
                                      start=(k == 0), stop=(k == KT - 1))
                elif n in (22, 23):
                    for half in range(2):
                        b = 2 * (n - 22) + half
                        for k in range(KT):
                            last = mm(bank[:, 256 * half:256 * half + 256], hT[:, k, P * b:P * b + P],
                                      w[:, k, 256:512], start=(k == 0), stop=(k == KT - 1))
                else:
                    for k in range(KT):
                        last = mm(bank[:, :], w[:, k, c:c + P], hT[:, k, :], start=(k == 0), stop=(k == KT - 1))
                last.then_inc(s["pe"], 1)
                for j, after in enumerate((18, 19, 21, 24, 25)):
                    if n == after:
                        rope(j)

            def hgrn_in(hh):
                pe.wait_ge(s["head"], hh + 1)
                if hh == 0:
                    wait_evacuated(pe, NG - 2)
                    wait_evacuated(pe, NG - 1)
                else:
                    pe.wait_ge(s["kv_e"], NB * hh)
                    pe.wait_ge(s["hs_m"], hh)
                for b in range(NB):
                    last = tr(pb[0][:, P * b:P * b + P], k_end[hh][:, P * b:P * b + P], ident)
                last.then_inc(s["ke_t"], 1)
                if hh == 0:
                    pe.wait_ge(s["r_done"], 4)
                    pe.wait_ge(s["r_rs"], 5)
                for b in range(NB):
                    t = slice(P * b, P * b + P)
                    mm(pb[5][:, t], k_dec[hh][0:HD, t], q_dec[hh][0:HD, t], start=True, stop=True)
                    last = mm(pb[6][:, t], k_dec[hh][HD:P, t], q_dec[hh][HD:P, t], start=True, stop=True)
                last.then_inc(s["hs_pe"], 1)
                pe.wait_ge(s["ke_e"], hh + 1)
                kT = k_endT[hh % 2]
                for b in range(NB):
                    pe.wait_ge(s["vb"], NB * hh + b + 1)
                    v = v_blk[b]
                    mm(pb[b][:, :], kT[:, P * b:P * b + P], v, start=True, stop=True).then_inc(s["kv"], 1)

            def hgrn_out(hh):
                pe.wait_ge(s["hs_m"], hh + 1)
                pe.wait_ge(s["state"], hh + 1)
                if hh == 0:
                    pe.wait_ge(s["r_done"], 5)
                out = O_BANK[hh // 2][HD * (hh % 2):HD * (hh % 2) + HD, :]
                q, st = q_dec[hh], st_sb[hh % 2]
                for b in range(NB):
                    mm(out[:, P * b:P * b + P], hv[:, b, HD * hh:HD * hh + HD], sc_a[hh % 2][:, P * b:P * b + P],
                       start=True, stop=False)
                    for c in range(CB * b, CB * b + CB):
                        t = slice(CH * c, CH * c + CH)
                        last = mm(out[:, t], st[:, c + 1:c + 2 + NCH * (HD - 1):NCH], q[:, t],
                                  start=False, stop=(c % CB == CB - 1))
                last.then_inc(s["ho"], 1)

            hgrn_in(0)
            hgrn_in(1)
            hgrn_out(0)
            hgrn_in(2)
            hgrn_out(1)
            hgrn_in(3)
            hgrn_out(2)

            def head_sums(p):
                pe.wait_ge(s["ho_q"], p + 1)
                if p == 0:
                    pe.wait_ge(s["ho_s"], 1)
                else:
                    pe.wait_ge(s["hs_m"], HG)
                mm(M_BANK[p][:, :], cst("head_ones"), o_rs[p], start=True, stop=True).then_inc(s["ho_m"], 1)

            def scores(u):
                a, b = divmod(u, NB)
                if u == 0:
                    pe.wait_ge(s["kv_e"], NB * HG)
                    pe.wait_ge(s["r_done"], 5)
                if u == 2:
                    pe.wait_ge(s["hs_m"], HG)
                if u >= 3:
                    pe.wait_ge(s["ex"], u - 2)
                r = slice(HD * (a % 2), HD * (a % 2) + HD)
                mm(pb[S_BANK[u % 3]][:, :], aq[a // 2][r, P * b:P * b + P], ak[r, :],
                   start=True, stop=True).then_inc(s["qk"], 1)

            def values(u):
                a, b = divmod(u, NB)
                pe.wait_ge(s["pt_e"], u + 1)
                pair = a // 2
                if u == 0:
                    pe.wait_ge(s["ho_s"], 2)
                if u == 2 * NB:
                    pe.wait_ge(s["ho_r"], 2)
                if u % (2 * NB) == 0 and pair >= 2:
                    pe.wait_ge(s["o_b"], pair - 1)
                r = slice(HD * (a % 2), HD * (a % 2) + HD)
                kv = a % 2
                for j in range(NB):
                    last = mm(pb[4 + pair % 2][r, P * b:P * b + P], av[:, j, HD * kv:HD * kv + HD],
                              pT_sb[u % 3][:, P * j:P * j + P], start=(j == 0), stop=(j == NB - 1))
                last.then_inc(s["pv"], 1)

            scores(0)
            head_sums(0)
            scores(1)
            hgrn_out(3)
            head_sums(1)
            for u in range(NU):
                if u + 2 < NU:
                    scores(u + 2)
                pe.wait_ge(s["pn"], u + 1)
                if u == 2:
                    pe.wait_ge(s["ho_r"], 2)
                if u >= 3:
                    pe.wait_ge(s["pt_e"], u - 2)
                for j in range(NB):
                    last = tr(pb[T_BANK[u % 3]][:, P * j:P * j + P], p_sb[u % 3][:, P * j:P * j + P], ident)
                last.then_inc(s["pt"], 1)
                if u >= 1:
                    values(u - 1)
            values(NU - 1)

            def projected(n, tiles, bank):
                b, half = divmod(n, 2)
                for k in tiles:
                    last = mm(bank[:, :], mixed[k][:, P * b:P * b + P], w_o[half][:, k, :],
                              start=(k == tiles[0]), stop=(k == tiles[-1]))
                last.then_inc(s["wo"], 1)

            def early(n):
                if n >= 2:
                    pe.wait_ge(s["res"], n - 1)
                projected(n, range(6), pb[6 + n % 2])

            pe.wait_ge(s["o_a"], 2)
            pe.wait_ge(s["o_b"], 4)
            pe.wait_ge(s["ex"], NU)
            pe.wait_ge(s["pt_e"], NU)
            pe.wait_ge(slot[4], 16)
            pe.wait_ge(slot[5], 16)
            early(0)
            early(1)

            def bt_left(q):
                if q % 2:
                    pe.wait_ge(s["bt_e"], q // 2 + 1)
                else:
                    pe.wait_ge(s["bt_v"], q // 2 + 1)

            pe.wait_ge(s["bc"], 2)
            for q in range(8):
                if q >= 6:
                    bt_left(q - 6)
                for dg in range(4 * q, 4 * q + 4):
                    last = tr(pb[q % 6][:, P * (dg % 4):P * (dg % 4) + P],
                              BtT[:, dg, :, :].rearrange("p s c -> p (s c)"), ident)
                last.then_inc(s["bt"], 1)
            pe.wait_ge(s["ct"], 1)
            for q in range(8):
                if q < 6:
                    bt_left(q + 2)
                else:
                    pe.wait_ge(s["ke"], q - 5)
                for dg in range(4 * q, 4 * q + 4):
                    zero_power, i0 = (SC - 1, 0) if dg < G5 else (0, 1)
                    last = mm(pb[(q + 2) % 6][0:C5, P * (dg % 4):P * (dg % 4) + P], BtT[:, dg, zero_power, :],
                              Ct[:, dg, i0:i0 + SC, :].rearrange("p i c -> p (i c)"), start=True, stop=True)
                last.then_inc(s["kp"], 1)
            pe.wait_ge(s["u_in"], 16 * SC)
            for q in range(4):
                if q < 3:
                    pe.wait_ge(s["ke"], 4 + 2 * q)
                else:
                    pe.wait_ge(s["z"], 1)
                for i in range(8):
                    dg = 8 * q + i
                    u = U5[:, dg % G5, :] if dg < G5 else U5[:, dg % G5, ::-1]
                    c = slice(NK * i, NK * i + NK)
                    mm(X_BANK[q][0][:, c], Bt[:, dg, :], u, start=True, stop=True)
                    mm(X_BANK[q][1][0:HD, c], Bt[:, dg, HD:P], u, start=True, stop=True)
                    last = mm(X_BANK[q][1][HD:P, c], Bt[:, dg, 0:HD], u, start=True, stop=True)
                last.then_inc(s["xin"], 1)
            early(2)
            early(3)
            for q in range(4):
                pe.wait_ge(s["z"], max(q + 1, 2))
                mm(pb[q][:, :], cst("half_swap"), flat(T2[:, 8 * q:8 * q + 8, :]),
                   start=True, stop=True).then_inc(s["zs"], 1)
            early(4)
            pe.wait_ge(s["m5"], 16 * (2 * SC - 1))
            pe.wait_ge(s["xs"], 1)
            for i in range(G5 // 2):
                for part in range(3):
                    for tile_ in range(2):
                        g = i + G5 // 2 * tile_
                        left = (U5[:, g, :], S5[:, g, :], S5[:, G5 + g, :])[part]
                        right = (M5[:, g, :], Ct[:, g, 1:NPOW, :].rearrange("p i c -> p (i c)"),
                                 Ct[:, G5 + g, 0:SC, :].rearrange("p i c -> p (i c)"))[part]
                        last = mm(pb[4 + i // 4][NK * tile_:NK * tile_ + NK, P * (i % 4):P * (i % 4) + P], left, right,
                                  start=(part == 0), stop=(part == 2))
            last.then_inc(s["y5"], 1)
            pe.wait_ge(s["y5_e"], 1)
            pe.wait_ge(s["y5_v"], 1)
            for t in range(SC):
                last = tr(pb[t // 4][:, P * (t % 4):P * (t % 4) + P], Y5[:, t, :, :].rearrange("p g c -> p (g c)"), ident)
            last.then_inc(s["yt"], 1)
            early(5)
            early(6)
            early(7)
            pe.wait_ge(s["z5"], 2)
            for m in range(2):
                for k in range(2):
                    last = mm(pb[m][:, :], pcol("w_glu")[:, 256 * k + P * m:256 * k + P * m + P], yT[k],
                              start=(k == 0), stop=(k == 1))
                last.then_inc(s["glu"], 1)
            pe.wait_ge(s["o_c"], 2)
            pe.wait_ge(s["res"], 2 * NB)
            for n in range(2 * NB):
                projected(n, range(6, KT), pb[n])

            for b in range(NB):
                pe.wait_ge(s["h2"], b + 1)
                for k in range(KT):
                    last = tr(pb[k][:, P * b:P * b + P], h[:, b, P * k:P * k + P], ident)
                    if b == NB - 1:
                        last.then_inc(s["h2t"], 1)
            for k in range(KT):
                if k == 0:
                    pe.wait_ge(s["h2_d"], 2)
                    pe.wait_ge(s["h2_a"], 2)
                elif k % 2:
                    pe.wait_ge(s["h2_a"], k // 2 + 1)
                else:
                    pe.wait_ge(s["h2_d"], k // 2 + 1)
                for b in range(NB):
                    last = mm(pb[b][:, 0:RW], hT[:, k, P * b:P * b + P], pcol("router_w")[:, RW * k:RW * k + RW],
                              start=(k == 0), stop=(k == KT - 1))
            last.then_inc(s["rl"], 1)
            pe.wait_ge(s["sel"], 1)
            chosen = rt[8][:, 0:NB * NE].rearrange("p (b e) -> p b e", b=NB)
            for b in range(NB):
                for c in range(b + 1):
                    mm(pb[1][:, NE * b:NE * b + NE], cst("before") if c == b else cst("ones"), chosen[:, c, :],
                       start=(c == 0), stop=(c == b))
            for c in range(NB):
                last = mm(pb[1][:, P:P + NE], cst("ones"), chosen[:, c, :], start=(c == 0), stop=(c == NB - 1))
            last.then_inc(s["cnt"], 1)

            def pick_rows(e, par):
                done, free = pe.snap(e + 1), (pe.snap(e - 1) if not isinstance(e, int) or e >= 2 else None)
                pe.wait_ge(s["oh"], done)
                if free is not None:
                    pe.wait_ge(s["xp_e"], free)
                for b in range(NB):
                    for half in range(2):
                        rows = h[:, b, :].rearrange("p (q k) -> p k q", k=KT)[:, 4 * half:4 * half + 4, :]
                        last = mm(pb[par][CAP * half:CAP * half + CAP, :].rearrange("p (k q) -> p k q", k=4),
                                  pick[par][:, b, :], rows, start=(b == 0), stop=(b == NB - 1))
                last.then_inc(s["xp"], 1)

            def turn(e, par):
                done, free = pe.snap(e + 1), (pe.snap(e) if not isinstance(e, int) or e >= 1 else None)
                pe.wait_ge(s["xp_e"], done)
                if free is not None:
                    pe.wait_ge(s["xt_e"], free)
                for k in range(4):
                    last = mm(pb[7][:, P * k:P * k + P], x_rows[par][:, P * k:P * k + P], ident, start=True, stop=True)
                last.then_inc(s["xt"], 1)

            def gate_up(e, par, loads):
                done, free = pe.snap(e + 1), (pe.snap(e - 1) if not isinstance(e, int) or e >= 2 else None)
                lot = [pe.snap((LOADS[3 * par + i] + loads) * 16) for i in range(2)]
                pe.wait_ge(s["xt_e"], done)
                if free is not None:
                    pe.wait_ge(s["hid"], free)
                pe.wait_ge(slot[3 * par], lot[0])
                pe.wait_ge(slot[3 * par + 1], lot[1])
                for k in range(KT):
                    mm(pb[2 + par][0:CAP, :], xT[par][:, k, :], W_gate[par][:, k, :], start=(k == 0), stop=(k == KT - 1))
                    last = mm(pb[2 + par][CAP:P, :], xT[par][:, k, :], W_up[par][:, k, :],
                              start=(k == 0), stop=(k == KT - 1))
                last.then_inc(s["gu"], 1)

            def hidden(e, par):
                done, free = pe.snap(e + 1), (pe.snap(e) if not isinstance(e, int) or e >= 1 else None)
                pe.wait_ge(s["hid"], done)
                if free is not None:
                    pe.wait_ge(s["ht_e"], free)
                pe.wait_ge(s["res"], 4 * NB)
                mm(pb[4][:, 0:CAP], hid[par][0:CAP, 0::FT], ident[0:CAP, 0:CAP], start=True, stop=True)
                for k in range(1, FT):
                    last = tr(pb[4][:, CAP * k:CAP * k + CAP], hid[par][0:CAP, k::FT], ident[0:CAP, 0:CAP])
                last.then_inc(s["ht"], 1)

            def down(e, par, loads):
                done, free = pe.snap(e + 1), (pe.snap(e - 1) if not isinstance(e, int) or e >= 2 else None)
                lot = pe.snap((LOADS[3 * par + 2] + loads) * 16)
                pe.wait_ge(s["ht_e"], done)
                if free is not None:
                    pe.wait_ge(s["ye"], free)
                pe.wait_ge(slot[3 * par + 2], lot)
                for k in range(FT):
                    mm(pb[5 + par][0:CAP, :], hidT[par][:, k, :], W_down[par][:, k, 0:512],
                       start=(k == 0), stop=(k == FT - 1))
                    last = mm(pb[5 + par][CAP:P, :], hidT[par][:, k, :], W_down[par][:, k, 512:1024],
                              start=(k == 0), stop=(k == FT - 1))
                last.then_inc(s["dn"], 1)

            pick_rows(0, 0)
            pick_rows(1, 1)
            turn(0, 0)
            gate_up(0, 0, 1)
            turn(1, 1)
            pick_rows(2, 0)

            def step(e, par, loads, turned=True, picked=True):
                gate_up(e + 1, 1 - par, loads + par)
                hidden(e, par)
                if turned:
                    turn(e + 2, par)
                down(e, par, loads)
                if picked:
                    pick_rows(e + 3, 1 - par)

            step(0, 0, 1)
            step(1, 1, 1)
            with pe.Fori(1, NE // 2 - 2) as j:
                step(j * 2, 0, j + 1)
                step(j * 2 + 1, 1, j + 1)
            step(NE - 4, 0, NE // 2 - 1)
            step(NE - 3, 1, NE // 2 - 1, picked=False)
            hidden(NE - 2, 0)
            down(NE - 2, 0, NE // 2)
            gate_up(NE - 1, 1, NE // 2)
            hidden(NE - 1, 1)
            down(NE - 1, 1, NE // 2)
            pe.wait_ge(s["ye"], NE)
            pe.wait_ge(s["over"], 1)
            n_over = pe.value_load(over_i[0:1, NOVER:NOVER + 1], min_val=0, max_val=NOVER)
            with pe.If(n_over > 0):
                with pe.Fori(0, n_over) as i:
                    pick_rows(i + NE, 1)
                    turn(i + NE, 1)
                    gate_up(i + NE, 1, i + NE // 2 + 1)
                    hidden(i + NE, 1)
                    down(i + NE, 1, i + NE // 2 + 1)

        def scalar_program(act, layer):
            A = nc.scalar.activation
            link = linker(act, s["act"])
            eps = cst("eps")
            act.dma_start(pk[:, :], pack[layer]).then_inc(s["pack"], 16)

            def evacuate(n):
                act.wait_ge(s["pe"], n + 1)
                if n == 25:
                    act.wait_ge(s_zeroed, ZEROINGS * 16)
                to, of = evac_views(n)
                A(to, of, ACT.Copy).then_inc(s["ev_a"], 1)

            for n in range(1, KT, 2):
                evacuate(n)
            act.wait_ge(s["pack"], 16)
            act.wait_ge(s["lb"], 1)
            A(lbs[:, 0:8], lbs[:, 0:8], ACT.Exp).then_inc(s["lb_e"], 1)
            act.wait_ge(s["h"], NB)
            A(pv_dt, pcol("log_dt"), ACT.Exp).then_inc(s["dt"], 1)
            act.wait_ge(s["ang"], 1)
            A(pv_rho, pv_lr, ACT.Exp)
            A(pv_rho8, pv_lr, ACT.Exp, scale=float(SC))
            A(pv_sin, pv_r, ACT.Sin)
            A(pv_cos, pv_rc, ACT.Sin).then_inc(s["lam"], 1)
            for n in range(9, 14, 2):
                evacuate(n)

            jobs = [hq[0], hq[1]] + Z + hg

            def sig_exp(j):
                n = {0: 12, 1: 13, 2: 8, 3: 9, 4: 10, 5: 11, 6: 20, 7: 21}[j]
                wait_evacuated(act, n)
                if j:
                    act.wait_ge(s["sig_r"], j)
                if 2 <= j < 6:
                    A(ht_e, jobs[j], ACT.Exp, scale=-1.0).then_inc(s["sig_e"], 1)
                else:
                    A(ht_e, jobs[j], ACT.Tanh, scale=0.5).then_inc(s["sig_e"], 1)

            def q_copies(p):
                act.wait_ge(s["q_silu"], p + 1)
                for i in range(2):
                    for half in range(2):
                        A(q_dec[2 * p + i][HD * half:HD * half + HD, :], hq[p][HD * i:HD * i + HD, :],
                          ACT.Copy, scale=0.5).then_inc(s["q_copy"], 1)

            def rope_square(j):
                wait_evacuated(act, [14, 16, 17, 18, 19][j])
                if j == 0:
                    act.wait_ge(s["pe"], 16)
                A(rope_sq[j], rope_x[j], ACT.Square).then_inc(s["r_sq"], 1)

            def rope_rstd(j):
                act.wait_ge(s["r_pe"], j + 1)
                link(A(rope_sq[j], R_BANK[j % 2][0][:, :], ACT.Ln, bias=eps, scale=1.0 / HD))
                A(rope_sq[j], rope_sq[j], ACT.Exp, scale=-0.5).then_inc(s["r_rs"], 1)

            sig_exp(0)
            sig_exp(1)
            q_copies(0)
            q_copies(1)
            evacuate(15)
            sig_exp(2)
            rope_square(0)
            evacuate(17)
            sig_exp(3)
            rope_square(1)
            rope_square(2)
            evacuate(19)
            rope_square(3)
            rope_square(4)
            sig_exp(4)
            rope_rstd(0)
            evacuate(21)
            sig_exp(5)
            rope_rstd(1)
            evacuate(23)
            rope_rstd(2)
            sig_exp(6)
            rope_rstd(3)
            evacuate(25)
            rope_rstd(4)
            sig_exp(7)

            def hgrn_copies(hh):
                act.wait_ge(s["ke_t"], hh + 1)
                if hh == 0:
                    act.wait_ge(s["pe"], NG)
                if hh >= 2:
                    act.wait_ge(s["kv"], NB * (hh - 1))
                A(k_endT[hh % 2], pb[0][:, :], ACT.Copy).then_inc(s["ke_e"], 1)
                if hh >= 2:
                    act.wait_ge(s["state"], hh - 1)
                A(dec_sb[hh % 2], dec_s[hh][:, None, :].broadcast_to([P, HD, NCH]), ACT.Copy).then_inc(s["dec"], 1)
                act.wait_ge(s["kv"], NB * hh + NB)
                for b in range(NB):
                    A(kv_sb[hh % 2][:, :, CB * b:CB * b + CB], pb[b][:, :].rearrange("p (c v) -> p v c", c=CB),
                      ACT.Copy).then_inc(s["kv_e"], 1)

            def pair_out(p):
                act.wait_ge(s["ho"], 2 * p + 2)
                A(o_rs[p], O_BANK[p][:, :], ACT.Square).then_inc(s["ho_q"], 1)
                A(o_sb[p], O_BANK[p][:, :], ACT.Copy).then_inc(s["ho_s"], 1)

            def head_rstd():
                for p in range(2):
                    act.wait_ge(s["ho_m"], p + 1)
                    ins = A(o_rs[p], M_BANK[p][:, :], ACT.Ln, bias=eps, scale=1.0 / HD)
                link(ins)
                for p in range(2):
                    A(o_rs[p], o_rs[p], ACT.Exp, scale=-0.5).then_inc(s["ho_r"], 1)

            hgrn_copies(0)
            hgrn_copies(1)
            hgrn_copies(2)
            pair_out(0)
            hgrn_copies(3)

            def probs(u):
                act.wait_ge(s["mx"], u + 1)
                if u >= 3:
                    act.wait_ge(s["pt"], u - 2)
                A(p_sb[u % 3], pb[S_BANK[u % 3]][:, :], ACT.Exp, bias=p_bias[u % 3], scale=SCALE,
                  accum_out=p_sum[u % 3]).then_inc(s["ex"], 1)

            probs(0)
            probs(1)
            pair_out(1)
            head_rstd()
            for u in range(NU):
                act.wait_ge(s["pt"], u + 1)
                if u >= 3:
                    act.wait_ge(s["pv"], u - 2)
                A(pT_sb[u % 3], pb[T_BANK[u % 3]][:, :], ACT.Copy).then_inc(s["pt_e"], 1)
                if u + 2 < NU:
                    probs(u + 2)
                if u % (2 * NB) == 1 and u > 1:
                    pair = u // (2 * NB) - 1
                    act.wait_ge(s["pv"], 2 * NB * (pair + 1))
                    A(aq[pair], pb[4 + pair % 2][:, :], ACT.Copy).then_inc(s["o_b"], 1)
            act.wait_ge(s["pv"], NU)
            A(aq[3], pb[5][:, :], ACT.Copy).then_inc(s["o_b"], 1)

            for q in range(1, 8, 2):
                act.wait_ge(s["bt"], q + 1)
                A(flat(Bt[:, 4 * q:4 * q + 4, :]), pb[q % 6][:, :], ACT.Copy).then_inc(s["bt_e"], 1)
            for q in range(8):
                act.wait_ge(s["kp"], q + 1)
                to = (Kf if q < 4 else Kb)[:, 4 * (q % 4):4 * (q % 4) + 4, :, :].rearrange("p g i c -> p (g i c)")
                A(to, pb[(q + 2) % 6][0:C5, :], ACT.Copy).then_inc(s["ke"], 1)
            act.wait_ge(s["y5"], 1)
            A(Y5[:, :, 0:4, :].rearrange("p t g c -> p g t c"),
              pb[4][:, :].rearrange("p (g t c) -> p g t c", g=4, t=SC), ACT.Copy).then_inc(s["y5_e"], 1)
            for i in range(2):
                act.wait_ge(s["ge"], i + 1)
                A(gt[i], gt[i], ACT.Tanh, scale=float(np.sqrt(2.0 / np.pi))).then_inc(s["gx"], 1)
            for i in range(2):
                act.wait_ge(s["glu"], i + 1)
                A(gt[i], pb[i][:, :], ACT.Tanh, scale=0.25, bias=small[:, 56 + i:57 + i]).then_inc(s["glx"], 1)

            A(small[:, 63:64], eps, ACT.Sqrt)
            for b in range(NB):
                act.wait_ge(s["res"], 2 * NB + 2 * b + 2)
                ins = A(h[:, b, :], x[:, b, :], ACT.Square, accum_out=sum_sq[:, b:b + 1])
            link(ins)
            A(rms, sum_sq, ACT.Sqrt, bias=eps, scale=1.0 / D).then_inc(s["rms2"], 1)
            for k in range(1, KT, 2):
                act.wait_ge(s["h2t"], k + 1)
                A(hT[:, k, :], pb[k][:, :], ACT.Copy).then_inc(s["h2_a"], 1)
            act.wait_ge(s["gs"], 1)
            A(rt[1][:, 0:16], rt[1][:, 0:16], ACT.Exp).then_inc(s["gx2"], 1)
            act.wait_ge(s["sel"], 1)
            A(small[:, 32:36], small[:, 28:32], ACT.Exp).then_inc(s["sx"], 1)

            def rows_in(e, par):
                done, free = act.snap(e + 1), (act.snap(e - 1) if not isinstance(e, int) or e >= 2 else None)
                act.wait_ge(s["xp"], done)
                if free is not None:
                    act.wait_ge(s["xt"], free)
                A(x_rows[par], pb[par][:, :], ACT.Copy).then_inc(s["xp_e"], 1)

            def turned(e, par):
                done, free = act.snap(e + 1), (act.snap(e - 1) if not isinstance(e, int) or e >= 2 else None)
                act.wait_ge(s["xt"], done)
                if free is not None:
                    act.wait_ge(s["gu"], free)
                A(xT[par].rearrange("p (h k) c -> p k h c", h=2), pb[7][:, :].rearrange("p (k h c) -> p k h c", k=4, h=2),
                  ACT.Copy).then_inc(s["xt_e"], 1)

            def gate_exp(e, par):
                done, free = act.snap(e + 1), (act.snap(e) if not isinstance(e, int) or e >= 1 else None)
                act.wait_ge(s["gu"], done)
                if free is not None:
                    act.wait_ge(s["er"], free)
                A(e_e[0:CAP, :], pb[2 + par][0:CAP, :], ACT.Tanh, scale=0.5).then_inc(s["ee"], 1)

            def rows(e, par, before):
                done, stored = act.snap(e + 1), act.snap(before * 32)
                row = act.snap(e * CAP)
                act.wait_ge(s["dn"], done)
                act.wait_ge(y_out[par], stored)
                A(y_sb[par], pb[5 + par][:, :], ACT.Copy, scale=0.5).then_inc(s["ye"], 1)
                act.wait_ge(s["ye"], done)
                for n in range(2):
                    act.dma_start(ybuf[bass.ds(row, CAP), 512 * n:512 * n + 512],
                                  y_sb[par][CAP * n:CAP * n + CAP, :]).then_inc(y_out[par], 16)

            rows_in(0, 0)
            rows_in(1, 1)
            turned(0, 0)
            gate_exp(0, 0)
            turned(1, 1)
            rows_in(2, 0)

            def step(e, par, before, more=True):
                gate_exp(e + 1, 1 - par)
                turned(e + 2, par)
                rows(e, par, before)
                if more:
                    rows_in(e + 3, 1 - par)

            step(0, 0, 0)
            step(1, 1, 0)
            with act.Fori(1, NE // 2 - 2) as j:
                step(j * 2, 0, j)
                step(j * 2 + 1, 1, j)
            step(NE - 4, 0, NE // 2 - 2)
            step(NE - 3, 1, NE // 2 - 2, more=False)
            rows(NE - 2, 0, NE // 2 - 1)
            gate_exp(NE - 1, 1)
            rows(NE - 1, 1, NE // 2 - 1)
            act.wait_ge(s["over"], 1)
            n_over = act.value_load(over_i[0:1, NOVER:NOVER + 1], min_val=0, max_val=NOVER)
            all_odd = act.snap((n_over + NE // 2) * 32)
            with act.If(n_over > 0):
                with act.Fori(0, n_over) as i:
                    rows_in(i + NE, 1)
                    turned(i + NE, 1)
                    gate_exp(i + NE, 1)
                    rows(i + NE, 1, i + NE // 2)
            act.wait_ge(y_out[0], 32 * (NE // 2))
            act.wait_ge(y_out[1], all_odd)
            A(small[:, 63:64], eps, ACT.Sqrt).then_inc(s["stored"], 1)
            for b in range(NB):
                act.wait_ge(s["moe"], 2 * b + 2)
                ins = A(hbuf[:, D * b:D * b + D], x[:, b, :], ACT.Square, accum_out=sum_sq[:, b:b + 1])
            link(ins)
            A(rms, sum_sq, ACT.Sqrt, bias=eps, scale=1.0 / D).then_inc(s["rms3"], 1)

        (pv_dt, pv_lr, pv_r, pv_rc, pv_rho, pv_rho8, pv_sin, pv_cos, pv_fr, pv_fi) = ss

        def vector_program(dve, layer):
            V = nc.vector
            TS, TT, STT = V.tensor_scalar, V.tensor_tensor, V.scalar_tensor_tensor
            link = linker(dve, s["dve"])

            def h_rows(done):
                for b in range(NB):
                    STT(out=h[:, b, :], in0=x[:, b, :], scalar=rstd[:, b:b + 1], in1=gB[:, :],
                        op0=ALU.mult, op1=ALU.mult).then_inc(done, 1)

            def evacuate(n):
                dve.wait_ge(s["pe"], n + 1)
                if n == 24:
                    dve.wait_ge(s_zeroed, ZEROINGS * 16)
                to, of = evac_views(n)
                V.tensor_copy(to, of).then_inc(s["ev_d"], 1)

            gain = dve.snap(layer * 16 + 16)
            dve.wait_ge(s_gain1, gain)
            h_rows(s["h"])
            for n in range(0, KT, 2):
                evacuate(n)
            dve.wait_ge(s["pack"], 16)
            lb = pcol("lb").rearrange("p (l h) -> p l h", l=L)
            link(TT(lbs[:, 8:12], lb[:, 0, :], lb[:, 1, :], ALU.max))
            for j in range(L):
                ins = TT(lbs[:, 4 * j:4 * j + 4], lb[:, j, :], lbs[:, 8:12], ALU.subtract)
            ins.then_inc(s["lb"], 1)
            dve.wait_ge(s["lb_e"], 1)
            link(TT(lbs[:, 8:12], lbs[:, 0:4], lbs[:, 4:8], ALU.add))
            link(V.reciprocal(lbs[:, 8:12], lbs[:, 8:12]))
            ws = pcol("lb_sum")
            link(TS(lbs[:, 12:16], lbs[:, 0:4], ws[:, 0:1], None, ALU.mult))
            link(STT(out=lbs[:, 12:16], in0=lbs[:, 4:8], scalar=ws[:, 1:2], in1=lbs[:, 12:16], op0=ALU.mult, op1=ALU.add))
            link(TT(lbs[:, 12:16], lbs[:, 12:16], lbs[:, 8:12], ALU.mult))
            link(TS(lbs[:, 16:20], lbs[:, 12:16], -1.0, 1.0, ALU.mult, ALU.add))
            link(TS(small[:, 56:58], pcol("b_glu"), 0.5, None, ALU.mult))
            evacuate(8)
            evacuate(10)
            dve.wait_ge(s["den"], 1)
            V.reciprocal(pv_den, pv_den).then_inc(s["inv"], 1)
            evacuate(12)

            def sigmoid(j):
                dve.wait_ge(s["sig_e"], j + 1)
                link(TS(ht_s, ht_e, 1.0, None, ALU.add))
                link(V.reciprocal(ht_s, ht_s))

            def silu(j, z, count):
                dve.wait_ge(s["sig_e"], j + 1)
                STT(out=z, in0=ht_e, scalar=1.0, in1=z, op0=ALU.add, op1=ALU.mult).then_inc(s["q_silu"], 1)
                dve.wait_ge(s["q_silu"], count)
                V.memset(small[:, 60:61], 0.0).then_inc(s["sig_r"], 1)

            def gate_chain(hh):
                one_less = lbs[:, 16 + hh:17 + hh]
                bound = lbs[:, 12 + hh:13 + hh]
                dve.wait_ge(s["sig_e"], 3 + hh)
                link(TS(ht_e, ht_e, 1.0e30, None, ALU.min))
                sigmoid(2 + hh)
                if hh:
                    dve.wait_ge(s["f_split"], hh)
                link(TS(ht_f, ht_s, one_less, bound, ALU.mult, ALU.add))
                V.memset(small[:, 61:62], 0.0).then_inc(s["f_ready"], 1)
                link(STT(out=ht_k, in0=ht_e, scalar=one_less, in1=ht_s, op0=ALU.mult, op1=ALU.mult))
                V.memset(small[:, 60:61], 0.0).then_inc(s["sig_r"], 1)
                dve.wait_ge(s["f_split"], hh + 1)
                V.tensor_tensor_scan(out=ht_F[0:HD, :], data0=ht_d0[0:HD, :], data1=ht_d1[0:HD, :], initial=0.0,
                                     op0=ALU.mult, op1=ALU.add)
                link(V.tensor_tensor_scan(out=ht_F[HD:P, ::-1], data0=ht_d0[HD:P, ::-1], data1=ht_d1[HD:P, ::-1],
                                          initial=0.0, op0=ALU.mult, op1=ALU.add))
                V.tensor_copy(dec_n[0:HD, :], ht_F[0:HD, CH - 1::CH])
                V.tensor_copy(dec_n[HD:P, :], ht_F[HD:P, 0::CH])
                V.tensor_copy(dec_s[hh][0:HD, :], ht_F[0:HD, CH - 1::CH])
                V.tensor_copy(dec_s[hh][HD:P, :], ht_F[HD:P, 0::CH])
                link(V.reciprocal(ht_R, ht_F))
                V.memset(dec_s[hh][:, 0:1], 0.0)
                V.memset(dec_s[hh][:, NCH - 1:NCH], 0.0)
                V.memset(dec_n[0:HD, NCH - 1:NCH], 0.0)
                link(V.memset(dec_n[HD:P, 0:1], 0.0))
                if hh == 0:
                    dve.wait_ge(s["pe"], KT + 1)
                link(TT(k_dec[hh], ht_k, ht_R, ALU.mult))
                TT(k_end[hh].rearrange("p (c t) -> p c t", t=CH), k_dec[hh].rearrange("p (c t) -> p c t", t=CH),
                   dec_n[:, :, None].broadcast_to([P, NCH, CH]), ALU.mult)
                dve.wait_ge(s["q_copy"], 8)
                TT(q_dec[hh], q_dec[hh], ht_F, ALU.mult).then_inc(s["head"], 1)
                dve.wait_ge(s["head"], hh + 1)

            def rope_gain(j):
                dve.wait_ge(s["r_sq"], j + 1)
                TS(rope_x[j], rope_x[j], pcol("k_g" if j == 0 else "q_g"), None, ALU.mult).then_inc(s["r_y"], 1)

            def rope_turn(j):
                dve.wait_ge(s["r_pe"], j + 1)
                TT(rope_t, R_BANK[j % 2][1][:, :], cst("sin"), ALU.mult)
                link(TT(rope_x[j], rope_x[j], cst("cos"), ALU.mult))
                link(TT(rope_x[j], rope_x[j], rope_t, ALU.add))
                dve.wait_ge(s["r_rs"], j + 1)
                TT(rope_x[j], rope_x[j], rope_sq[j], ALU.mult).then_inc(s["r_done"], 1)
                dve.wait_ge(s["r_done"], j + 1)

            silu(0, hq[0], 1)
            silu(1, hq[1], 2)
            evacuate(14)
            gate_chain(0)
            evacuate(16)
            rope_gain(0)
            rope_gain(1)
            gate_chain(1)
            evacuate(18)
            rope_gain(2)
            rope_gain(3)
            rope_turn(0)
            gate_chain(2)
            evacuate(20)
            rope_gain(4)
            rope_turn(1)
            gate_chain(3)
            evacuate(22)
            rope_turn(2)
            evacuate(24)
            silu(6, hg[0], 3)
            rope_turn(3)
            rope_turn(4)
            silu(7, hg[1], 4)

            def masked_scores(hh):
                dve.wait_ge(s["hs_pe"], hh + 1)
                if hh >= 2:
                    dve.wait_ge(s["ho"], hh - 1)
                if hh == 0:
                    dve.wait_ge(s["pe"], NG)
                mask = [cst(m)[:, None, :].broadcast_to([P, NB, P]) for m in ("mask_f", "mask_b")]
                b4 = lambda ap: ap.rearrange("p (b t) -> p b t", b=NB)
                TT(b4(sc_t), b4(pb[5][:, :]), mask[0], ALU.mult)
                link(TT(b4(sc_a[hh % 2]), b4(pb[6][:, :]), mask[1], ALU.mult))
                TT(sc_a[hh % 2], sc_a[hh % 2], sc_t, ALU.add).then_inc(s["hs_m"], 1)
                dve.wait_ge(s["hs_m"], hh + 1)

            def states(hh):
                dve.wait_ge(s["kv_e"], NB * hh + NB)
                dve.wait_ge(s["dec"], hh + 1)
                if hh >= 2:
                    dve.wait_ge(s["ho"], hh - 1)
                i = hh % 2
                if hh < 2:
                    V.memset(st_sb[i][0:HD, 0:2], 0.0)
                    V.memset(st_sb[i][HD:P, NCH * HD:NCH * HD + 2], 0.0)
                n, dec, kv = NCH * HD, flat(dec_sb[i]), flat(kv_sb[i])
                V.tensor_tensor_scan(out=st_sb[i][0:HD, 2:n + 2], data0=dec[0:HD, :], data1=kv[0:HD, :], initial=0.0,
                                     op0=ALU.mult, op1=ALU.add)
                V.tensor_tensor_scan(out=st_sb[i][HD:P, n - 1::-1], data0=dec[HD:P, ::-1], data1=kv[HD:P, ::-1],
                                     initial=0.0, op0=ALU.mult, op1=ALU.add).then_inc(s["state"], 1)

            masked_scores(0)
            states(0)
            masked_scores(1)
            states(1)
            masked_scores(2)
            states(2)
            masked_scores(3)
            states(3)

            def row_max(u):
                dve.wait_ge(s["qk"], u + 1)
                if u >= 3:
                    dve.wait_ge(s["ex"], u - 2)
                link(V.reduce_max(p_max[u % 3], pb[S_BANK[u % 3]][:, :], AX.X))
                TS(p_bias[u % 3], p_max[u % 3], -SCALE, None, ALU.mult).then_inc(s["mx"], 1)

            def head_norm(p):
                dve.wait_ge(s["ho_r"], p + 1)
                link(STT(out=o_sb[p], in0=o_sb[p], scalar=pcol("hgrn_g"), in1=o_rs[p], op0=ALU.mult, op1=ALU.mult))
                STT(out=hq[p], in0=o_sb[p], scalar=0.5, in1=hg[p], op0=ALU.mult, op1=ALU.mult).then_inc(s["o_a"], 1)

            row_max(0)
            row_max(1)
            for u in range(NU):
                dve.wait_ge(s["ex"], u + 1)
                link(V.reciprocal(p_inv[u % 3], p_sum[u % 3]))
                TS(p_sb[u % 3], p_sb[u % 3], p_inv[u % 3], None, ALU.mult).then_inc(s["pn"], 1)
                if u + 2 < NU:
                    row_max(u + 2)
                if u in (2, 3):
                    head_norm(u - 2)

            def residual(n, bank, done):
                b, half = divmod(n, 2)
                dve.wait_ge(s["wo"], done)
                xs = x[:, b, 512 * half:512 * half + 512]
                TT(xs, xs, bank[:, :], ALU.add).then_inc(s["res"], 1)

            def early(n):
                residual(n, pb[6 + n % 2], n + 1)

            dve.wait_ge(s["pv"], NU)
            dve.wait_ge(s["bc"], 1)
            back = slice(G5, DG)
            ct_b = Ct[:, back, :, :]
            ct_t = ring[:, 3, 0:G5 * NPOW * C5].rearrange("p (d i c) -> p d i c", d=G5, i=NPOW)
            c_re, c_im = (s5[:, S5P[n][0]:S5P[n][0] + DG * C5].rearrange("p (d c) -> p d c", d=DG) for n in ("c_re", "c_im"))

            def power(w):
                return w[:, ::-1, back].rearrange("p i d -> p d i")[:, :, :, None].broadcast_to([P, G5, NPOW, C5])

            def value(v):
                return v[:, back, :][:, :, None, :].broadcast_to([P, G5, NPOW, C5])

            TT(ct_b, power(A3), value(c_re), ALU.mult)
            link(TT(ct_t, power(A4), value(c_im), ALU.mult))
            TT(ct_b, ct_b, ct_t, ALU.add).then_inc(s["ct"], 1)
            early(0)
            early(1)
            for q in range(0, 8, 2):
                dve.wait_ge(s["bt"], q + 1)
                V.tensor_copy(flat(Bt[:, 4 * q:4 * q + 4, :]), pb[q % 6][:, :]).then_inc(s["bt_v"], 1)
            dve.wait_ge(s["kp"], 8)
            dve.wait_ge(s["tab"], 1)
            for q in range(4):
                dve.wait_ge(s["xin"], q + 1)
                r = slice(8 * q, 8 * q + 8)
                a, b = (bank[:, :].rearrange("p (d k) -> p d k", d=8) for bank in X_BANK[q])
                TT(T1[:, r, :], a, cosT[:, r, :], ALU.mult)
                link(TT(T2[:, r, :], b, sinT[:, r, :], ALU.mult))
                link(TT(T1[:, r, :], T1[:, r, :], T2[:, r, :], ALU.add))
                if q == 0:
                    dve.wait_ge(s["rho"], 1)
                V.tensor_tensor_scan(out=flat(T2[:, r, :]), data0=flat(rho[:, r, :]), data1=flat(T1[:, r, :]), initial=0.0,
                                     op0=ALU.mult, op1=ALU.add).then_inc(s["z"], 1)
                if q == 0:
                    dve.wait_ge(s["ke"], 8)
                    diag_f, diag_b = Kf[:, :, 0, :], Kb[:, :, SC - 1, :]
                    TT(diag_f, diag_f, diag_b, ALU.add).then_inc(s["kdiag"], 1)
                dve.wait_ge(s["z"], q + 1)
                link(TT(T1[:, r, :], T2[:, r, :], cosT[:, r, :], ALU.mult))
            V.memset(S5[:, 0:G5, 0], 0.0)
            V.memset(S5[:, G5:DG, NK - 1], 0.0)
            early(2)
            early(3)
            for q in range(4):
                r = slice(8 * q, 8 * q + 8)
                dve.wait_ge(s["zs"], q + 1)
                link(TT(T2[:, r, :], pb[q][:, :].rearrange("p (d k) -> p d k", d=8), sinT[:, r, :], ALU.mult))
                to = S5[:, r, 1:NK] if q < 2 else S5[:, r, NK - 2::-1]
                ins = TT(to, T1[:, r, 0:NK - 1], T2[:, r, 0:NK - 1], ALU.subtract)
            ins.then_inc(s["xs"], 1)
            early(4)
            dve.wait_ge(s["y5"], 1)
            V.tensor_copy(Y5[:, :, 4:8, :].rearrange("p t g c -> p g t c"),
                          pb[5][:, :].rearrange("p (g t c) -> p g t c", g=4, t=SC)).then_inc(s["y5_v"], 1)
            dve.wait_ge(s["yt"], 1)
            for m in range(2):
                z, t = yT[m], gt[m]
                for half in range(2):
                    w = slice(256 * half, 256 * half + 256)
                    y = pb[half][:, :].rearrange("p (t i k) -> p t i k", t=4, i=2)[:, :, m, :]
                    t3 = lambda ap: ap[:, w].rearrange("p (t k) -> p t k", t=4)
                    ins = STT(out=t3(z), in0=t3(uT[m]), scalar=pcol("s5_d")[:, m:m + 1], in1=y, op0=ALU.mult, op1=ALU.add)
                link(ins)
                link(TT(t, z, z, ALU.mult))
                link(TS(t, t, 0.044715, 1.0, ALU.mult, ALU.add))
                TT(t, t, z, ALU.mult).then_inc(s["ge"], 1)
            early(5)
            for m in range(2):
                dve.wait_ge(s["gx"], m + 1)
                STT(out=yT[m], in0=gt[m], scalar=1.0, in1=yT[m], op0=ALU.add, op1=ALU.mult).then_inc(s["z5"], 1)
            early(6)
            early(7)
            for m in range(2):
                z, t, r = yT[m], gt[m], gt[2 + m]
                dve.wait_ge(s["glx"], m + 1)
                dve.wait_ge(s["z5"], 2)
                link(TS(r, t, 0.25, 0.25, ALU.mult, ALU.add))
                TT(uT[m].rearrange("p (k t) -> p t k", t=SC), z.rearrange("p (t k) -> p t k", t=SC),
                   r.rearrange("p (t k) -> p t k", t=SC), ALU.mult).then_inc(s["o_c"], 1)
            for n in range(2 * NB):
                residual(n, pb[n], 2 * NB + n + 1)
            dve.wait_ge(s["gain2"], 16)
            dve.wait_ge(s["rms2"], 1)
            link(V.reciprocal(rstd, rms))
            h_rows(s["h2"])
            for k in range(0, KT, 2):
                dve.wait_ge(s["h2t"], k + 1)
                V.tensor_copy(hT[:, k, :], pb[k][:, :]).then_inc(s["h2_d"], 1)

            def v3(i, n):
                return rt[i][:, 0:NB * n].rearrange("p (b e) -> p b e", b=NB)

            def bc(ap, n):
                return ap[:, :, None].broadcast_to([P, NB, n])

            def per_block(ap, n):
                return ap[:, None, :].broadcast_to([P, NB, n])

            logits = v3(0, RW)
            dve.wait_ge(s["rl"], 1)
            for b in range(NB):
                ins = TT(logits[:, b, :], pb[b][:, 0:RW], pcol("router_b"), ALU.add)
            link(ins)
            g_log, e_log = logits[:, :, 0:EG], logits[:, :, EG:RW]
            g_rel, g_hot, e_in, hot1, hot2, e_tmp = v3(1, EG), v3(2, EG), v3(3, NE), v3(4, NE), v3(5, NE), v3(6, NE)
            chosen, e_msk = v3(8, NE), v3(7, NE)
            col = [rt[9][:, 4 * i:4 * i + 4] for i in range(10)]

            def first_of(hot, values, top, ids, n):
                link(TT(hot, values, bc(top, n), ALU.is_equal))
                link(TT(hot, hot, per_block(ids, n), ALU.mult))
                link(V.tensor_reduce(out=col[9], in_=hot, axis=AX.X, op=ALU.min))
                link(TT(hot, per_block(ids, n), bc(col[9], n), ALU.is_equal))

            link(V.reduce_max(col[0], g_log, AX.X))
            TT(g_rel, g_log, bc(col[0], EG), ALU.subtract).then_inc(s["gs"], 1)
            first_of(g_hot, g_log, col[0], cst("group_id"), EG)
            link(TS(rt[2][:, 0:NB * EG], rt[2][:, 0:NB * EG], 1.0, NEG, ALU.subtract, ALU.mult))
            grp = lambda ap: ap.rearrange("p b (g e) -> p b g e", g=EG)
            link(TT(grp(e_in), grp(e_log), g_hot[:, :, :, None].broadcast_to([P, NB, EG, EPG]), ALU.add))
            link(V.reduce_max(col[1], e_in, AX.X))
            first_of(hot1, e_in, col[1], cst("expert_id"), NE)
            link(STT(out=rt[7][:, 0:NB * NE], in0=rt[4][:, 0:NB * NE], scalar=-2.0 * NEG, in1=rt[3][:, 0:NB * NE],
                     op0=ALU.mult, op1=ALU.add))
            link(V.reduce_max(col[2], e_msk, AX.X))
            first_of(hot2, e_msk, col[2], cst("expert_id"), NE)
            link(TT(chosen, hot1, hot2, ALU.add))
            TT(small[:, 28:32], col[2], col[1], ALU.subtract).then_inc(s["sel"], 1)
            dve.wait_ge(s["cnt"], 1)
            pos = pb[1][:, 0:NB * NE].rearrange("p (b e) -> p b e", b=NB)
            cnt = pb[1][:, P:P + NE]
            far, near, mine = v3(7, NE), v3(6, NE), v3(3, NE)
            ext, run, base = rt[10][:, 32:64], rt[10][:, 64:96], rt[10][:, 96:128]
            many = qd[:, 1760:1760 + 7 * NE].rearrange("p (e m) -> p e m", m=7)
            TT(near, pos, per_block(cst("expert_row"), NE), ALU.add)
            link(TT(many, cnt[:, :, None].broadcast_to([P, NE, 7]), cst("chunk_end")[:, None, :].broadcast_to([P, NE, 7]),
                    ALU.is_gt))
            link(V.tensor_reduce(out=ext, in_=many, axis=AX.X, op=ALU.add))
            link(V.tensor_tensor_scan(out=run, data0=cst("ones")[:, 0:NE], data1=ext, initial=0.0,
                                      op0=ALU.mult, op1=ALU.add))
            link(TT(base, run, ext, ALU.subtract))
            link(STT(out=base, in0=base, scalar=float(CAP), in1=cst("far_row"), op0=ALU.mult, op1=ALU.add))
            link(STT(out=far, in0=pos, scalar=float(CAP), in1=per_block(base, NE), op0=ALU.is_ge, op1=ALU.mult))
            link(TT(far, far, near, ALU.add))
            for j, hot in enumerate((hot1, hot2)):
                link(TT(mine, far, hot, ALU.mult))
                link(V.tensor_reduce(out=col[5 + j], in_=mine, axis=AX.X, op=ALU.add))
                ins = TS(rel[j], col[5 + j], float(CAP), None, ALU.add)
            link(ins)

            def selection(e, par):
                done, free = dve.snap(e + 1), (dve.snap(e - 1) if not isinstance(e, int) or e >= 2 else None)
                steps = [dve.snap(e * 2 + 1), dve.snap(e * 2 + 2)]
                if free is not None:
                    dve.wait_ge(s["xp"], free)
                    dve.wait_ge(s["oh"], dve.snap(e))
                TS(small[:, 0:2 * NB], small[:, 0:2 * NB], -float(CAP), None, ALU.add).then_inc(s["oc"], 1)
                dve.wait_ge(s["oc"], steps[0])
                slots = cst("slot_id")[:, None, :].broadcast_to([P, NB, CAP])
                TT(pick[par], slots, rel[0][:, :, None].broadcast_to([P, NB, CAP]), ALU.is_equal)
                TT(pick_t, slots, rel[1][:, :, None].broadcast_to([P, NB, CAP]), ALU.is_equal).then_inc(s["oc"], 1)
                dve.wait_ge(s["oc"], steps[1])
                TT(pick[par], pick[par], pick_t, ALU.add).then_inc(s["oh"], 1)

            selection(0, 0)
            selection(1, 1)
            for j in range(2):
                ins = V.tensor_copy(dest_i[:, NB * j:NB * j + NB], col[5 + j])
            ins.then_inc(s["dest"], 1)
            dve.wait_ge(s["gx2"], 1)
            link(V.tensor_reduce(out=col[3], in_=g_rel, axis=AX.X, op=ALU.add))
            link(V.reciprocal(col[3], col[3]))
            dve.wait_ge(s["sx"], 1)
            link(TS(col[4], small[:, 32:36], 1.0, None, ALU.add))
            link(V.reciprocal(col[4], col[4]))
            link(TT(gate_w[:, 0:NB], col[4], col[3], ALU.mult))
            link(TT(gate_w[:, NB:2 * NB], gate_w[:, 0:NB], small[:, 32:36], ALU.mult))
            wide = hbuf[:, 4096:4096 + NOVER * NE].rearrange("p (i e) -> p i e", i=NOVER)
            link(TT(wide, run[:, None, :].broadcast_to([P, NOVER, NE]),
                    cst("over_id")[:, :, None].broadcast_to([P, NOVER, NE]), ALU.is_le))
            link(V.tensor_reduce(out=rt[9][:, 100:100 + NOVER], in_=wide, axis=AX.X, op=ALU.add))
            link(TS(rt[9][:, 100:100 + NOVER], rt[9][:, 100:100 + NOVER], float(NE - 1), None, ALU.min))
            link(V.tensor_copy(over_i[:, 0:NOVER], rt[9][:, 100:100 + NOVER]))
            V.tensor_copy(over_i[:, NOVER:NOVER + 1], run[:, NE - 1:NE]).then_inc(s["over"], 1)

            def hidden_rows(e, par):
                done, free = dve.snap(e + 1), (dve.snap(e - 1) if not isinstance(e, int) or e >= 2 else None)
                dve.wait_ge(s["ee"], done)
                if free is not None:
                    dve.wait_ge(s["ht"], free)
                top, bottom = pb[2 + par][0:CAP, :], pb[2 + par][CAP:P, :]
                STT(out=e_s[0:CAP, :], in0=e_e[0:CAP, :], scalar=1.0, in1=top, op0=ALU.add, op1=ALU.mult).then_inc(s["ec"], 1)
                dve.wait_ge(s["ec"], done)
                V.memset(small[:, 62:63], 0.0).then_inc(s["er"], 1)
                TT(hid[par][0:CAP, :], e_s[0:CAP, :], bottom, ALU.mult).then_inc(s["hid"], 1)

            def hidden_t(e, par):
                done, free = dve.snap(e + 1), (dve.snap(e - 1) if not isinstance(e, int) or e >= 2 else None)
                dve.wait_ge(s["ht"], done)
                if free is not None:
                    dve.wait_ge(s["dn"], free)
                V.tensor_copy(flat(hidT[par]), pb[4][:, 0:FT * CAP]).then_inc(s["ht_e"], 1)

            hidden_rows(0, 0)

            selection(2, 0)

            def step(e, par, more=True):
                if more:
                    selection(e + 3, 1 - par)
                hidden_t(e, par)
                hidden_rows(e + 1, 1 - par)

            step(0, 0)
            step(1, 1)
            with dve.Fori(1, NE // 2 - 2) as j:
                step(j * 2, 0)
                step(j * 2 + 1, 1)
            step(NE - 4, 0)
            step(NE - 3, 1, more=False)
            step(NE - 2, 0, more=False)
            hidden_t(NE - 1, 1)
            dve.wait_ge(s["dn"], NE)
            dve.wait_ge(s["over"], 1)
            n_over = dve.value_load(over_i[0:1, NOVER:NOVER + 1], min_val=0, max_val=NOVER)
            with dve.If(n_over > 0):
                with dve.Fori(0, n_over) as i:
                    selection(i + NE, 1)
                    hidden_rows(i + NE, 1)
                    hidden_t(i + NE, 1)
            gathered = dve.snap(layer * 32 + 32)
            for b in range(NB):
                dve.wait_ge(s_gathered[b], gathered)
                for j in range(2):
                    i = NB * j + b
                    if j:
                        dve.wait_ge(s["moe"], 2 * b + 1)
                    STT(out=x[:, b, :], in0=hbuf[:, D * i:D * i + D], scalar=gate_w[:, i:i + 1], in1=x[:, b, :],
                        op0=ALU.mult, op1=ALU.add).then_inc(s["moe"], 1)
            dve.wait_ge(s["rms3"], 1)
            link(V.reciprocal(rstd, rms))

        def pool_program(pool, layer):
            G = nc.gpsimd
            TS, TT = G.tensor_scalar, G.tensor_tensor
            link = linker(pool, s["pool"])

            def scan_operands(hh):
                pool.wait_ge(s["f_ready"], hh + 1)
                if hh:
                    pool.wait_ge(s["head"], hh)
                link(TT(ht_d1, ht_f, cst("chunk_start"), ALU.mult))
                TT(ht_d0, ht_f, ht_d1, ALU.subtract).then_inc(s["f_split"], 1)

            def square(c, sn, t0, t1):
                link(TT(t0, c, c, ALU.mult))
                link(TT(t1, sn, sn, ALU.mult))
                link(TT(sn, sn, c, ALU.mult))
                link(TT(sn, sn, sn, ALU.add))
                link(TT(c, t0, t1, ALU.subtract))

            a_re, a_im = pcol("a_re"), pcol("a_im")
            pool.wait_ge(s["dt"], 1)
            tmp = [Wr[:, i, :] for i in range(4)]
            link(TT(pv_lr, a_re, pv_dt, ALU.mult))
            link(TT(pv_sin, a_im, pv_dt, ALU.mult))
            link(TS(tmp[0], pv_sin, float(1.0 / TWO_PI), ROUND, ALU.mult, ALU.add))
            link(TS(tmp[0], tmp[0], ROUND, None, ALU.subtract))
            for part in TURN:
                link(TS(tmp[1], tmp[0], -part, None, ALU.mult))
                link(TT(pv_sin, pv_sin, tmp[1], ALU.add))
            link(TS(pv_r, pv_sin, PI_DOWN, -PI_DOWN, ALU.min, ALU.max))
            link(TS(tmp[1], pv_r, 0.0, 2.0, ALU.max, ALU.mult))
            link(TT(tmp[1], pv_r, tmp[1], ALU.subtract))
            TS(pv_rc, tmp[1], float(np.pi / 2), None, ALU.add).then_inc(s["ang"], 1)
            link(TT(tmp[2], a_re, a_re, ALU.mult))
            link(TT(tmp[3], a_im, a_im, ALU.mult))
            TT(pv_den, tmp[2], tmp[3], ALU.add).then_inc(s["den"], 1)
            pool.wait_ge(s["lam"], 1)
            c1, s1, c2, s2 = Wi[:, 0, :], Wi[:, 1, :], Wi[:, 2, :], Wi[:, 3, :]
            link(G.tensor_copy(c1, pv_cos))
            link(G.tensor_copy(s1, pv_sin))
            for _ in range(3):
                square(c1, s1, c2, s2)
            tm = ring[:, 1, 3072:4096].rearrange("p (d k) -> p d k", d=DG)

            def turns(n):
                lo, hi = slice(0, n), slice(n, 2 * n)
                cb, sb_ = (a[:, :, None].broadcast_to([P, DG, n]) for a in (c1, s1))
                t = tm[:, :, 0:n]
                link(TT(cosT[:, :, hi], cosT[:, :, lo], cb, ALU.mult))
                link(TT(t, sinT[:, :, lo], sb_, ALU.mult))
                link(TT(cosT[:, :, hi], cosT[:, :, hi], t, ALU.subtract))
                link(TT(sinT[:, :, hi], sinT[:, :, lo], cb, ALU.mult))
                link(TT(t, cosT[:, :, lo], sb_, ALU.mult))
                link(TT(sinT[:, :, hi], sinT[:, :, hi], t, ALU.add))
                square(c1, s1, c2, s2)

            scan_operands(0)
            pool.wait_ge(s["pe"], 16)
            G.memset(cosT[:, :, 0], 1.0)
            link(G.memset(sinT[:, :, 0], 0.0))
            for n in (1, 2, 4):
                turns(n)
            scan_operands(1)
            turns(8)
            turns(16)
            scan_operands(2)
            turns(32)
            scan_operands(3)
            TS(flat(sinT), flat(sinT), cst("sign"), None, ALU.mult).then_inc(s["tab"], 1)
            pool.wait_ge(s["tab"], 1)
            link(TT(pv_cos, pv_cos, pv_rho, ALU.mult))
            link(TT(pv_sin, pv_sin, pv_rho, ALU.mult))
            G.memset(Wr[:, 0, :], 1.0)
            link(G.memset(Wi[:, 0, :], 0.0))
            link(G.tensor_copy(Wr[:, 1, :], pv_cos))
            link(G.tensor_copy(Wi[:, 1, :], pv_sin))
            for n in (1, 2, 4):
                lo, hi = slice(1, n + 1), slice(n + 1, 2 * n + 1)
                br, bi = (a[:, n, :][:, None, :].broadcast_to([P, n, DG]) for a in (Wr, Wi))
                t = W_t[:, 0:n, :]
                link(TT(Wr[:, hi, :], Wr[:, lo, :], br, ALU.mult))
                link(TT(t, Wi[:, lo, :], bi, ALU.mult))
                link(TT(Wr[:, hi, :], Wr[:, hi, :], t, ALU.subtract))
                link(TT(Wi[:, hi, :], Wr[:, lo, :], bi, ALU.mult))
                link(TT(t, Wi[:, lo, :], br, ALU.mult))
                link(TT(Wi[:, hi, :], Wi[:, hi, :], t, ALU.add))
            t0, t2 = W_t[:, 0, :], W_t[:, 2, :]
            link(TS(t2, pv_cos, 1.0, None, ALU.subtract))
            link(TT(pv_fr, t2, a_re, ALU.mult))
            link(TT(t0, pv_sin, a_im, ALU.mult))
            link(TT(pv_fr, pv_fr, t0, ALU.add))
            link(TT(pv_fi, pv_sin, a_re, ALU.mult))
            link(TT(t0, t2, a_im, ALU.mult))
            link(TT(pv_fi, pv_fi, t0, ALU.subtract))
            pool.wait_ge(s["inv"], 1)
            link(TT(pv_fr, pv_fr, pv_den, ALU.mult))
            link(TT(pv_fi, pv_fi, pv_den, ALU.mult))

            wait_evacuated(pool, 22)
            wait_evacuated(pool, 23)
            pool.wait_ge(s["pe"], NG)
            pool.wait_ge(s["r_done"], 5)
            for n in range(NB * HG):
                hh, b = divmod(n, NB)
                if n >= 4:
                    pool.wait_ge(s["kv"], n - 3)
                TT(v_blk[b].rearrange("p (c v) -> p c v", c=CB),
                   hv[:, b, HD * hh:HD * hh + HD][:, None, :].broadcast_to([P, CB, HD]),
                   cst("chunk_of")[:, :, None].broadcast_to([P, CB, HD]), ALU.mult).then_inc(s["vb"], 1)

            def sp(name):
                a, n = S5P[name]
                return s5[:, a:a + n]

            pool.wait_ge(s["s5p"], 16)
            pool.wait_ge(s["ho"], HG)
            d3 = lambda ap: ap.rearrange("p (d c) -> p d c", d=DG)
            b_re, b_im, c_re, c_im = (d3(sp(n)) for n in ("b_re", "b_im", "c_re", "c_im"))
            fr, fi = (a[:, :, None].broadcast_to([P, DG, C5]) for a in (pv_fr, pv_fi))
            q0, q1, q2 = (d3(s_tmp[:, 512 * i:512 * i + 512]) for i in range(3))
            link(TT(q0, b_re, fi, ALU.mult))
            link(TT(q1, b_im, fi, ALU.mult))
            link(TT(q2, b_im, fr, ALU.mult))
            link(TT(b_re, b_re, fr, ALU.mult))
            link(TT(b_re, b_re, q1, ALU.subtract))
            link(TT(b_im, q0, q2, ALU.add))
            w2 = lambda ap: ap.rearrange("p i d -> p (i d)")
            for to, a_, b_, sub in ((A1, ("is_re", Wr), ("is_im", Wi), False), (A2, ("is_im", Wr), ("is_re", Wi), True),
                                    (A3, ("is_re", Wr), ("is_im", Wi), True), (A4, ("is_im", Wr), ("is_re", Wi), False)):
                t = s_tmp[:, 0:NPOW * DG]
                link(TS(w2(to), w2(a_[1]), cst(a_[0]), None, ALU.mult))
                link(TS(t, w2(b_[1]), cst(b_[0]), None, ALU.mult))
                link(TT(w2(to), w2(to), t, ALU.subtract if sub else ALU.add))
            link(TS(w2(A4), w2(A4), -1.0, None, ALU.mult))
            def times(to, dg, i0, n, down_, pr, pi, vr, vi, tmp_):
                for k, (pwr, val) in enumerate(((pr, vr), (pi, vi))):
                    w = pwr[:, i0:i0 + n, dg]
                    if down_:
                        w = w[:, ::-1, :]
                    w = w.rearrange("p i d -> p d i")[:, :, :, None].broadcast_to([P, G5, n, C5])
                    v = val[:, dg, :][:, :, None, :].broadcast_to([P, G5, n, C5])
                    link(TT(tmp_ if k else to, w, v, ALU.mult))
                return TT(to, to, tmp_, ALU.add)

            forward, backward = slice(0, G5), slice(G5, DG)
            t8 = s_tmp[:, 0:G5 * SC * C5].rearrange("p (d i c) -> p d i c", d=G5, i=SC)
            t9 = s_tmp[:, 0:G5 * NPOW * C5].rearrange("p (d i c) -> p d i c", d=G5, i=NPOW)
            pool.wait_ge(s["o_a"], 2)
            link(times(BtT[:, forward, :, :], forward, 0, SC, True, A1, A2, b_re, b_im, t8))
            times(BtT[:, backward, :, :], backward, 0, SC, False, A1, A2, b_re, b_im, t8).then_inc(s["bc"], 1)
            pool.wait_ge(s["bc"], 1)
            times(Ct[:, forward, :, :], forward, 0, NPOW, False, A3, A4, c_re, c_im, t9).then_inc(s["bc"], 1)
            link(G.tensor_copy(rho, pv_rho8[:, :, None].broadcast_to([P, DG, NK])))
            G.memset(rho[:, :, 0], 0.0).then_inc(s["rho"], 1)

            pool.wait_ge(s["dest"], 1)
            pool.wait_ge(s_zeroed, ZEROINGS * 16)
            pool.wait_ge(s["stored"], 1)
            for b in range(NB):
                for i in (b, NB + b):
                    G.indirect_dma_start(out=hbuf[:, D * i:D * i + D], out_offset=None, in_=ybuf,
                                         in_offset=bass.IndirectOffsetOnAxis(ap=dest_i[:, i:i + 1], axis=0)
                                         ).then_inc(s_gathered[b], 16)

        with nc.Fori(0, L) as layer:
            with nc.Block() as block:
                @block.sync
                def _(sp):
                    sync_program(sp, layer)

                @block.tensor
                def _(pe):
                    tensor_program(pe, layer)

                @block.scalar
                def _(act):
                    scalar_program(act, layer)

                @block.vector
                def _(dve):
                    vector_program(dve, layer)

                @block.gpsimd
                def _(pool):
                    pool_program(pool, layer)
            numbers = [q.num for q in [*s.values(), *slot, *y_out]]
            assert max(numbers) - min(numbers) + 1 == len(numbers)
            nc.multi_engine_barrier(list(nc.engines), sems_to_clear=range(min(numbers), max(numbers) + 1))

        with nc.Block() as block:
            @block.vector
            def _(dve):
                dve.wait_ge(s_gain1, 16 * (L + 1))
                for b in range(NB):
                    nc.vector.scalar_tensor_tensor(out=h[:, b, :], in0=x[:, b, :], scalar=rstd[:, b:b + 1],
                                                   in1=gB[:, :], op0=ALU.mult, op1=ALU.mult).then_inc(s_fd, 1)

            @block.sync
            def _(sp):
                for b in range(NB):
                    sp.wait_ge(s_fd, b + 1)
                    sp.dma_start(out[P * b:P * b + P, :], h[:, b, :]).then_inc(s_out, 16)
                sp.wait_ge(s_out, 16 * NB)


TURN = (6.28125, float(np.float32(TWO_PI - 6.28125)), float(TWO_PI - 6.28125 - np.float32(TWO_PI - 6.28125)))
PI_DOWN = 3.1415925


def constants():
    c = np.zeros((P, CONST_W), np.float32)

    def put(name, value):
        a, n = CONST[name]
        c[:, a:a + n] = value

    p = np.arange(P)[:, None]
    q = np.arange(P)[None, :]
    put("ident", p == q)
    same = (p // CH) == (q // CH)
    put("mask_f", same & (p <= q))
    put("mask_b", same & (p >= q))
    put("head_ones", (p // HD) == (q // HD))
    put("rope_swap", np.where((q % 2 == 0) & (p == q + 1), -1.0, 0.0) + np.where((q % 2 == 1) & (p == q - 1), 1.0, 0.0))
    put("half_swap", p == (q + HD) % P)
    put("before", p < q)
    put("ones", 1.0)
    pairs, grid = HD // 4, 64
    freqs = np.power(np.float32(10000.0), -np.arange(pairs, dtype=np.float32) / np.float32(pairs)).astype(np.float32)
    t = np.arange(T)
    ang = np.concatenate([(t // grid).astype(np.float32)[:, None] * freqs, (t % grid).astype(np.float32)[:, None] * freqs], 1)
    by_row = ang.astype(np.float32)[:, (np.arange(P) % HD) // 2].T
    put("cos", np.cos(by_row))
    put("sin", np.sin(by_row))
    put("chunk_start", np.where(p < HD, t[None, :] % CH == 0, t[None, :] % CH == CH - 1))
    put("chunk_of", (p // CH) == np.arange(CB)[None, :])
    put("group_id", np.arange(EG)[None, :] - BIG)
    put("expert_id", np.arange(NE)[None, :] - BIG)
    put("expert_row", np.arange(NE)[None, :] * CAP)
    put("far_row", (NE - 1) * CAP - np.arange(NE)[None, :] * CAP)
    put("chunk_end", np.arange(1, 8)[None, :] * CAP)
    put("over_id", np.arange(NOVER)[None, :])
    put("slot_id", np.arange(CAP)[None, :])
    put("is_re", p < HD)
    put("is_im", p >= HD)
    put("sign", np.where(p < HD, 1.0, -1.0))
    put("eps", EPS)
    return c


def kernel(**inputs):
    import concourse.bacc as bacc
    from concourse.bass_utils import run_bass_kernel_spmd

    a = {k: np.asarray(v) for k, v in inputs.items()}
    f = np.ascontiguousarray

    w = a["w_in"].reshape(L, KT, P, 2304)
    head = lambda at, i: np.arange(at + HD * i, at + HD * i + HD)
    z = np.concatenate([np.concatenate([head(768, i), head(1024, i)]) for i in range(HG)])
    heads = np.concatenate([head(0, i) for pair in range(4) for i in (pair, pair + 4)])
    order = [z, np.concatenate([np.arange(0, 256), np.arange(1792, 2048)]), 1280 + heads,
             np.concatenate([np.arange(512, 768), np.arange(256, 512)]), np.arange(2048, 2304)]
    w_in = f(np.concatenate([w[..., o].transpose(0, 2, 1, 3).reshape(L, P, -1) for o in order], axis=2))
    mixed = np.concatenate([np.arange(256), 256 + heads, np.arange(768, 1024)])
    w_out = f(a["w_out"][:, mixed].reshape(L, KT, P, 2, 512).transpose(0, 3, 2, 1, 4).reshape(L, 2, P, 4096))

    pack = np.zeros((L, P, PACK_W), np.float32)

    def put(name, value):
        at, n = PACK[name]
        pack[:, :, at:at + n] = value

    bounds = a["hgrn_lower_bounds"].reshape(L, 2, HG, HD).transpose(1, 3, 0, 2).reshape(P, L * HG)
    put("lb", bounds[None])
    put("lb_sum", np.array([[0.0] + [1.0 if 1 <= j <= l else 0.0 for j in range(1, L)] for l in range(L)])[:, None, :])
    twice = lambda v: np.concatenate([v, v], axis=1)[:, :, None]
    put("hgrn_g", twice(a["hgrn_norm_g"]))
    put("q_g", twice(a["attn_q_norm_g"]))
    put("k_g", twice(a["attn_k_norm_g"]))
    put("s5_d", a["s5_d"].reshape(L, 2, P).transpose(0, 2, 1))
    put("b_glu", a["s5_b_glu"].reshape(L, 2, P).transpose(0, 2, 1))
    put("router_b", np.concatenate([a["router_group_b"], a["router_expert_b"]], axis=1)[:, None, :])
    rw = np.concatenate([a["router_group_w"], a["router_expert_w"]], axis=2).reshape(L, KT, P, RW)
    put("router_w", rw.transpose(0, 2, 1, 3).reshape(L, P, KT * RW))
    put("w_glu", a["s5_w_glu"].reshape(L, 2, P, 256).transpose(0, 2, 1, 3).reshape(L, P, 512))

    both = lambda v: np.concatenate([v, v], axis=1)
    put("a_re", both(a["s5_a_re"].transpose(0, 3, 1, 2).reshape(L, HD, DG)))
    put("a_im", both(a["s5_a_im"].transpose(0, 3, 1, 2).reshape(L, HD, DG)))
    put("log_dt", a["s5_log_dt"].reshape(L, 1, DG))

    s5p = np.zeros((L, P, S5P_W), np.float32)

    def put5(name, value):
        at, n = S5P[name]
        s5p[:, :, at:at + n] = np.concatenate([value, value], axis=1)

    for part in ("re", "im"):
        put5("b_" + part, a["s5_b_" + part].transpose(0, 3, 1, 2, 4).reshape(L, HD, DG * C5))
        put5("c_" + part, a["s5_c_" + part].transpose(0, 4, 1, 2, 3).reshape(L, HD, DG * C5))

    rows = np.concatenate([np.stack([a["norm1_g"], a["norm2_g"]], axis=1).reshape(2 * L, D), a["final_norm_g"][None]])
    gains = f(np.broadcast_to(rows[:, None, :], (2 * L + 1, P, D)))

    arrays = {
        "x_in": f(a["x"].reshape(T, D)), "w_in": w_in, "w_out": w_out, "pack": pack, "s5p": s5p, "gains": gains,
        "wg": f(a["expert_w_gate"].reshape(L * NE, D, FF)),
        "wu": f(a["expert_w_up"].reshape(L * NE, D, FF)), "wd": f(a["expert_w_down"].reshape(L * NE, FF, D)),
        "consts": constants(),
    }
    nc = bacc.Bacc("TRN2", target_bir_lowering=False, num_devices=1)
    args = [nc.dram_tensor(name, v.shape, F32, kind="ExternalInput").ap() for name, v in arrays.items()]
    out = nc.dram_tensor("out", (T, D), F32, kind="ExternalOutput").ap()
    trunk(nc, *args, out)
    r = run_bass_kernel_spmd(nc, [arrays], core_ids=[0])
    return np.asarray(r.results[0]["out"]).reshape(1, T, D)
```
